# Optimizing a Trainium2 kernel written in Bass

```python
import math
import jax, jax.numpy as jnp
from jax import lax
import numpy as np

D_MODEL = 1024
BATCH = 1
SEQ = 256
DEPTH = 2

HEAD_DIM = 64
SB_HEADS = 8
DIFF_HEADS = 4
SB_WIDTH = SB_HEADS * HEAD_DIM
DIFF_QK_WIDTH = DIFF_HEADS * 2 * HEAD_DIM
DIFF_VDIM = 2 * HEAD_DIM
DIFF_WIDTH = DIFF_HEADS * DIFF_VDIM
MIX_WIDTH = SB_WIDTH + DIFF_WIDTH
QKV_WIDTH = 3 * SB_WIDTH + 2 * DIFF_QK_WIDTH + DIFF_WIDTH
SPLITS = [SB_WIDTH, 2 * SB_WIDTH, 3 * SB_WIDTH,
          3 * SB_WIDTH + DIFF_QK_WIDTH, 3 * SB_WIDTH + 2 * DIFF_QK_WIDTH]
Q_BLOCK = 128
N_BUCKETS = 32
MAX_DISTANCE = 128
D_FF_DENSE = 2816
N_EXPERTS = 8
TOP_K = 2
D_FF_EXPERT = 3584
MOE_BLOCK = 128
N_DENSE = (DEPTH + 1) // 2
N_MOE = DEPTH // 2
NORM_EPS = 1e-6

kernel_name = "hybrid_stickbreak_diffattn_moe"

def rms_norm(x, g):
    xf = x.astype(jnp.float32)
    y = xf * lax.rsqrt(jnp.mean(xf * xf, axis=-1, keepdims=True) + NORM_EPS)
    return (y * g.astype(jnp.float32)).astype(x.dtype)

def t5_causal_bucket(n):
    max_exact = N_BUCKETS // 2
    nf = jnp.maximum(n, 1).astype(jnp.float32)
    large = max_exact + (jnp.log(nf / max_exact) / math.log(MAX_DISTANCE / max_exact)
                         * (N_BUCKETS - max_exact)).astype(jnp.int32)
    large = jnp.minimum(large, N_BUCKETS - 1)
    return jnp.where(n < max_exact, n, large)

def stick_breaking_attention(q, k, v):
    S = q.shape[1]
    scale = HEAD_DIM ** -0.5
    outs = []
    for blk in range(S // Q_BLOCK):
        q0 = blk * Q_BLOCK
        kl = q0 + Q_BLOCK
        z = jnp.einsum('bqhd,bkhd->bhqk', q[:, q0:kl], k[:, :kl]).astype(jnp.float32) * scale
        t_pos = q0 + jnp.arange(Q_BLOCK)[:, None]
        s_pos = jnp.arange(kl)[None, :]
        mask = s_pos < t_pos
        log_stay = jnp.where(mask, jax.nn.log_sigmoid(-z), 0.0)
        between = lax.cumsum(log_stay, axis=3, reverse=True) - log_stay
        a = jnp.where(mask, jnp.exp(jax.nn.log_sigmoid(z) + between), 0.0)
        outs.append(jnp.einsum('bhqk,bkhd->bqhd', a.astype(v.dtype), v[:, :kl]))
    return jnp.concatenate(outs, axis=1)

def differential_attention(q, k, v, bias_by_dist, lam):
    S = q.shape[1]
    scale = HEAD_DIM ** -0.5
    outs = []
    for blk in range(S // Q_BLOCK):
        q0 = blk * Q_BLOCK
        kl = q0 + Q_BLOCK
        z = jnp.einsum('bqhcd,bkhcd->bhcqk', q[:, q0:kl], k[:, :kl]).astype(jnp.float32) * scale
        dist = (q0 + jnp.arange(Q_BLOCK)[:, None]) - jnp.arange(kl)[None, :]
        bias = jnp.take(bias_by_dist, jnp.maximum(dist, 0), axis=0)
        z = z + jnp.transpose(bias, (2, 0, 1))[None, :, None]
        z = jnp.where(dist >= 0, z, -jnp.inf)
        p = jax.nn.softmax(z, axis=-1)
        w = p[:, :, 0] - lam * p[:, :, 1]
        outs.append(jnp.einsum('bhqk,bkhe->bqhe', w.astype(v.dtype), v[:, :kl]))
    return jnp.concatenate(outs, axis=1)

def swiglu(h, w_gate, w_up, w_down):
    return (jax.nn.silu(h @ w_gate) * (h @ w_up)) @ w_down

def moe_swiglu(h, router_w, w_gate, w_up, w_down):
    B, S, D = h.shape
    n = B * S
    xf = h.reshape(n, D)
    logits = jnp.dot(xf.astype(jnp.float32), router_w.astype(jnp.float32))
    top_logit, top_idx = lax.top_k(logits, TOP_K)
    gates = jax.nn.softmax(top_logit, axis=-1)
    n_assign = n * TOP_K
    expert_ids = top_idx.reshape(-1)
    token_ids = jnp.arange(n_assign, dtype=jnp.int32) // TOP_K
    order = jnp.argsort(expert_ids)
    sorted_exp = expert_ids[order]
    sorted_tok = token_ids[order]
    sorted_gate = gates.reshape(-1)[order]
    counts = jnp.bincount(expert_ids, length=N_EXPERTS)
    starts = jnp.cumsum(counts) - counts
    padded = (counts + MOE_BLOCK - 1) // MOE_BLOCK * MOE_BLOCK
    pad_ends = jnp.cumsum(padded)
    pad_starts = pad_ends - padded
    dest = pad_starts[sorted_exp] + (jnp.arange(n_assign, dtype=jnp.int32) - starts[sorted_exp])
    n_blocks = -(-n_assign // MOE_BLOCK) + N_EXPERTS
    cap = n_blocks * MOE_BLOCK
    buf = jnp.zeros((cap, D), xf.dtype).at[dest].set(xf[sorted_tok])
    block_exp = jnp.minimum(
        jnp.searchsorted(pad_ends, jnp.arange(n_blocks, dtype=jnp.int32) * MOE_BLOCK, side='right'),
        N_EXPERTS - 1)

    def expert_block(args):
        xb, e = args
        return swiglu(xb, w_gate[e], w_up[e], w_down[e])

    yb = lax.map(expert_block, (buf.reshape(n_blocks, MOE_BLOCK, D), block_exp))
    y = yb.reshape(cap, D)[dest] * sorted_gate[:, None].astype(xf.dtype)
    out = jax.ops.segment_sum(y, sorted_tok, num_segments=n)
    return out.reshape(B, S, D)

def setup_inputs(seed: int = 0) -> dict:
    key = jax.random.key(seed)
    ks = jax.random.split(key, 24)
    f32 = jnp.float32
    nrm = lambda k, shape, s: jax.random.normal(k, shape, f32) * s
    gain = lambda k, shape: 1.0 + 0.02 * jax.random.normal(k, shape, f32)
    return {
        "x": jax.random.normal(ks[0], (BATCH, SEQ, D_MODEL), f32),
        "w_in": nrm(ks[1], (DEPTH, D_MODEL, QKV_WIDTH), D_MODEL ** -0.5),
        "w_out": nrm(ks[2], (DEPTH, MIX_WIDTH, D_MODEL), MIX_WIDTH ** -0.5),
        "attn_norm": gain(ks[3], (DEPTH, D_MODEL)),
        "ffn_norm": gain(ks[4], (DEPTH, D_MODEL)),
        "sb_out_norm": gain(ks[5], (DEPTH, HEAD_DIM)),
        "diff_subln": gain(ks[6], (DEPTH, DIFF_VDIM)),
        "lambda_q1": nrm(ks[7], (DEPTH, HEAD_DIM), 0.1),
        "lambda_k1": nrm(ks[8], (DEPTH, HEAD_DIM), 0.1),
        "lambda_q2": nrm(ks[9], (DEPTH, HEAD_DIM), 0.1),
        "lambda_k2": nrm(ks[10], (DEPTH, HEAD_DIM), 0.1),
        "rel_bias": nrm(ks[11], (N_BUCKETS, DIFF_HEADS), 0.5),
        "dense_w_gate": nrm(ks[12], (N_DENSE, D_MODEL, D_FF_DENSE), D_MODEL ** -0.5),
        "dense_w_up": nrm(ks[13], (N_DENSE, D_MODEL, D_FF_DENSE), D_MODEL ** -0.5),
        "dense_w_down": nrm(ks[14], (N_DENSE, D_FF_DENSE, D_MODEL), D_FF_DENSE ** -0.5),
        "router_w": nrm(ks[15], (N_MOE, D_MODEL, N_EXPERTS), D_MODEL ** -0.5),
        "expert_w_gate": nrm(ks[16], (N_MOE, N_EXPERTS, D_MODEL, D_FF_EXPERT), D_MODEL ** -0.5),
        "expert_w_up": nrm(ks[17], (N_MOE, N_EXPERTS, D_MODEL, D_FF_EXPERT), D_MODEL ** -0.5),
        "expert_w_down": nrm(ks[18], (N_MOE, N_EXPERTS, D_FF_EXPERT, D_MODEL), D_FF_EXPERT ** -0.5),
        "final_norm": gain(ks[19], (D_MODEL,)),
    }

def reference(x, w_in, w_out, attn_norm, ffn_norm, sb_out_norm, diff_subln,
              lambda_q1, lambda_k1, lambda_q2, lambda_k2, rel_bias,
              dense_w_gate, dense_w_up, dense_w_down, router_w,
              expert_w_gate, expert_w_up, expert_w_down, final_norm):
    B, S, _ = x.shape
    bias_by_dist = rel_bias.astype(jnp.float32)[t5_causal_bucket(jnp.arange(S, dtype=jnp.int32))]
    for i in range(DEPTH):
        h = rms_norm(x, attn_norm[i])
        proj = jnp.einsum('bsd,de->bse', h, w_in[i])
        sb_q, sb_k, sb_v, df_q, df_k, df_v = jnp.split(proj, SPLITS, axis=-1)
        sb = stick_breaking_attention(sb_q.reshape(B, S, SB_HEADS, HEAD_DIM),
                                      sb_k.reshape(B, S, SB_HEADS, HEAD_DIM),
                                      sb_v.reshape(B, S, SB_HEADS, HEAD_DIM))
        sb = rms_norm(sb, sb_out_norm[i]).reshape(B, S, SB_WIDTH)
        lambda_init = 0.8 - 0.6 * math.exp(-0.3 * i)
        lam = (jnp.exp(jnp.sum(lambda_q1[i].astype(jnp.float32) * lambda_k1[i].astype(jnp.float32)))
               - jnp.exp(jnp.sum(lambda_q2[i].astype(jnp.float32) * lambda_k2[i].astype(jnp.float32)))
               + lambda_init)
        df = differential_attention(df_q.reshape(B, S, DIFF_HEADS, 2, HEAD_DIM),
                                    df_k.reshape(B, S, DIFF_HEADS, 2, HEAD_DIM),
                                    df_v.reshape(B, S, DIFF_HEADS, DIFF_VDIM),
                                    bias_by_dist, lam)
        df = (rms_norm(df, diff_subln[i]) * (1.0 - lambda_init)).reshape(B, S, DIFF_WIDTH)
        x = x + jnp.einsum('bse,ed->bsd', jnp.concatenate([sb, df], axis=-1), w_out[i])
        h2 = rms_norm(x, ffn_norm[i])
        if i % 2 == 0:
            j = i // 2
            x = x + swiglu(h2, dense_w_gate[j], dense_w_up[j], dense_w_down[j])
        else:
            j = i // 2
            x = x + moe_swiglu(h2, router_w[j], expert_w_gate[j], expert_w_up[j], expert_w_down[j])
    return rms_norm(x, final_norm)


_drawn_inputs = setup_inputs


def setup_inputs(seed=0):
    import zlib

    import numpy as np

    out = dict(_drawn_inputs(seed))
    spreads = {}
    factors = {'lambda_q2': 3.016, 'final_norm': 2.843}
    for name, (base, spread) in spreads.items():
        noise = np.random.default_rng([zlib.crc32(name.encode()), seed]).standard_normal(out[name].shape)
        drawn = base * np.exp(spread * noise) if base else spread * noise
        out[name] = __import__('jax').numpy.asarray(drawn.astype(out[name].dtype))
    for name, factor in factors.items():
        out[name] = (out[name] * factor).astype(out[name].dtype)
    return out
```

```python
from contextlib import ExitStack
import math

import numpy as np

import concourse.bass as bass
from concourse import mybir

F32 = mybir.dt.float32
F32R = mybir.dt.float32r
I32 = mybir.dt.int32
ALU = mybir.AluOpType
ACT = mybir.ActivationFunctionType
AX = mybir.AxisListType

P = 128
D = 1024
S = 256
TT = S // P
KT = D // P
DEPTH = 2
SB_HEADS, DF_HEADS, HD = 8, 4, 64
HALF = SB_HEADS * HD
QKV = 6 * HALF
FD = 2816
FE = 3584
NE = 8
EPS = 1e-6
CH = 512
N_BUCKETS, MAX_DISTANCE = 32, 128
MASKED = -1.0e30
PIECE = 2048
RAW = 6
SPL = 3
D_FULL = FD // CH
D_REST = FD - D_FULL * CH
FT = FD // P
E_CH = FE // CH
PROJ = 12
WOUT = 4
DENSE_GU = 4 * D_FULL + 2
DENSE_DN = FD * D // (P * PIECE)
LAYER1 = PROJ + WOUT + DENSE_GU + DENSE_DN
MOE0 = LAYER1 + PROJ + WOUT
PER_BLOCK = 6 * E_CH
MAX_BLOCKS = S * 2 // P + NE - 1
TAB = MAX_BLOCKS + 1
NOT_CHOSEN = 1000.0
C_ID, C_NTRI, C_NONE, C_TRIS, C_ONE, C_IOTA = (P * i for i in range(6))
C_REV = 6 * P
C_E = C_REV + NE
C_LE = C_E + NE
C_B = C_LE + NE * NE
C_OH = C_B + TAB
C_MASKED = C_OH + 384
C_FLIP = C_MASKED + DF_HEADS
C_END = C_FLIP + P
CONSTS = C_OH


def constants():
    c = np.zeros((P, C_END), np.float32)
    r = np.arange(P)
    c[:, C_ID:C_ID + P] = np.eye(P)
    c[:, C_NTRI:C_NTRI + P] = -(r[:, None] >= r[None, :]).astype(np.float32)
    c[:, C_NONE:C_NONE + P] = -1.0
    c[:, C_TRIS:C_TRIS + P] = r[:, None] < r[None, :]
    c[:, C_ONE:C_ONE + P] = 1.0
    c[:, C_IOTA:C_IOTA + P] = r[None, :]
    e = np.arange(NE)
    c[:, C_REV:C_REV + NE] = NE - e
    c[:, C_E:C_E + NE] = e
    c[:, C_LE:C_LE + NE * NE] = (e[None, :] <= e[:, None]).astype(np.float32).reshape(-1)
    c[:, C_B:C_B + TAB] = np.arange(TAB)
    i = np.arange(384)
    dist = S - 1 - i
    exact = N_BUCKETS // 2
    n = np.maximum(dist, 1).astype(np.float32)
    large = exact + (np.log(n / np.float32(exact)) / np.float32(math.log(MAX_DISTANCE / exact))
                     * np.float32(N_BUCKETS - exact)).astype(np.int32)
    bucket = np.where(dist < exact, dist, np.minimum(large, N_BUCKETS - 1))
    bucket = np.where(dist < 0, N_BUCKETS, bucket)
    c[bucket, C_OH + i] = 1.0
    c[:, C_FLIP:C_FLIP + P] = np.eye(P)[::-1]
    c[N_BUCKETS, C_MASKED:C_MASKED + DF_HEADS] = MASKED
    return c


def lambda_init(layer):
    return 0.8 - 0.6 * math.exp(-0.3 * layer)


def build(nc, x, w_in, w_out, attn_norm, ffn_norm, sb_out_norm, diff_subln, lambda_q1, lambda_k1,
          lambda_q2, lambda_k2, rel_bias, dense_w_gate, dense_w_up, dense_w_down, router_w,
          expert_w_gate, expert_w_up, expert_w_down, final_norm, consts, out):
    with ExitStack() as ctx:
        def sb(name, shape, dt=F32, stack=ctx):
            return stack.enter_context(nc.sbuf_tensor(name, shape, dt))

        def sem(name):
            return ctx.enter_context(nc.semaphore(name))

        raw = sb("raw", [P, RAW, PIECE])
        w_hi = sb("w_hi", [P, SPL, PIECE], F32R)
        w_lo = sb("w_lo", [P, SPL, PIECE], F32R)
        xs = sb("xs", [P, TT, D])
        aT_hi = sb("aT_hi", [P, KT, S], F32R)
        aT_lo = sb("aT_lo", [P, KT, S], F32R)
        hn = sb("hn", [P, TT, D])
        sq = sb("sq", [P, TT * HALF])
        gain = sb("gain", [P, 2, D])
        g_sb = sb("g_sb", [P, DEPTH, HD])
        g_df = sb("g_df", [P, DEPTH, 2 * HD])
        cst = sb("cst", [P, CONSTS])
        ss = sb("ss", [P, 16])
        var = sb("var", [P, 16])
        lnv = sb("lnv", [P, 16])
        rs0 = sb("rs0", [P, 16])
        nw1 = sb("nw1", [P, 16])
        nw2 = sb("nw2", [P, 16])
        rstd = sb("rstd", [P, 16])
        nlam = sb("nlam", [P, DEPTH])
        bias = sb("bias", [P, DF_HEADS, S])
        ps = ctx.enter_context(nc.psum_tensor("ps", [P, 8, 512], F32))

        with ExitStack() as phase:
            def sp_(name, shape, dt=F32):
                return sb(name, shape, dt, phase)
            qk_sb = sp_("qk_sb", [P, 8, S])
            qk_df = sp_("qk_df", [P, 8, S])
            v_sb = sp_("v_sb", [P, TT, HALF])
            v_df = sp_("v_df", [P, TT, HALF])
            bias_up = sp_("bias_up", [P, DF_HEADS, S])
            flip = sp_("flip", [P, P])
            ab = sp_("ab", [P, 2, 384])
            spl = sp_("spl", [P, 2, 384])
            att = sp_("att", [P, 2, 384])
            zb = sp_("zb", [P, 2, 2, S])
            wd = sp_("wd", [P, 2, S])
            wT = sp_("wT", [P, 2, 384])
            mx = sp_("mx", [P, 2, 2])
            es = sp_("es", [P, 2, 2])
            rr = sp_("rr", [P, TT, DF_HEADS, 2])
            coef = sp_("coef", [P, 2, 1])
            lam_in = sp_("lam_in", [P, 4, DEPTH, HD])
            lam_pr = sp_("lam_pr", [P, 2, DEPTH, HD])
            lam_s = sp_("lam_s", [P, 2, DEPTH])
            lam_e = sp_("lam_e", [P, 2, DEPTH])
            lam_d = sp_("lam_d", [P, DEPTH])
            bkt = sp_("bkt", [N_BUCKETS + 1, 384 + DF_HEADS])
            vrow = sp_("vrow", [DF_HEADS, 384])
        with ExitStack() as phase:
            hT_hi = sb("hT_hi", [P, FT, S], F32R, phase)
            hT_lo = sb("hT_lo", [P, FT, S], F32R, phase)
        with ExitStack() as phase:
            def se(name, shape, dt=F32):
                return sb(name, shape, dt, phase)
            rT = se("rT", [P, KT, S])
            rw = se("rw", [P, KT, NE])
            lg = se("lg", [P, TT, NE])
            lg2 = se("lg2", [P, TT, NE])
            m1 = se("m1", [P, TT])
            m2 = se("m2", [P, TT])
            eq1, rk1, oh1 = se("eq1", [P, TT, NE]), se("rk1", [P, TT, NE]), se("oh1", [P, TT, NE])
            eq2, rk2, oh2 = se("eq2", [P, TT, NE]), se("rk2", [P, TT, NE]), se("oh2", [P, TT, NE])
            r1, r2 = se("r1", [P, TT]), se("r2", [P, TT])
            dm, ed, dn = se("dm", [P, TT]), se("ed", [P, TT]), se("dn", [P, TT])
            g1, g2 = se("g1", [P, TT]), se("g2", [P, TT])
            chosen = se("chosen", [P, TT, NE])
            gg1, gg = se("gg1", [P, TT, NE]), se("gg", [P, TT, NE])
            pm1, posm0, posm = se("pm1", [P, TT, NE]), se("posm0", [P, TT, NE]), se("posm", [P, TT, NE])
            cnt = se("cnt", [P, NE])
            nb1, nb2, nbe = se("nb1", [P, NE]), se("nb2", [P, NE]), se("nbe", [P, NE])
            le8 = se("le8", [P, NE, NE])
            ends = se("ends", [P, NE])
            cmpb = se("cmpb", [P, TAB, NE])
            eb = se("eb", [P, TAB])
            stb = se("stb", [P, TAB, NE])
            start = se("start", [P, TAB])
            local = se("local", [P, TAB])
            cm = se("cm", [P, TAB, NE])
            tmpb = se("tmpb", [P, 2, TT, TAB, NE])
            sel0 = se("sel0", [P, TT, TAB])
            sel = se("sel", [P, TT, TAB])
            gate_prev = se("gate_prev", [P, TT, TAB + 1])
            ebi = se("ebi", [P, TAB], I32)
            nbi = se("nbi", [P, 1], I32)
            xe_hi = se("xe_hi", [P, KT, P], F32R)
            xe_lo = se("xe_lo", [P, KT, P], F32R)
            onehot = se("onehot", [P, TT, P], F32R)
            onehotT = se("onehotT", [P, TT, P], F32R)
            he_hi = se("he_hi", [P, 4, P], F32R)
            he_lo = se("he_lo", [P, 4, P], F32R)
            ye_hi = se("ye_hi", [P, D], F32R)
            ye_lo = se("ye_lo", [P, D], F32R)
            sil = se("sil", [P, 2, CH])
            hid = se("hid", [P, 2, CH])

        scratch = nc.dram_tensor("bias_scratch", (DF_HEADS, 384), F32, kind="Internal").ap()
        hn_hi = aT_hi[:].rearrange("p k s -> p (k s)").rearrange("p (t d) -> p t d", t=TT)
        hn_lo = aT_lo[:].rearrange("p k s -> p (k s)").rearrange("p (t d) -> p t d", t=TT)
        ident = cst[:, C_ID:C_ID + P]
        neg_tri = cst[:, C_NTRI:C_NTRI + P]
        neg_one = cst[:, C_NONE:C_NONE + P]
        tri_strict = cst[:, C_TRIS:C_TRIS + P]
        ones = cst[:, C_ONE:C_ONE + P]
        iota = cst[:, C_IOTA:C_IOTA + P]

        raw_in = [sem(f"raw_in{i}") for i in range(RAW)]
        hi_ready, lo_ready, piece_used = sem("hi_ready"), sem("lo_ready"), sem("piece_used")
        x_in, cst_in, small_in, lam_ld, bkt_in = (sem(n) for n in ("x_in", "cst_in", "small_in", "lam_ld", "bkt_in"))
        rw_in = sem("rw_in")
        gain_in = [sem("gain_in0"), sem("gain_in1")]
        x_done, ss_done, var_done, rs_done, rows_done = (
            sem(n) for n in ("x_done", "ss_done", "var_done", "rs_done", "rows_done"))
        t_done, t_hi, t_lo = sem("t_done"), sem("t_hi"), sem("t_lo")
        proj_saved, proj_saved2 = sem("proj_saved"), sem("proj_saved2")
        z_done, ln_done, sp_done, spm_done, tri_done, a_done, am_done, pv_done = (
            sem(n) for n in ("z_done", "ln_done", "sp_done", "spm_done", "tri_done", "a_done", "am_done", "pv_done"))
        sbo_saved = sem("sbo_saved")
        zd_done, mx_done, e_done, w_done, wt_done, wt_saved, pvd_done = (
            sem(n) for n in ("zd_done", "mx_done", "e_done", "w_done", "wt_done", "wt_saved", "pvd_done"))
        raw_y = sem("raw_y")
        lam_sum, lam_exp, nlam_done = sem("lam_sum"), sem("lam_exp"), sem("nlam_done")
        vrow_mm, vrow_done, scratch_done, bias_in = sem("vrow_mm"), sem("vrow_done"), sem("scratch_done"), sem("bias_in")
        bias_mm, bias_done = sem("bias_mm"), sem("bias_done")
        silu_done, hid_done, hT_hi_done, hT_lo_done = (
            sem(n) for n in ("silu_done", "hid_done", "hT_hi_done", "hT_lo_done"))
        rT_done, lg_done, gap_done, ge_done, chosen_done, pos_done, tab_done = (
            sem(n) for n in ("rT_done", "lg_done", "gap_done", "ge_done", "chosen_done", "pos_done", "tab_done"))
        hn_hi_done, hn_lo_done = sem("hn_hi_done"), sem("hn_lo_done")
        ga_done, ga_hi, ga_lo = sem("ga_done"), sem("ga_hi"), sem("ga_lo")
        esilu_done, ehid_done, et_done, eh_hi, eh_lo = (
            sem(n) for n in ("esilu_done", "ehid_done", "et_done", "eh_hi", "eh_lo"))
        y_hi, y_lo = sem("y_hi"), sem("y_lo")
        sc_done, sc_added, hot_t, hot_saved, hot_ready = (
            sem(n) for n in ("sc_done", "sc_added", "hot_t", "hot_saved", "hot_ready"))
        out_rows, out_sent = sem("out_rows"), sem("out_sent")
        dve_chain, act_chain = sem("dve_chain"), sem("act_chain")

        win_v = [w_in[l].rearrange("(k p) n -> p k n", p=P) for l in range(DEPTH)]
        wout_v = [w_out[l].rearrange("(k p) n -> p k n", p=P) for l in range(DEPTH)]
        gate_v = dense_w_gate[0].rearrange("(k p) n -> p k n", p=P)
        up_v = dense_w_up[0].rearrange("(k p) n -> p k n", p=P)
        down_v = dense_w_down[0].rearrange("(f p) n -> p f n", p=P)
        egate_v = expert_w_gate[0].rearrange("e (k p) n -> e p k n", p=P)
        eup_v = expert_w_up[0].rearrange("e (k p) n -> e p k n", p=P)
        edown_v = expert_w_down[0].rearrange("e (f p) n -> e p f n", p=P)

        def halves(view, col):
            return [view[:, 4 * h:4 * h + 4, col:col + CH] for h in range(2)]

        sources = []
        for l in range(DEPTH):
            for u in range(PROJ // 2):
                sources += halves(win_v[l], u * CH)
            for u in range(WOUT // 2):
                sources += halves(wout_v[l], u * CH)
            if l == 0:
                for n in range(D_FULL):
                    sources += halves(gate_v, n * CH) + halves(up_v, n * CH)
                sources += [gate_v[:, :, D_FULL * CH:FD], up_v[:, :, D_FULL * CH:FD]]
                sources += [down_v[:, 2 * i:2 * i + 2, :] for i in range(DENSE_DN)]
        assert len(sources) == MOE0

        def expert_pieces():
            order = []
            for c in range(E_CH + 1):
                if c < E_CH:
                    order += [("gate", c, 0), ("gate", c, 1), ("up", c, 0), ("up", c, 1)]
                if c > 0:
                    order += [("down", c - 1, 0), ("down", c - 1, 1)]
            return order

        ORDER = expert_pieces()
        assert len(ORDER) == PER_BLOCK and PER_BLOCK % RAW == 0 and PER_BLOCK % SPL == 0
        AT = {k: i for i, k in enumerate(ORDER)}
        ROUNDS = PER_BLOCK // RAW

        def landed(n, b=None):
            return 16 * (n // RAW + 1) if b is None else b * (16 * ROUNDS) + 16 * (n // RAW + 1)

        def nth(n, b=None):
            return n if b is None else b * PER_BLOCK + n

        def split_hi(act, n, b=None):
            act.wait_ge(raw_in[n % RAW], landed(n, b))
            if n >= SPL:
                act.wait_ge(piece_used, nth(n - SPL + 1, b))
            nc.scalar.activation(w_hi[:, n % SPL, :], raw[:, n % RAW, :], ACT.Copy).then_inc(hi_ready, 1)

        def split_lo(dve, n, b=None):
            dve.wait_ge(hi_ready, nth(n + 1, b))
            nc.vector.tensor_tensor(w_lo[:, n % SPL, :], raw[:, n % RAW, :],
                                    w_hi[:, n % SPL, :].bitcast(F32), ALU.subtract).then_inc(lo_ready, 1)

        block = ctx.enter_context(nc.Block())

        @block.sync
        def _(sp):
            sp.dma_start(xs[:], x[0].rearrange("(t p) d -> p t d", p=P)).then_inc(x_in, 16)

            def load(n, src, b=None):
                if n >= RAW:
                    sp.wait_ge(lo_ready, nth(n - RAW + 1, b))
                dst = raw[:, n % RAW, :].rearrange("p (k n) -> p k n", n=src.shape[-1])
                sp.dma_start(dst, src).then_inc(raw_in[n % RAW], 16)

            for n, src in enumerate(sources):
                load(n, src)
            sp.wait_ge(tab_done, 1)
            blocks = sp.value_load(nbi[0:1, 0:1], min_val=4, max_val=MAX_BLOCKS)
            with sp.Fori(0, blocks) as b:
                e = sp.value_load(ebi[0:1, bass.ds(b, 1)], min_val=0, max_val=NE - 1)
                for i, (kind, c, h) in enumerate(ORDER):
                    if kind == "down":
                        src = edown_v[bass.ds(e, 1), :, 4 * c + 2 * h:4 * c + 2 * h + 2, :]
                    else:
                        v = egate_v if kind == "gate" else eup_v
                        src = v[bass.ds(e, 1), :, 4 * h:4 * h + 4, c * CH:c * CH + CH]
                    load(MOE0 + i, src.rearrange("e p k n -> (e p) k n"), b)
            sp.wait_ge(out_rows, TT)
            sp.dma_start(out[0].rearrange("(t p) d -> p t d", p=P), hn[:]).then_inc(out_sent, 16)
            sp.wait_ge(out_sent, 16)

        @block.gpsimd
        def _(pool):
            pool.dma_start(cst[:], consts[:, 0:CONSTS]).then_inc(cst_in, 16)
            norms = [attn_norm[0], ffn_norm[0], attn_norm[1], ffn_norm[1], final_norm]
            for m in range(2):
                pool.dma_start(gain[:, m, :], norms[m].partition_broadcast(P)).then_inc(gain_in[m], 16)
            for l in range(DEPTH):
                pool.dma_start(g_sb[:, l, :], sb_out_norm[l].partition_broadcast(P)).then_inc(small_in, 16)
                pool.dma_start(g_df[:, l, :], diff_subln[l].partition_broadcast(P)).then_inc(small_in, 16)
                for i, v in enumerate((lambda_q1, lambda_q2, lambda_k1, lambda_k2)):
                    pool.dma_start(lam_in[:, i, l, :], v[l].partition_broadcast(P)).then_inc(lam_ld, 16)

            def load_buckets():
                pool.dma_start(bkt[:, 0:384], consts[0:N_BUCKETS + 1, C_OH:C_OH + 384]).then_inc(bkt_in, 16)
                pool.dma_start(bkt[0:N_BUCKETS, 384:384 + DF_HEADS], rel_bias[:, :]).then_inc(bkt_in, 16)
                pool.dma_start(bkt[N_BUCKETS:N_BUCKETS + 1, 384:384 + DF_HEADS],
                               consts[N_BUCKETS:N_BUCKETS + 1, C_MASKED:C_FLIP]).then_inc(bkt_in, 16)
                pool.dma_start(flip[:], consts[:, C_FLIP:C_END]).then_inc(bkt_in, 16)

            load_buckets()

            def causal(tile, parity):
                v = tile[:, parity, :].rearrange("p (a q) -> p a q", q=P)[:, 0:3:2, :]
                return nc.gpsimd.affine_select(out=v, in_=v, compare_op=ALU.is_gt, fill=0.0, base=0,
                                               pattern=[[0, 2], [1, P]], channel_multiplier=-1)

            for l in range(DEPTH):
                if l == 0:
                    pool.wait_ge(vrow_done, 1)
                    pool.dma_start(scratch, vrow[:]).then_inc(scratch_done, 16)
                    pool.wait_ge(scratch_done, 16)
                    pool.dma_start(bias_up[:], bass.AP(scratch.tensor, 0, [[1, P], [384, DF_HEADS], [1, S]])).then_inc(bias_in, 16)
                if l == 1:
                    pool.wait_ge(rows_done, 3)
                    pool.dma_start(gain[:, 1, :], norms[3].partition_broadcast(P)).then_inc(gain_in[1], 16)
                for s in range(SB_HEADS + 1):
                    i = SB_HEADS * l + s
                    if s < SB_HEADS:
                        pool.wait_ge(sp_done, i + 1)
                        causal(spl, s % 2).then_inc(spm_done, 1)
                    if s >= 1:
                        pool.wait_ge(a_done, i)
                        causal(att, (s - 1) % 2).then_inc(am_done, 1)
                if l == 0:
                    pool.wait_ge(rows_done, 1)
                    pool.dma_start(gain[:, 0, :], norms[2].partition_broadcast(P)).then_inc(gain_in[0], 16)
                else:
                    pool.wait_ge(rows_done, 4)
                    pool.dma_start(gain[:, 0, :], norms[4].partition_broadcast(P)).then_inc(gain_in[0], 16)
            pool.wait_ge(piece_used, MOE0)
            pool.dma_start(rw[:], router_w[0].rearrange("(k p) e -> p k e", p=P)).then_inc(rw_in, 16)

        @block.tensor
        def _(pe):
            def mm3(o, s_hi, s_lo, m_hi, m_lo, start, stop):
                pe.matmul(o, s_hi, m_hi, start=start, stop=False, skip_group_check=True)
                pe.matmul(o, s_hi, m_lo, start=False, stop=False, skip_group_check=True)
                return pe.matmul(o, s_lo, m_hi, start=False, stop=stop, skip_group_check=True)

            def piece(n, b=None):
                pe.wait_ge(lo_ready, nth(n + 1, b))
                return w_hi[:, n % SPL, :], w_lo[:, n % SPL, :]

            def columns_out(n, bank, half, k_tiles=4, width=CH):
                hi, lo = piece(n)
                for ct in range(width // P):
                    o = ps[:, bank + ct // 2, (ct % 2) * S:(ct % 2) * S + S]
                    for k in range(k_tiles):
                        kk = k_tiles * half + k
                        c0 = k * width + ct * P
                        last = mm3(o, hi[:, c0:c0 + P], lo[:, c0:c0 + P], aT_hi[:, kk, :], aT_lo[:, kk, :],
                                   start=(kk == 0 and ct % 2 == 0), stop=(kk == KT - 1))
                last.then_inc(piece_used, 1)

            def rows_out(n, bank, half):
                hi, lo = piece(n)
                for t in range(TT):
                    for k in range(4):
                        kk = 4 * half + k
                        last = mm3(ps[:, bank + t, :], aT_hi[:, kk, t * P:t * P + P], aT_lo[:, kk, t * P:t * P + P],
                                   hi[:, k * CH:k * CH + CH], lo[:, k * CH:k * CH + CH],
                                   start=(kk == 0), stop=(kk == KT - 1))
                last.then_inc(piece_used, 1)

            def turn_rows(r):
                pe.wait_ge(rows_done, r + 1)
                for j in range(4):
                    for q in range(4):
                        k, t = 2 * j + q // 2, q % 2
                        last = pe.transpose(ps[:, 4 + j, q * P:q * P + P], hn[:, t, k * P:k * P + P], ident)
                    last.then_inc(t_done, 1)

            pe.wait_ge(cst_in, 16)
            pe.wait_ge(bkt_in, 64)
            pe.matmul(ps[0:DF_HEADS, 7, 0:384], bkt[:, 384:384 + DF_HEADS], bkt[:, 0:384],
                      start=True, stop=True).then_inc(vrow_mm, 1)
            pe.wait_ge(vrow_done, 1)
            for l in range(DEPTH):
                n0 = LAYER1 * l
                turn_rows(3 * l)
                if l == 0:
                    pe.wait_ge(bias_in, 16)
                    for h in range(DF_HEADS):
                        last = pe.matmul(ps[:, 2 + h // 2, (h % 2) * S:(h % 2) * S + S], flip[:], bias_up[:, h, :],
                                         start=(h % 2 == 0), stop=(h % 2 == 1), skip_group_check=True)
                    last.then_inc(bias_mm, 1)
                    pe.wait_ge(bias_done, 1)
                pe.wait_ge(t_lo, 12 * l + 4)

                def project(piece_of_layer):
                    u, half = piece_of_layer // 2, piece_of_layer % 2
                    if half == 0 and u >= 2:
                        pe.wait_ge(proj_saved if u % 2 == 0 else proj_saved2, 3 * l + u // 2)
                    (rows_out if u in (2, 5) else columns_out)(n0 + piece_of_layer, 2 * (u % 2), half)

                for i in range(6):
                    project(i)
                pe.wait_ge(proj_saved, 3 * l + 2)
                pe.wait_ge(proj_saved2, 3 * l + 1)
                for s in range(SB_HEADS + 2):
                    if s < SB_HEADS:
                        h0 = HD * (s % 2)
                        q = qk_sb[h0:h0 + HD, s // 2, :]
                        k = qk_sb[h0:h0 + HD, 4 + s // 2, :]
                        bank = ps[:, 4 + s % 2, :]
                        if s >= 2:
                            pe.wait_ge(a_done, SB_HEADS * l + s - 1)
                        pe.matmul(bank[:, 0:S], k[:, 0:P], q, start=True, stop=False, skip_group_check=True)
                        pe.matmul(bank[:, S:S + P], k[:, P:S], q[:, P:S], start=False, stop=False,
                                  skip_group_check=True).then_inc(z_done, 1)
                    if s < 6:
                        project(6 + s)
                    if 1 <= s <= SB_HEADS:
                        j = s - 1
                        bank = ps[:, 4 + j % 2, :]
                        pe.wait_ge(spm_done, SB_HEADS * l + j + 1)
                        pe.matmul(bank[:, 0:384], neg_tri, spl[:, j % 2, :], start=False, stop=False, skip_group_check=True)
                        pe.matmul(bank[:, P:S], neg_one, spl[:, j % 2, S:S + P], start=False, stop=True,
                                  skip_group_check=True).then_inc(tri_done, 1)
                    if s >= 2:
                        j = s - 2
                        pe.wait_ge(am_done, SB_HEADS * l + j + 1)
                        a = att[:, j % 2, :]
                        c = slice(HD * j, HD * j + HD)
                        pe.matmul(ps[:, 6, c], a[:, 0:P], v_sb[:, 0, c], start=True, stop=True, skip_group_check=True)
                        pe.matmul(ps[:, 7, c], a[:, P:S], v_sb[:, 0, c], start=True, stop=False, skip_group_check=True)
                        last = pe.matmul(ps[:, 7, c], a[:, S:384], v_sb[:, 1, c], start=False, stop=True, skip_group_check=True)
                last.then_inc(pv_done, 1)

                steps = 2 * DF_HEADS
                pe.wait_ge(proj_saved, 3 * l + 3)
                pe.wait_ge(proj_saved2, 3 * l + 3)
                for s in range(steps + 2):
                    if s < steps:
                        h, t = s // 2, s % 2
                        if s >= 2:
                            pe.wait_ge(wt_saved, steps * l + s - 1)
                        n_k = P * (t + 1)
                        for c in range(2):
                            q = qk_df[HD * c:HD * c + HD, h, t * P:t * P + P]
                            k = qk_df[HD * c:HD * c + HD, 4 + h, 0:n_k]
                            last = pe.matmul(ps[:, 4 * (s % 2) + c, 0:n_k], q, k, start=True, stop=True)
                        last.then_inc(zd_done, 1)
                    if 1 <= s <= steps:
                        j = s - 1
                        t = j % 2
                        pe.wait_ge(w_done, steps * l + j + 1)
                        for kb in range(t + 1):
                            last = pe.transpose(ps[:, 4 * (j % 2), kb * P:kb * P + P], wd[:, j % 2, kb * P:kb * P + P], ident)
                        last.then_inc(wt_done, 1)
                    if s >= 2:
                        j = s - 2
                        h, t = j // 2, j % 2
                        pe.wait_ge(wt_saved, steps * l + j + 1)
                        if j == 0:
                            pe.wait_ge(sbo_saved, l + 1)
                        c = slice(2 * HD * h, 2 * HD * h + 2 * HD)
                        for kb in range(t + 1):
                            last = pe.matmul(ps[:, 6 + t, c], wT[:, j % 2, kb * P:kb * P + P], v_df[:, kb, c],
                                             start=(kb == 0), stop=(kb == t), skip_group_check=True)
                last.then_inc(pvd_done, 1)

                turn_rows(3 * l + 1)
                pe.wait_ge(t_lo, 12 * l + 8)
                for u in range(2):
                    for half in range(2):
                        rows_out(n0 + PROJ + 2 * u + half, 2 * u, half)
                turn_rows(3 * l + 2)
                if l == 0:
                    pe.wait_ge(t_lo, 12)
                    for n in range(D_FULL + 1):
                        if n >= 2:
                            pe.wait_ge(hT_lo_done, n - 1)
                        g = PROJ + WOUT + 4 * n
                        bank = 4 * (n % 2)
                        if n < D_FULL:
                            for half in range(2):
                                columns_out(g + half, bank, half)
                            for half in range(2):
                                columns_out(g + 2 + half, bank + 2, half)
                        else:
                            columns_out(g, bank, 0, KT, D_REST)
                            columns_out(g + 1, bank + 2, 0, KT, D_REST)
                    pe.wait_ge(hT_lo_done, D_FULL + 1)
                    for i in range(DENSE_DN):
                        hi, lo = piece(PROJ + WOUT + DENSE_GU + i)
                        for t in range(TT):
                            for f in range(2):
                                ff = 2 * i + f
                                for c in range(2):
                                    at = f * D + c * CH
                                    last = mm3(ps[:, 2 * t + c, :], hT_hi[:, ff, t * P:t * P + P], hT_lo[:, ff, t * P:t * P + P],
                                               hi[:, at:at + CH], lo[:, at:at + CH], start=(ff == 0), stop=(ff == FT - 1))
                        last.then_inc(piece_used, 1)

            pe.wait_ge(rT_done, 4)
            pe.wait_ge(rw_in, 16)
            for t in range(TT):
                for k in range(KT):
                    last = pe.matmul(ps[:, 0, t * NE:t * NE + NE], rT[:, k, t * P:t * P + P], rw[:, k, :],
                                     start=(k == 0), stop=(k == KT - 1), skip_group_check=True)
            last.then_inc(lg_done, 1)
            pe.wait_ge(chosen_done, 1)
            pe.matmul(ps[:, 1, 0:NE], tri_strict, chosen[:, 0, :], start=True, stop=True, skip_group_check=True)
            pe.matmul(ps[:, 1, NE:2 * NE], tri_strict, chosen[:, 1, :], start=True, stop=False, skip_group_check=True)
            pe.matmul(ps[:, 1, NE:2 * NE], ones, chosen[:, 0, :], start=False, stop=True, skip_group_check=True)
            pe.matmul(ps[:, 1, 2 * NE:3 * NE], ones, chosen[:, 0, :], start=True, stop=False, skip_group_check=True)
            pe.matmul(ps[:, 1, 2 * NE:3 * NE], ones, chosen[:, 1, :], start=False, stop=True,
                      skip_group_check=True).then_inc(pos_done, 1)

            def gather(count):
                pe.wait_ge(hot_ready, count)
                for j in range(2):
                    for q in range(4):
                        k = 4 * j + q
                        for t in range(TT):
                            for part in (hn_hi, hn_lo):
                                last = pe.matmul(ps[:, 1 + 2 * j, q * P:q * P + P], part[:, t, k * P:k * P + P], onehot[:, t, :],
                                                 start=(t == 0 and part is hn_hi), stop=(t == 1 and part is hn_lo),
                                                 skip_group_check=True)
                last.then_inc(ga_done, 1)

            def scatter(t):
                for c in range(2):
                    for part in (ye_hi, ye_lo):
                        last = pe.matmul(ps[:, 6 + c, :], onehotT[:, t, :], part[:, c * CH:c * CH + CH],
                                         start=(part is ye_hi), stop=(part is ye_lo), skip_group_check=True)
                last.then_inc(sc_done, 1)

            pe.wait_ge(tab_done, 1)
            blocks = pe.value_load(nbi[0:1, 0:1], min_val=4, max_val=MAX_BLOCKS)
            pe.wait_ge(hn_lo_done, 1)
            pe.wait_ge(hot_saved, 1)
            for c in range(2):
                pe.matmul(ps[:, 4 + c, :], onehotT[:, 0, :], hn_hi[:, 0, c * CH:c * CH + CH], start=True, stop=True)
            gather(1)
            with pe.Fori(0, blocks) as b:
                pe.wait_ge(ga_lo, b + 1)

                def expert_in(kind, c, half):
                    n = MOE0 + AT[(kind, c, half)]
                    hi, lo = piece(n, b)
                    bank = (0 if kind == "gate" else 2) + c % 2
                    for k in range(4):
                        kk = 4 * half + k
                        last = mm3(ps[:, bank, :], xe_hi[:, kk, :], xe_lo[:, kk, :], hi[:, k * CH:k * CH + CH],
                                   lo[:, k * CH:k * CH + CH], start=(kk == 0), stop=(kk == KT - 1))
                    last.then_inc(piece_used, 1)

                def turn_hidden(c):
                    pe.wait_ge(ehid_done, b * E_CH + c + 1)
                    for f in range(4):
                        last = pe.transpose(ps[:, 7, f * P:f * P + P], hid[:, c % 2, f * P:f * P + P], ident)
                    last.then_inc(et_done, 1)

                def expert_down(c, half):
                    hi, lo = piece(MOE0 + AT[("down", c, half)], b)
                    if half == 0:
                        pe.wait_ge(eh_lo, b * E_CH + c + 1)
                    for f in range(2):
                        ff = 2 * half + f
                        for o in range(2):
                            at = f * D + o * CH
                            last = mm3(ps[:, 4 + o, :], he_hi[:, ff, :], he_lo[:, ff, :], hi[:, at:at + CH], lo[:, at:at + CH],
                                       start=(c == 0 and ff == 0), stop=(c == E_CH - 1 and ff == 3))
                    last.then_inc(piece_used, 1)

                for c in range(E_CH + 1):
                    if c < E_CH:
                        expert_in("gate", c, 0)
                        expert_in("gate", c, 1)
                    if c == 0:
                        pe.wait_ge(y_lo, b + 1)
                        pe.wait_ge(hot_saved, b + 1)
                        scatter(0)
                    if c == 1:
                        pe.wait_ge(sc_added, b * TT + TT)
                    if c > 0:
                        turn_hidden(c - 1)
                    if c == 2:
                        for t in range(TT):
                            last = pe.transpose(ps[:, 6, t * P:t * P + P], onehot[:, t, :].bitcast(F32), ident)
                        last.then_inc(hot_t, 1)
                    if c < E_CH:
                        expert_in("up", c, 0)
                        expert_in("up", c, 1)
                    else:
                        gather(b + 2)
                    if c == 0:
                        pe.wait_ge(sc_added, b * TT + 1)
                        scatter(1)
                    if c > 0:
                        expert_down(c - 1, 0)
                        expert_down(c - 1, 1)
            pe.wait_ge(y_lo, blocks + 1)
            pe.wait_ge(hot_saved, blocks + 1)
            for t in range(TT):
                if t == 1:
                    pe.wait_ge(sc_added, blocks * TT + 1)
                scatter(t)

        @block.scalar
        def _(act):
            steps = [0]

            def link(ins):
                steps[0] += 1
                ins.then_inc(act_chain, 1)
                act.wait_ge(act_chain, steps[0])

            events = [0]

            def inverse_root(width):
                events[0] += 1
                act.wait_ge(var_done, events[0])
                link(nc.scalar.activation(lnv[:, 0:width], var[:, 0:width], ACT.Ln))
                nc.scalar.activation(rs0[:, 0:width], lnv[:, 0:width], ACT.Exp, scale=-0.5).then_inc(rs_done, 1)

            def norm(m):
                if m == 0:
                    act.wait_ge(x_in, 16)
                else:
                    act.wait_ge(x_done, m)
                for t in range(TT):
                    last = nc.scalar.activation(sq[:, :], xs[:, t, :], ACT.Square, accum_out=ss[:, t:t + 1])
                    if t == 0:
                        link(last)
                last.then_inc(ss_done, 1)
                inverse_root(TT)

            def turned(r):
                for j in range(4):
                    act.wait_ge(t_done, 4 * r + j + 1)
                    if r == 5:
                        nc.scalar.activation(rT[:, 2 * j:2 * j + 2, :].rearrange("p a s -> p (a s)"), ps[:, 4 + j, :],
                                             ACT.Copy).then_inc(rT_done, 1)
                    else:
                        nc.scalar.activation(aT_hi[:, 2 * j:2 * j + 2, :].rearrange("p a s -> p (a s)"), ps[:, 4 + j, :],
                                             ACT.Copy).then_inc(t_hi, 1)

            for l in range(DEPTH):
                n0 = LAYER1 * l
                for n in range(n0, n0 + 3):
                    split_hi(act, n)
                if l == 0:
                    act.wait_ge(lam_sum, 1)
                    nc.scalar.activation(lam_e[:], lam_s[:], ACT.Exp).then_inc(lam_exp, 1)
                norm(2 * l)
                turned(3 * l)

                def save_columns(u):
                    act.wait_ge(piece_used, n0 + 2 * u + 2)
                    dst = qk_sb if u == 0 else qk_df
                    return nc.scalar.activation(dst[:, 0:4, :].rearrange("p a s -> p (a s)"),
                                                ps[:, 2 * (u % 2):2 * (u % 2) + 2, :].rearrange("p a s -> p (a s)"),
                                                ACT.Copy, scale=HD ** -0.5)

                for n in range(3, 6):
                    split_hi(act, n0 + n)
                    if n == 4:
                        save_columns(0).then_inc(proj_saved, 1)
                split_hi(act, n0 + 6)
                act.wait_ge(piece_used, n0 + 6)
                nc.scalar.activation(v_sb[:].rearrange("p a s -> p (a s)"), ps[:, 0:2, :].rearrange("p a s -> p (a s)"),
                                     ACT.Copy).then_inc(proj_saved, 1)
                split_hi(act, n0 + 7)
                for s in range(SB_HEADS + 1):
                    if s < SB_HEADS:
                        act.wait_ge(z_done, SB_HEADS * l + s + 1)
                        link(nc.scalar.activation(ab[:, s % 2, :], ps[:, 4 + s % 2, 0:384], ACT.Abs))
                        link(nc.scalar.activation(ab[:, s % 2, :], ab[:, s % 2, :], ACT.Exp, scale=-1.0))
                        nc.scalar.activation(ab[:, s % 2, :], ab[:, s % 2, :], ACT.Ln, bias=1.0).then_inc(ln_done, 1)
                    if s < 7:
                        split_hi(act, n0 + 8 + s)
                    if s == 2:
                        save_columns(3).then_inc(proj_saved2, 1)
                    if s == 4:
                        act.wait_ge(piece_used, n0 + 10)
                        nc.scalar.activation(qk_df[:, 4:8, :].rearrange("p a s -> p (a s)"),
                                             ps[:, 0:2, :].rearrange("p a s -> p (a s)"), ACT.Copy).then_inc(proj_saved, 1)
                    if s >= 1:
                        j = s - 1
                        act.wait_ge(tri_done, SB_HEADS * l + j + 1)
                        nc.scalar.activation(att[:, j % 2, :], ps[:, 4 + j % 2, 0:384], ACT.Exp).then_inc(a_done, 1)
                act.wait_ge(pv_done, l + 1)
                nc.scalar.activation(sq[:, :], ps[:, 6:8, :].rearrange("p a s -> p (a s)"), ACT.Square).then_inc(ss_done, 1)
                inverse_root(TT * SB_HEADS)

                n_steps = 2 * DF_HEADS
                for s in range(n_steps + 1):
                    if s < n_steps:
                        n_k = P * (s % 2 + 1)
                        act.wait_ge(mx_done, n_steps * l + s + 1)
                        for c in range(2):
                            z = zb[:, s % 2, c, 0:n_k]
                            last = nc.scalar.activation(z, z, ACT.Exp, bias=mx[:, s % 2, c:c + 1],
                                                        accum_out=es[:, s % 2, c:c + 1])
                        last.then_inc(e_done, 1)
                    if s >= 1:
                        j = s - 1
                        n_k = P * (j % 2 + 1)
                        act.wait_ge(wt_done, n_steps * l + j + 1)
                        nc.scalar.activation(wT[:, j % 2, 0:n_k], ps[:, 4 * (j % 2), 0:n_k], ACT.Copy).then_inc(wt_saved, 1)
                act.wait_ge(raw_y, l + 1)
                for t in range(TT):
                    last = nc.scalar.activation(sq[:, t * HALF:(t + 1) * HALF], hn[:, t, HALF:D], ACT.Square)
                last.then_inc(ss_done, 1)
                inverse_root(TT * DF_HEADS)
                turned(3 * l + 1)
                split_hi(act, n0 + 15)
                if l == 0:
                    for n in range(16, 19):
                        split_hi(act, n)
                norm(2 * l + 1)
                turned(3 * l + 2)
                if l == 0:
                    for n in range(D_FULL + 1):
                        last_chunk = n == D_FULL
                        g = PROJ + WOUT + 4 * n
                        for i in range(g + 3, min(g + 7, PROJ + WOUT + DENSE_GU)):
                            split_hi(act, i)
                        if last_chunk:
                            for i in range(PROJ + WOUT + DENSE_GU, PROJ + WOUT + DENSE_GU + 2):
                                split_hi(act, i)
                        bank = 4 * (n % 2)
                        width = D_REST * TT if last_chunk else 2 * CH
                        act.wait_ge(piece_used, min(g + 4, PROJ + WOUT + DENSE_GU))
                        h = hn[:, n % 2, 0:width]
                        nc.scalar.activation(h, ps[:, bank:bank + 2, :].rearrange("p a s -> p (a s)")[:, 0:width],
                                             ACT.Silu).then_inc(silu_done, 1)
                        act.wait_ge(hid_done, n + 1)
                        nc.scalar.activation(hT_hi[:, 4 * n:4 * n + width // S, :].rearrange("p a s -> p (a s)"), h,
                                             ACT.Copy).then_inc(hT_hi_done, 1)
                    for i in range(PROJ + WOUT + DENSE_GU + 2, LAYER1):
                        split_hi(act, i)

            act.wait_ge(lg_done, 1)
            for t in range(TT):
                last = nc.scalar.activation(hn_hi[:, t, :], hn[:, t, :], ACT.Copy)
            last.then_inc(hn_hi_done, 1)
            act.wait_ge(gap_done, 1)
            nc.scalar.activation(ed[:], dm[:], ACT.Exp).then_inc(ge_done, 1)

            def gathered(count):
                act.wait_ge(ga_done, count)
                for j in range(2):
                    nc.scalar.activation(xe_hi[:, 4 * j:4 * j + 4, :].rearrange("p a s -> p (a s)"), ps[:, 1 + 2 * j, :],
                                         ACT.Copy).then_inc(ga_hi, 1)

            def output_hi(b):
                act.wait_ge(piece_used, nth(MOE0, b))
                nc.scalar.activation(ye_hi[:], ps[:, 4:6, :].rearrange("p a s -> p (a s)"), ACT.Copy).then_inc(y_hi, 1)

            act.wait_ge(tab_done, 1)
            blocks = act.value_load(nbi[0:1, 0:1], min_val=4, max_val=MAX_BLOCKS)
            gathered(1)
            with act.Fori(0, blocks) as b:
                def hi_of(kind, c, half):
                    split_hi(act, MOE0 + AT[(kind, c, half)], b)

                def silu(c):
                    act.wait_ge(piece_used, nth(MOE0 + AT[("up", c, 1)] + 1, b))
                    nc.scalar.activation(sil[:, c % 2, :], ps[:, c % 2, :], ACT.Silu).then_inc(esilu_done, 1)

                for c in range(E_CH + 1):
                    if c < E_CH:
                        hi_of("gate", c, 0)
                    if c == 0:
                        output_hi(b)
                    else:
                        silu(c - 1)
                    if c < E_CH:
                        hi_of("gate", c, 1)
                        hi_of("up", c, 0)
                        hi_of("up", c, 1)
                    else:
                        hi_of("down", c - 1, 0)
                        hi_of("down", c - 1, 1)
                    if c > 0:
                        act.wait_ge(et_done, b * E_CH + c)
                        nc.scalar.activation(he_hi[:].rearrange("p a s -> p (a s)"), ps[:, 7, :], ACT.Copy).then_inc(eh_hi, 1)
                        if c < E_CH:
                            hi_of("down", c - 1, 0)
                            hi_of("down", c - 1, 1)
                gathered(b + 2)
            output_hi(blocks)
            act.wait_ge(x_done, 4)
            for t in range(TT):
                last = nc.scalar.activation(sq[:, :], xs[:, t, :], ACT.Square, accum_out=ss[:, t:t + 1])
                if t == 0:
                    link(last)
            last.then_inc(ss_done, 1)
            inverse_root(TT)

        @block.vector
        def _(dve):
            steps = [0]

            def link(ins):
                steps[0] += 1
                ins.then_inc(dve_chain, 1)
                dve.wait_ge(dve_chain, steps[0])

            events = [0]
            V = nc.vector

            def newton(width):
                events[0] += 1
                dve.wait_ge(rs_done, events[0])
                y, v = rs0[:, 0:width], var[:, 0:width]
                link(V.tensor_tensor(nw1[:, 0:width], y, y, ALU.mult))
                link(V.tensor_tensor(nw2[:, 0:width], nw1[:, 0:width], v, ALU.mult))
                link(V.tensor_scalar(nw1[:, 0:width], nw2[:, 0:width], -0.5, 1.5, ALU.mult, ALU.add))
                link(V.tensor_tensor(rstd[:, 0:width], nw1[:, 0:width], y, ALU.mult))

            def variance(width, size):
                V.tensor_scalar(var[:, 0:width], ss[:, 0:width], 1.0 / size, EPS, ALU.mult, ALU.add).then_inc(var_done, 1)

            def norm(m):
                dve.wait_ge(ss_done, [1, 4, 5, 8, 9][m])
                variance(TT, D)
                newton(TT)
                dve.wait_ge(gain_in[m % 2], 16 * (m // 2 + 1))
                for t in range(TT):
                    last = V.scalar_tensor_tensor(out=hn[:, t, :], in0=xs[:, t, :], scalar=rstd[:, t:t + 1],
                                                  in1=gain[:, m % 2, :], op0=ALU.mult, op1=ALU.mult)
                    if m == 4:
                        last.then_inc(out_rows, 1)
                if m < 4:
                    last.then_inc(rows_done, 1)

            def turned(r):
                for j in range(4):
                    dve.wait_ge(t_hi, 4 * r + j + 1)
                    V.tensor_tensor(aT_lo[:, 2 * j:2 * j + 2, :].rearrange("p a s -> p (a s)"), ps[:, 4 + j, :],
                                    aT_hi[:, 2 * j:2 * j + 2, :].rearrange("p a s -> p (a s)").bitcast(F32),
                                    ALU.subtract).then_inc(t_lo, 1)

            dve.wait_ge(lam_ld, 16 * 4 * DEPTH)
            link(V.tensor_tensor(lam_pr[:], lam_in[:, 0:2], lam_in[:, 2:4], ALU.mult))
            V.tensor_reduce(lam_s[:], lam_pr[:], AX.X, ALU.add).then_inc(lam_sum, 1)
            dve.wait_ge(vrow_mm, 1)
            V.tensor_copy(vrow[:], ps[0:DF_HEADS, 7, 0:384]).then_inc(vrow_done, 1)
            dve.wait_ge(small_in, 16 * 2 * DEPTH)
            for l in range(DEPTH):
                link(V.tensor_scalar(g_df[:, l, :], g_df[:, l, :], 1.0 - lambda_init(l), None, ALU.mult))
            for n in range(3):
                split_lo(dve, n)
            dve.wait_ge(lam_exp, 1)
            link(V.tensor_tensor(lam_d[:], lam_e[:, 1, :], lam_e[:, 0, :], ALU.subtract))
            for l in range(DEPTH):
                link(V.tensor_scalar(nlam[:, l:l + 1], lam_d[:, l:l + 1], -lambda_init(l), None, ALU.add))

            for l in range(DEPTH):
                n0 = LAYER1 * l
                if l == 1:
                    for n in range(n0, n0 + 3):
                        split_lo(dve, n)
                norm(2 * l)
                turned(3 * l)
                if l == 0:
                    dve.wait_ge(bias_mm, 1)
                    V.tensor_copy(bias[:].rearrange("p h k -> p (h k)"), ps[:, 2:4, :].rearrange("p a s -> p (a s)")).then_inc(bias_done, 1)
                for n in range(3, 7):
                    split_lo(dve, n0 + n)
                    if n == 5:
                        dve.wait_ge(piece_used, n0 + 4)
                        V.tensor_copy(qk_sb[:, 4:8, :].rearrange("p a s -> p (a s)"),
                                      ps[:, 2:4, :].rearrange("p a s -> p (a s)")).then_inc(proj_saved2, 1)
                split_lo(dve, n0 + 7)
                for s in range(SB_HEADS):
                    dve.wait_ge(ln_done, SB_HEADS * l + s + 1)
                    V.scalar_tensor_tensor(out=spl[:, s % 2, :], in0=ps[:, 4 + s % 2, 0:384], scalar=0.0,
                                           in1=ab[:, s % 2, :], op0=ALU.max, op1=ALU.add).then_inc(sp_done, 1)
                    if s < 7:
                        split_lo(dve, n0 + 8 + s)
                    if s == 6:
                        dve.wait_ge(piece_used, n0 + 12)
                        V.tensor_copy(v_df[:].rearrange("p a s -> p (a s)"),
                                      ps[:, 2:4, :].rearrange("p a s -> p (a s)")).then_inc(proj_saved2, 1)
                dve.wait_ge(ss_done, 4 * l + 2)
                link(V.tensor_reduce(ss[:, 0:16], sq[:].rearrange("p (a d) -> p a d", d=HD), AX.X, ALU.add))
                variance(16, HD)
                newton(16)
                for t in range(TT):
                    last = V.tensor_tensor(hn[:, t, 0:HALF].rearrange("p (h d) -> p h d", d=HD),
                                           ps[:, 6 + t, :].rearrange("p (h d) -> p h d", d=HD),
                                           rstd[:, 8 * t:8 * t + 8].unsqueeze(2).to_broadcast([P, SB_HEADS, HD]), ALU.mult)
                last.then_inc(sbo_saved, 1)
                dve.wait_ge(sbo_saved, l + 1)
                for t in range(TT):
                    hv = hn[:, t, 0:HALF].rearrange("p (h d) -> p h d", d=HD)
                    V.tensor_tensor(hv, hv, g_sb[:, l, :].unsqueeze(1).to_broadcast([P, SB_HEADS, HD]), ALU.mult)

                n_steps = 2 * DF_HEADS

                def scores(s):
                    h, n_k = s // 2, P * (s % 2 + 1)
                    dve.wait_ge(zd_done, n_steps * l + s + 1)
                    z = zb[:, s % 2, :, 0:n_k]
                    link(V.tensor_tensor(z, ps[:, 4 * (s % 2):4 * (s % 2) + 2, 0:n_k],
                                         bias[:, h, S - n_k:S].unsqueeze(1).to_broadcast([P, 2, n_k]), ALU.add))
                    V.tensor_reduce(mx[:, s % 2, :], z, AX.X, ALU.max, negate=True).then_inc(mx_done, 1)

                def weigh(s):
                    h, t, n_k = s // 2, s % 2, P * (s % 2 + 1)
                    dve.wait_ge(e_done, n_steps * l + s + 1)
                    link(V.reciprocal(rr[:, t, h, :], es[:, s % 2, :]))
                    link(V.scalar_tensor_tensor(out=coef[:, s % 2, :], in0=es[:, s % 2, 0:1], scalar=nlam[:, l:l + 1],
                                                in1=rr[:, t, h, 1:2], op0=ALU.mult, op1=ALU.mult))
                    V.scalar_tensor_tensor(out=wd[:, s % 2, 0:n_k], in0=zb[:, s % 2, 1, 0:n_k], scalar=coef[:, s % 2, :],
                                           in1=zb[:, s % 2, 0, 0:n_k], op0=ALU.mult, op1=ALU.add).then_inc(w_done, 1)

                scores(0)
                for s in range(n_steps):
                    if s + 1 < n_steps:
                        scores(s + 1)
                    weigh(s)
                dve.wait_ge(pvd_done, l + 1)
                for t in range(TT):
                    last = V.tensor_tensor(hn[:, t, HALF:D].rearrange("p (h d) -> p h d", h=DF_HEADS),
                                           ps[:, 6 + t, :].rearrange("p (h d) -> p h d", h=DF_HEADS),
                                           rr[:, t, :, 0:1].to_broadcast([P, DF_HEADS, 2 * HD]), ALU.mult)
                last.then_inc(raw_y, 1)
                dve.wait_ge(ss_done, 4 * l + 3)
                link(V.tensor_reduce(ss[:, 0:8], sq[:].rearrange("p (a d) -> p a d", d=2 * HD), AX.X, ALU.add))
                variance(8, 2 * HD)
                newton(8)
                for t in range(TT):
                    hv = hn[:, t, HALF:D].rearrange("p (h d) -> p h d", h=DF_HEADS)
                    last = V.tensor_tensor(hv, hv, rstd[:, 4 * t:4 * t + 4].unsqueeze(2).to_broadcast([P, DF_HEADS, 2 * HD]),
                                           ALU.mult)
                link(last)
                for t in range(TT):
                    hv = hn[:, t, HALF:D].rearrange("p (h d) -> p h d", h=DF_HEADS)
                    last = V.tensor_tensor(hv, hv, g_df[:, l, :].unsqueeze(1).to_broadcast([P, DF_HEADS, 2 * HD]), ALU.mult)
                last.then_inc(rows_done, 1)
                turned(3 * l + 1)
                split_lo(dve, n0 + 15)
                if l == 0:
                    for n in range(16, 19):
                        split_lo(dve, n)
                for u in range(2):
                    dve.wait_ge(piece_used, n0 + PROJ + 2 * u + 2)
                    for t in range(TT):
                        xv = xs[:, t, u * CH:u * CH + CH]
                        last = V.tensor_tensor(xv, xv, ps[:, 2 * u + t, :], ALU.add)
                last.then_inc(x_done, 1)
                norm(2 * l + 1)
                if l == 0:
                    turned(2)
                    for n in range(D_FULL + 1):
                        last_chunk = n == D_FULL
                        g = PROJ + WOUT + 4 * n
                        for i in range(g + 3, min(g + 7, PROJ + WOUT + DENSE_GU)):
                            split_lo(dve, i)
                        if last_chunk:
                            for i in range(PROJ + WOUT + DENSE_GU, PROJ + WOUT + DENSE_GU + 2):
                                split_lo(dve, i)
                        bank = 4 * (n % 2) + 2
                        width = D_REST * TT if last_chunk else 2 * CH
                        dve.wait_ge(silu_done, n + 1)
                        h = hn[:, n % 2, 0:width]
                        V.tensor_tensor(h, h, ps[:, bank:bank + 2, :].rearrange("p a s -> p (a s)")[:, 0:width],
                                        ALU.mult).then_inc(hid_done, 1)
                        dve.wait_ge(hT_hi_done, n + 1)
                        V.tensor_tensor(hT_lo[:, 4 * n:4 * n + width // S, :].rearrange("p a s -> p (a s)"), h,
                                        hT_hi[:, 4 * n:4 * n + width // S, :].rearrange("p a s -> p (a s)").bitcast(F32),
                                        ALU.subtract).then_inc(hT_lo_done, 1)
                    for i in range(PROJ + WOUT + DENSE_GU + 2, LAYER1):
                        split_lo(dve, i)
                    dve.wait_ge(piece_used, LAYER1)
                    for t in range(TT):
                        last = V.tensor_tensor(xs[:, t, :], xs[:, t, :],
                                               ps[:, 2 * t:2 * t + 2, :].rearrange("p a s -> p (a s)"), ALU.add)
                    last.then_inc(x_done, 1)

            def row(a, width=NE):
                return cst[:, a:a + width]

            def over_e(a):
                return a.unsqueeze(2).to_broadcast([P, TT, NE])

            dve.wait_ge(lg_done, 1)
            link(V.tensor_copy(lg[:].rearrange("p t e -> p (t e)"), ps[:, 0, 0:TT * NE]))
            rev = row(C_REV).unsqueeze(1).to_broadcast([P, TT, NE])
            for lgs, m, eq, rk, r, oh in ((lg, m1, eq1, rk1, r1, oh1), (lg2, m2, eq2, rk2, r2, oh2)):
                link(V.tensor_reduce(m[:], lgs[:], AX.X, ALU.max))
                link(V.tensor_tensor(eq[:], lgs[:], over_e(m[:]), ALU.is_equal))
                link(V.tensor_tensor(rk[:], eq[:], rev, ALU.mult))
                link(V.tensor_reduce(r[:], rk[:], AX.X, ALU.max))
                link(V.tensor_tensor(oh[:], rk[:], over_e(r[:]), ALU.is_equal))
                if lgs is lg:
                    link(V.scalar_tensor_tensor(out=lg2[:], in0=oh1[:], scalar=-3.0e38, in1=lg[:], op0=ALU.mult, op1=ALU.add))
            V.tensor_tensor(chosen[:], oh1[:], oh2[:], ALU.add).then_inc(chosen_done, 1)
            V.tensor_tensor(dm[:], m2[:], m1[:], ALU.subtract).then_inc(gap_done, 1)
            dve.wait_ge(ge_done, 1)
            link(V.tensor_scalar(dn[:], ed[:], 1.0, None, ALU.add))
            link(V.reciprocal(g1[:], dn[:]))
            link(V.tensor_tensor(g2[:], ed[:], g1[:], ALU.mult))
            link(V.tensor_tensor(gg1[:], oh1[:], over_e(g1[:]), ALU.mult))
            link(V.tensor_tensor(gg[:], oh2[:], over_e(g2[:]), ALU.mult))
            link(V.tensor_tensor(gg[:], gg[:], gg1[:], ALU.add))
            dve.wait_ge(pos_done, 1)
            link(V.tensor_scalar(posm0[:].rearrange("p t e -> p (t e)"), ps[:, 1, 0:TT * NE], NOT_CHOSEN, None, ALU.add))
            link(V.tensor_tensor(pm1[:], posm0[:], chosen[:], ALU.mult))
            link(V.tensor_scalar(posm[:], pm1[:], -NOT_CHOSEN, None, ALU.add))
            link(V.tensor_copy(cnt[:], ps[:, 1, TT * NE:TT * NE + NE]))
            link(V.tensor_scalar(nb1[:], cnt[:], 0.0, None, ALU.is_gt))
            link(V.tensor_scalar(nb2[:], cnt[:], float(P), None, ALU.is_gt))
            link(V.tensor_tensor(nbe[:], nb1[:], nb2[:], ALU.add))
            link(V.tensor_tensor(le8[:], cst[:, C_LE:C_LE + NE * NE].rearrange("p (j e) -> p j e", e=NE),
                                 nbe[:].unsqueeze(1).to_broadcast([P, NE, NE]), ALU.mult))
            link(V.tensor_reduce(ends[:], le8[:], AX.X, ALU.add))
            ends_b = ends[:].unsqueeze(1).to_broadcast([P, TAB, NE])
            link(V.tensor_tensor(cmpb[:], ends_b, row(C_B, TAB).unsqueeze(2).to_broadcast([P, TAB, NE]), ALU.is_le))
            link(V.tensor_reduce(eb[:], cmpb[:], AX.X, ALU.add))
            link(V.tensor_tensor(stb[:], cmpb[:], ends_b, ALU.mult))
            link(V.tensor_reduce(start[:], stb[:], AX.X, ALU.max))
            link(V.tensor_tensor(local[:], row(C_B, TAB), start[:], ALU.subtract))
            link(V.tensor_tensor(cm[:], row(C_E).unsqueeze(1).to_broadcast([P, TAB, NE]),
                                 eb[:].unsqueeze(2).to_broadcast([P, TAB, NE]), ALU.is_equal))
            link(V.memset(gate_prev[:], 0.0))
            for t in range(TT):
                for i, (table, res) in enumerate(((posm, sel0), (gg, gate_prev[:, :, 1:TAB + 1]))):
                    link(V.tensor_tensor(tmpb[:, i, t], cm[:], table[:, t, :].unsqueeze(1).to_broadcast([P, TAB, NE]), ALU.mult))
                    link(V.tensor_reduce(res[:, t, :], tmpb[:, i, t], AX.X, ALU.add))
                link(V.scalar_tensor_tensor(out=sel[:, t, :], in0=local[:], scalar=-float(P), in1=sel0[:, t, :],
                                            op0=ALU.mult, op1=ALU.add))
            link(V.tensor_scalar(ebi[:], eb[:], float(NE - 1), None, ALU.min))
            V.tensor_copy(nbi[:], ends[:, NE - 1:NE]).then_inc(tab_done, 1)
            V.memset(onehotT[:].bitcast(F32), 0.0).then_inc(hot_saved, 1)
            dve.wait_ge(hn_hi_done, 1)
            for t in range(TT):
                last = V.tensor_tensor(hn_lo[:, t, :], hn[:, t, :], hn_hi[:, t, :].bitcast(F32), ALU.subtract)
            last.then_inc(hn_lo_done, 1)

            def one_hot(b):
                for t in range(TT):
                    last = V.tensor_scalar(onehot[:, t, :], iota, sel[:, t, bass.ds(b, 1)], None, ALU.is_equal)
                last.then_inc(hot_ready, 1)

            def gathered(count):
                for j in range(2):
                    dve.wait_ge(ga_hi, count + j - 1)
                    last = V.tensor_tensor(xe_lo[:, 4 * j:4 * j + 4, :].rearrange("p a s -> p (a s)"), ps[:, 1 + 2 * j, :],
                                           xe_hi[:, 4 * j:4 * j + 4, :].rearrange("p a s -> p (a s)").bitcast(F32),
                                           ALU.subtract)
                last.then_inc(ga_lo, 1)

            def output_lo(count):
                dve.wait_ge(y_hi, count)
                V.tensor_tensor(ye_lo[:], ps[:, 4:6, :].rearrange("p a s -> p (a s)"), ye_hi[:].bitcast(F32),
                                ALU.subtract).then_inc(y_lo, 1)

            def add_back(t, gate_at, count):
                dve.wait_ge(sc_done, count)
                return V.scalar_tensor_tensor(out=xs[:, t, :], in0=ps[:, 6:8, :].rearrange("p a s -> p (a s)"),
                                              scalar=gate_at, in1=xs[:, t, :], op0=ALU.mult, op1=ALU.add)

            dve.wait_ge(tab_done, 1)
            blocks = dve.value_load(nbi[0:1, 0:1], min_val=4, max_val=MAX_BLOCKS)
            one_hot(0)
            gathered(2)
            with dve.Fori(0, blocks) as b:
                def lo_of(kind, c, half):
                    split_lo(dve, MOE0 + AT[(kind, c, half)], b)

                for c in range(E_CH + 1):
                    if c < E_CH:
                        lo_of("gate", c, 0)
                    if c == 0:
                        output_lo(b + 1)
                    else:
                        dve.wait_ge(esilu_done, b * E_CH + c)
                        V.tensor_tensor(hid[:, (c - 1) % 2, :], sil[:, (c - 1) % 2, :], ps[:, 2 + (c - 1) % 2, :],
                                        ALU.mult).then_inc(ehid_done, 1)
                    if c == 1:
                        add_back(1, gate_prev[:, 1, bass.ds(b, 1)], b * TT + 2).then_inc(sc_added, 1)
                    if c < E_CH:
                        lo_of("gate", c, 1)
                        lo_of("up", c, 0)
                        if c == 0:
                            add_back(0, gate_prev[:, 0, bass.ds(b, 1)], b * TT + 1).then_inc(sc_added, 1)
                        lo_of("up", c, 1)
                    else:
                        lo_of("down", c - 1, 0)
                        lo_of("down", c - 1, 1)
                    if c == 2:
                        dve.wait_ge(hot_t, b + 1)
                        V.tensor_copy(onehotT[:].rearrange("p t s -> p (t s)"), ps[:, 6, 0:TT * P]).then_inc(hot_saved, 1)
                    if c == 4:
                        one_hot(b + 1)
                    if c > 0:
                        dve.wait_ge(eh_hi, b * E_CH + c)
                        V.tensor_tensor(he_lo[:].rearrange("p a s -> p (a s)"), ps[:, 7, :],
                                        he_hi[:].rearrange("p a s -> p (a s)").bitcast(F32), ALU.subtract).then_inc(eh_lo, 1)
                        if c < E_CH:
                            lo_of("down", c - 1, 0)
                            lo_of("down", c - 1, 1)
                gathered(b * 2 + 4)
            output_lo(blocks + 1)
            for t in range(TT):
                add_back(t, gate_prev[:, t, bass.ds(blocks, 1)], blocks * TT + t + 1).then_inc(sc_added if t == 0 else x_done, 1)
            norm(4)


_INS = ["x", "w_in", "w_out", "attn_norm", "ffn_norm", "sb_out_norm", "diff_subln", "lambda_q1", "lambda_k1",
        "lambda_q2", "lambda_k2", "rel_bias", "dense_w_gate", "dense_w_up", "dense_w_down", "router_w",
        "expert_w_gate", "expert_w_up", "expert_w_down", "final_norm"]


def kernel(**inputs):
    import concourse.bacc as bacc
    from concourse.bass_utils import run_bass_kernel_spmd

    nc = bacc.Bacc("TRN2", target_bir_lowering=False, num_devices=1)
    arrays = {f"in_{n}": np.ascontiguousarray(inputs[n]) for n in _INS}
    arrays["in_consts"] = constants()
    args = [nc.dram_tensor(n, a.shape, mybir.dt.from_np(a.dtype), kind="ExternalInput").ap() for n, a in arrays.items()]
    out = nc.dram_tensor("out_x", (1, S, D), F32, kind="ExternalOutput").ap()
    build(nc, *args, out)
    r = run_bass_kernel_spmd(nc, [arrays], core_ids=[0])
    return r.results[0]["out_x"]
```

```python
from contextlib import ExitStack
import math

import numpy as np

import concourse.bass as bass
from concourse import mybir

F32 = mybir.dt.float32
F32R = mybir.dt.float32r
BF16 = mybir.dt.bfloat16
I32 = mybir.dt.int32
ALU = mybir.AluOpType
ACT = mybir.ActivationFunctionType
AX = mybir.AxisListType

P = 128
D = 1024
S = 256
TT = S // P
KT = D // P
DEPTH = 2
SB_HEADS, DF_HEADS, HD = 8, 4, 64
HALF = SB_HEADS * HD
QKV = 6 * HALF
FD = 2816
FE = 3584
NE = 8
EPS = 1e-6
CH = 512
N_BUCKETS, MAX_DISTANCE = 32, 128
MASKED = -1.0e30
PIECE = 2048
RAW = 6
SPL = 3
D_FULL = FD // CH
D_REST = FD - D_FULL * CH
FT = FD // P
E_CH = FE // CH
PROJ = 12
WOUT = 4
DENSE_GU = 4 * D_FULL + 2
DENSE_DN = FD * D // (P * PIECE)
LAYER1 = PROJ + WOUT + DENSE_GU + DENSE_DN
MOE0 = LAYER1 + PROJ + WOUT
PER_BLOCK = 6 * E_CH
MAX_BLOCKS = S * 2 // P + NE - 1
TAB = MAX_BLOCKS + 1
NOT_CHOSEN = 1000.0
PAIRS = SB_HEADS // 2
ZW = 3 * P
STEPS = DF_HEADS * TT
ROOT_SEED = 1597463007.0
SIGN = -2 ** 31
C_ID, C_NTRI, C_NONE, C_TRIS, C_ONE, C_IOTA = (P * i for i in range(6))
C_REV = 6 * P
C_E = C_REV + NE
C_LE = C_E + NE
C_B = C_LE + NE * NE
C_OH = C_B + TAB
C_MASKED = C_OH + 384
C_FLIP = C_MASKED + DF_HEADS
C_END = C_FLIP + P
CONSTS = C_OH


def constants():
    c = np.zeros((P, C_END), np.float32)
    r = np.arange(P)
    c[:, C_ID:C_ID + P] = np.eye(P)
    c[:, C_NTRI:C_NTRI + P] = -(r[:, None] >= r[None, :]).astype(np.float32)
    c[:, C_NONE:C_NONE + P] = -1.0
    c[:, C_TRIS:C_TRIS + P] = r[:, None] < r[None, :]
    c[:, C_ONE:C_ONE + P] = 1.0
    c[:, C_IOTA:C_IOTA + P] = r[None, :]
    e = np.arange(NE)
    c[:, C_REV:C_REV + NE] = NE - e
    c[:, C_E:C_E + NE] = e
    c[:, C_LE:C_LE + NE * NE] = (e[None, :] <= e[:, None]).astype(np.float32).reshape(-1)
    c[:, C_B:C_B + TAB] = np.arange(TAB)
    i = np.arange(384)
    dist = S - 1 - i
    exact = N_BUCKETS // 2
    n = np.maximum(dist, 1).astype(np.float32)
    large = exact + (np.log(n / np.float32(exact)) / np.float32(math.log(MAX_DISTANCE / exact))
                     * np.float32(N_BUCKETS - exact)).astype(np.int32)
    bucket = np.where(dist < exact, dist, np.minimum(large, N_BUCKETS - 1))
    bucket = np.where(dist < 0, N_BUCKETS, bucket)
    c[bucket, C_OH + i] = 1.0
    c[:, C_FLIP:C_FLIP + P] = np.eye(P)[::-1]
    c[N_BUCKETS, C_MASKED:C_MASKED + DF_HEADS] = MASKED
    return c


def lambda_init(layer):
    return 0.8 - 0.6 * math.exp(-0.3 * layer)


def build(nc, x, w_in, w_out, attn_norm, ffn_norm, sb_out_norm, diff_subln, lambda_q1, lambda_k1,
          lambda_q2, lambda_k2, rel_bias, dense_w_gate, dense_w_up, dense_w_down, router_w,
          expert_w_gate, expert_w_up, expert_w_down, final_norm, consts, out):
    with ExitStack() as ctx:
        def sb(name, shape, dt=F32, stack=ctx):
            return stack.enter_context(nc.sbuf_tensor(name, shape, dt))

        def sem(name):
            return ctx.enter_context(nc.semaphore(name))

        raw = sb("raw", [P, RAW, PIECE])
        w_hi = sb("w_hi", [P, SPL, PIECE], F32R)
        w_lo = sb("w_lo", [P, SPL, PIECE], F32R)
        xs = sb("xs", [P, TT, D])
        aT_hi = sb("aT_hi", [P, KT, S], F32R)
        aT_lo = sb("aT_lo", [P, KT, S], F32R)
        hn = sb("hn", [P, TT, D])
        sq = sb("sq", [P, TT * HALF])
        gain = sb("gain", [P, 2, D])
        g_sb = sb("g_sb", [P, DEPTH, HD])
        g_df = sb("g_df", [P, DEPTH, 2 * HD])
        cst = sb("cst", [P, CONSTS])
        ss = sb("ss", [P, 16])
        var = sb("var", [P, 16])
        nw1 = sb("nw1", [P, 16])
        nw2 = sb("nw2", [P, 16])
        rstd = sb("rstd", [P, 16])
        nlam = sb("nlam", [P, DEPTH])
        bias = sb("bias", [P, DF_HEADS, S])
        ps = ctx.enter_context(nc.psum_tensor("ps", [P, 8, 512], F32))

        with ExitStack() as phase:
            def sp_(name, shape, dt=F32):
                return sb(name, shape, dt, phase)
            qk_sb = sp_("qk_sb", [P, 8, S])
            qk_df = sp_("qk_df", [P, 8, S])
            v_sb = sp_("v_sb", [P, TT, HALF])
            v_df = sp_("v_df", [P, TT, HALF])
            ab = sp_("ab", [P, 2, 2, ZW])
            spl = sp_("spl", [P, 2, 2, ZW])
            zb = sp_("zb", [P, 3, 2, S])
            bias_up = zb[:, 0:2].rearrange("p a c k -> p (a c) k")
            wT = sp_("wT", [P, 2, S])
            mx = sp_("mx", [P, 3, 2])
            es = sp_("es", [P, 3, 2])
            rr = sp_("rr", [P, TT, DF_HEADS, 2])
            r0s = sp_("r0s", [P, TT, DF_HEADS])
            scl = sp_("scl", [P, TT, DF_HEADS])
            coef = sp_("coef", [P, 3, 1])
            with ExitStack() as early:
                lam_in = sb("lam_in", [P, 4, DEPTH, HD], F32, early)
                lam_pr = sb("lam_pr", [P, 2, DEPTH, HD], F32, early)
                lam_s = sb("lam_s", [P, 2, DEPTH], F32, early)
                lam_e = sb("lam_e", [P, 2, DEPTH], F32, early)
                lam_d = sb("lam_d", [P, DEPTH], F32, early)
                bkt = sb("bkt", [N_BUCKETS + 1, 384 + DF_HEADS], F32, early)
                vrow = sb("vrow", [DF_HEADS, 384], F32, early)
                flip = sb("flip", [P, P], F32, early)
            att = sp_("att", [P, 2, 2, ZW])
            wd = sp_("wd", [P, 2, S])
        with ExitStack() as phase:
            hT_hi = sb("hT_hi", [P, FT, S], F32R, phase)
            hT_lo = sb("hT_lo", [P, FT, S], F32R, phase)
        with ExitStack() as phase:
            def se(name, shape, dt=F32):
                return sb(name, shape, dt, phase)
            rT = se("rT", [P, KT, S])
            rw = se("rw", [P, KT, NE])
            lg = se("lg", [P, TT, NE])
            lg2 = se("lg2", [P, TT, NE])
            m1 = se("m1", [P, TT])
            m2 = se("m2", [P, TT])
            eq1, rk1, oh1 = se("eq1", [P, TT, NE]), se("rk1", [P, TT, NE]), se("oh1", [P, TT, NE])
            eq2, rk2, oh2 = se("eq2", [P, TT, NE]), se("rk2", [P, TT, NE]), se("oh2", [P, TT, NE])
            r1, r2 = se("r1", [P, TT]), se("r2", [P, TT])
            dm, ed, dn = se("dm", [P, TT]), se("ed", [P, TT]), se("dn", [P, TT])
            g1, g2 = se("g1", [P, TT]), se("g2", [P, TT])
            chosen = se("chosen", [P, TT, NE])
            gg1, gg = se("gg1", [P, TT, NE]), se("gg", [P, TT, NE])
            pm1, posm0, posm = se("pm1", [P, TT, NE]), se("posm0", [P, TT, NE]), se("posm", [P, TT, NE])
            cnt = se("cnt", [P, NE])
            nb1, nb2, nbe = se("nb1", [P, NE]), se("nb2", [P, NE]), se("nbe", [P, NE])
            le8 = se("le8", [P, NE, NE])
            ends = se("ends", [P, NE])
            cmpb = se("cmpb", [P, TAB, NE])
            eb = se("eb", [P, TAB])
            stb = se("stb", [P, TAB, NE])
            start = se("start", [P, TAB])
            local = se("local", [P, TAB])
            cm = se("cm", [P, TAB, NE])
            tmpb = se("tmpb", [P, 2, TT, TAB, NE])
            sel0 = se("sel0", [P, TT, TAB])
            sel = se("sel", [P, TT, TAB])
            gate = se("gate", [P, TT, TAB])
            ebi = se("ebi", [P, TAB], I32)
            nbi = se("nbi", [P, 1], I32)
            xe_hi = se("xe_hi", [P, KT, P], F32R)
            xe_lo = se("xe_lo", [P, KT, P], F32R)
            rows3 = se("rows3", [P, 3, TT, D], BF16)
            onehot = se("onehot", [P, TT, P], BF16)
            hot32 = se("hot32", [P, TT, P])
            onehotT = se("onehotT", [P, TT, P], F32R)
            he_hi = se("he_hi", [P, 4, P], F32R)
            he_lo = se("he_lo", [P, 4, P], F32R)
            ye_hi = se("ye_hi", [P, D], F32R)
            ye_lo = se("ye_lo", [P, D], F32R)
            sil = se("sil", [P, 2, CH])
            hid = se("hid", [P, 2, CH])

        scratch = nc.dram_tensor("bias_scratch", (DF_HEADS, 384), F32, kind="Internal").ap()
        ident = cst[:, C_ID:C_ID + P]
        neg_tri = cst[:, C_NTRI:C_NTRI + P]
        neg_one = cst[:, C_NONE:C_NONE + P]
        tri_strict = cst[:, C_TRIS:C_TRIS + P]
        ones = cst[:, C_ONE:C_ONE + P]
        iota = cst[:, C_IOTA:C_IOTA + P]

        raw_in = [sem(f"raw_in{i}") for i in range(RAW)]
        hi_ready, lo_ready, piece_used = sem("hi_ready"), sem("lo_ready"), sem("piece_used")
        x_in = [sem("x_in0"), sem("x_in1")]
        cst_in, small_in, lam_ld, bkt_in = (sem(n) for n in ("cst_in", "small_in", "lam_ld", "bkt_in"))
        rw_in = sem("rw_in")
        gain_first, gain_in = sem("gain_first"), [sem("gain_in0"), sem("gain_in1")]
        x_done, ss_done = sem("x_done"), sem("ss_done")
        rows_done = [sem("rows_done0"), sem("rows_done1")]
        t_done, t_hi, t_lo = sem("t_done"), sem("t_hi"), sem("t_lo")
        proj_saved, proj_saved2 = sem("proj_saved"), sem("proj_saved2")
        z_done, absz_done, ln_done, sp_done, spm_done, tri_done, a_done, am_done, pv_done = (
            sem(n) for n in ("z_done", "absz_done", "ln_done", "sp_done", "spm_done", "tri_done", "a_done", "am_done", "pv_done"))
        z0_done, zd0_done, v_df_saved = sem("z0_done"), sem("zd0_done"), sem("v_df_saved")
        sbo_saved = sem("sbo_saved")
        zd_done, mx_done, e_done, w_done, wt_done, wt_saved, pvd_done = (
            sem(n) for n in ("zd_done", "mx_done", "e_done", "w_done", "wt_done", "wt_saved", "pvd_done"))
        lam_sum, lam_exp, nlam_done = sem("lam_sum"), sem("lam_exp"), sem("nlam_done")
        vrow_mm, vrow_done, scratch_done, bias_in = sem("vrow_mm"), sem("vrow_done"), sem("scratch_done"), sem("bias_in")
        bias_mm, bias_done = sem("bias_mm"), sem("bias_done")
        silu_done, hid_done, hT_hi_done, hT_lo_done = (
            sem(n) for n in ("silu_done", "hid_done", "hT_hi_done", "hT_lo_done"))
        rT_done, lg_done, gap_done, ge_done, chosen_done, pos_done, tab_done = (
            sem(n) for n in ("rT_done", "lg_done", "gap_done", "ge_done", "chosen_done", "pos_done", "tab_done"))
        part_done, rest_done = sem("part_done"), sem("rest_done")
        ga_done, ga_hi, ga_lo = sem("ga_done"), sem("ga_hi"), sem("ga_lo")
        esilu_done, ehid_done, et_done, eh_hi, eh_lo = (
            sem(n) for n in ("esilu_done", "ehid_done", "et_done", "eh_hi", "eh_lo"))
        y_hi, y_lo = sem("y_hi"), sem("y_lo")
        sc_done, sc_added = [sem("sc_done0"), sem("sc_done1")], [sem("sc_added0"), sem("sc_added1")]
        hot_t, hot_saved, hot_ready = (sem(n) for n in ("hot_t", "hot_saved", "hot_ready"))
        out_rows, out_sent = sem("out_rows"), sem("out_sent")
        dve_chain, act_chain = sem("dve_chain"), sem("act_chain")

        win_v = [w_in[l].rearrange("(k p) n -> p k n", p=P) for l in range(DEPTH)]
        wout_v = [w_out[l].rearrange("(k p) n -> p k n", p=P) for l in range(DEPTH)]
        gate_v = dense_w_gate[0].rearrange("(k p) n -> p k n", p=P)
        up_v = dense_w_up[0].rearrange("(k p) n -> p k n", p=P)
        down_v = dense_w_down[0].rearrange("(f p) n -> p f n", p=P)
        egate_v = expert_w_gate[0].rearrange("e (k p) n -> e p k n", p=P)
        eup_v = expert_w_up[0].rearrange("e (k p) n -> e p k n", p=P)
        edown_v = expert_w_down[0].rearrange("e (f p) n -> e p f n", p=P)

        def halves(view, col):
            return [view[:, 4 * h:4 * h + 4, col:col + CH] for h in range(2)]

        sources = []
        for l in range(DEPTH):
            for u in range(PROJ // 2):
                sources += halves(win_v[l], u * CH)
            for u in range(WOUT // 2):
                sources += halves(wout_v[l], u * CH)
            if l == 0:
                for n in range(D_FULL):
                    sources += halves(gate_v, n * CH) + halves(up_v, n * CH)
                sources += [gate_v[:, :, D_FULL * CH:FD], up_v[:, :, D_FULL * CH:FD]]
                sources += [down_v[:, 2 * i:2 * i + 2, :] for i in range(DENSE_DN)]
        assert len(sources) == MOE0

        def expert_pieces():
            order = []
            for c in range(E_CH + 1):
                if c < E_CH:
                    order += [("gate", c, 0), ("gate", c, 1), ("up", c, 0), ("up", c, 1)]
                if c > 0:
                    order += [("down", c - 1, 0), ("down", c - 1, 1)]
            return order

        ORDER = expert_pieces()
        assert len(ORDER) == PER_BLOCK and PER_BLOCK % RAW == 0 and PER_BLOCK % SPL == 0
        AT = {k: i for i, k in enumerate(ORDER)}
        ROUNDS = PER_BLOCK // RAW

        def landed(n, b=None):
            return 16 * (n // RAW + 1) if b is None else b * (16 * ROUNDS) + 16 * (n // RAW + 1)

        def nth(n, b=None):
            return n if b is None else b * PER_BLOCK + n

        def split_hi(act, n, b=None):
            act.wait_ge(raw_in[n % RAW], landed(n, b))
            if n >= SPL:
                act.wait_ge(piece_used, nth(n - SPL + 1, b))
            nc.scalar.activation(w_hi[:, n % SPL, :], raw[:, n % RAW, :], ACT.Copy).then_inc(hi_ready, 1)

        def split_lo(dve, n, b=None):
            dve.wait_ge(hi_ready, nth(n + 1, b))
            nc.vector.tensor_tensor(w_lo[:, n % SPL, :], raw[:, n % RAW, :],
                                    w_hi[:, n % SPL, :].bitcast(F32), ALU.subtract).then_inc(lo_ready, 1)

        block = ctx.enter_context(nc.Block())

        @block.sync
        def _(sp):
            for t in range(TT):
                sp.dma_start(xs[:, t, :], x[0, t * P:t * P + P, :]).then_inc(x_in[t], 16)

            def load(n, src, b=None):
                if n >= RAW:
                    sp.wait_ge(lo_ready, nth(n - RAW + 1, b))
                dst = raw[:, n % RAW, :].rearrange("p (k n) -> p k n", n=src.shape[-1])
                sp.dma_start(dst, src).then_inc(raw_in[n % RAW], 16)

            for n, src in enumerate(sources):
                load(n, src)

            def load_block(b, e):
                for i, (kind, c, h) in enumerate(ORDER):
                    if kind == "down":
                        src = edown_v[e, :, 4 * c + 2 * h:4 * c + 2 * h + 2, :]
                    else:
                        src = (egate_v if kind == "gate" else eup_v)[e, :, 4 * h:4 * h + 4, c * CH:c * CH + CH]
                    load(MOE0 + i, src.rearrange("e p k n -> (e p) k n"), b)

            load_block(0, slice(0, 1))
            sp.wait_ge(tab_done, 1)
            blocks = sp.value_load(nbi[0:1, 0:1], min_val=4, max_val=MAX_BLOCKS)
            with sp.Fori(1, blocks) as b:
                load_block(b, bass.ds(sp.value_load(ebi[0:1, bass.ds(b, 1)], min_val=0, max_val=NE - 1), 1))
            for t in range(TT):
                sp.wait_ge(out_rows, t + 1)
                sp.dma_start(out[0, t * P:t * P + P, :], hn[:, t, :]).then_inc(out_sent, 16)
            sp.wait_ge(out_sent, 16 * TT)

        @block.gpsimd
        def _(pool):
            norms = [attn_norm[0], ffn_norm[0], attn_norm[1], ffn_norm[1], final_norm]

            def load_gain(m):
                pool.dma_start(gain[:, m % 2, :], norms[m].partition_broadcast(P)).then_inc(gain_in[m % 2], 16)

            pool.dma_start(bkt[:, 0:384], consts[0:N_BUCKETS + 1, C_OH:C_OH + 384]).then_inc(bkt_in, 16)
            pool.dma_start(bkt[0:N_BUCKETS, 384:384 + DF_HEADS], rel_bias[:, :]).then_inc(bkt_in, 16)
            pool.dma_start(bkt[N_BUCKETS:N_BUCKETS + 1, 384:384 + DF_HEADS],
                           consts[N_BUCKETS:N_BUCKETS + 1, C_MASKED:C_FLIP]).then_inc(bkt_in, 16)
            pool.dma_start(flip[:], consts[:, C_FLIP:C_END]).then_inc(bkt_in, 16)
            for i, v in enumerate((lambda_q1, lambda_q2, lambda_k1, lambda_k2)):
                pool.dma_start(lam_in[:, i], v.rearrange("l d -> (l d)").partition_broadcast(P)).then_inc(lam_ld, 16)
            pool.dma_start(g_sb[:].rearrange("p l d -> p (l d)"),
                           sb_out_norm.rearrange("l d -> (l d)").partition_broadcast(P)).then_inc(small_in, 16)
            pool.dma_start(g_df[:].rearrange("p l d -> p (l d)"),
                           diff_subln.rearrange("l d -> (l d)").partition_broadcast(P)).then_inc(small_in, 16)
            load_gain(1)
            pool.wait_ge(vrow_done, 1)
            pool.dma_start(scratch, vrow[:]).then_inc(scratch_done, 16)
            pool.wait_ge(scratch_done, 16)
            pool.dma_start(bias_up, bass.AP(scratch.tensor, 0, [[1, P], [384, DF_HEADS], [1, S]])).then_inc(bias_in, 16)

            def causal(tile, parity):
                for h in range(2):
                    v = tile[:, parity, h].rearrange("p (a q) -> p a q", q=P)[:, 0:3:2, :]
                    last = nc.gpsimd.affine_select(out=v, in_=v, compare_op=ALU.is_gt, fill=0.0, base=0,
                                                   pattern=[[0, 2], [1, P]], channel_multiplier=-1)
                return last

            for l in range(DEPTH):
                for g in range(PAIRS):
                    i = PAIRS * l + g
                    pool.wait_ge(sp_done, i + 1)
                    causal(spl, g % 2).then_inc(spm_done, 1)
                    pool.wait_ge(a_done, i + 1)
                    causal(att, g % 2).then_inc(am_done, 1)
                    if g == 0:
                        pool.wait_ge(rows_done[1], 3 * l + 1)
                        load_gain(2 * l + 2)
                if l == 0:
                    pool.wait_ge(rows_done[1], 3)
                    load_gain(3)
            pool.wait_ge(piece_used, MOE0)
            pool.dma_start(rw[:], router_w[0].rearrange("(k p) e -> p k e", p=P)).then_inc(rw_in, 16)

        @block.tensor
        def _(pe):
            def mm3(o, s_hi, s_lo, m_hi, m_lo, start, stop):
                pe.matmul(o, s_hi, m_hi, start=start, stop=False, skip_group_check=True)
                pe.matmul(o, s_hi, m_lo, start=False, stop=False, skip_group_check=True)
                return pe.matmul(o, s_lo, m_hi, start=False, stop=stop, skip_group_check=True)

            def piece(n, b=None):
                pe.wait_ge(lo_ready, nth(n + 1, b))
                return w_hi[:, n % SPL, :], w_lo[:, n % SPL, :]

            def columns_out(n, bank, half, k_tiles=4, width=CH):
                hi, lo = piece(n)
                for ct in range(width // P):
                    o = ps[:, bank + ct // 2, (ct % 2) * S:(ct % 2) * S + S]
                    for k in range(k_tiles):
                        kk = k_tiles * half + k
                        c0 = k * width + ct * P
                        last = mm3(o, hi[:, c0:c0 + P], lo[:, c0:c0 + P], aT_hi[:, kk, :], aT_lo[:, kk, :],
                                   start=(kk == 0 and ct % 2 == 0), stop=(kk == KT - 1))
                last.then_inc(piece_used, 1)

            def rows_out(n, bank, half):
                hi, lo = piece(n)
                for t in range(TT):
                    for k in range(4):
                        kk = 4 * half + k
                        last = mm3(ps[:, bank + t, :], aT_hi[:, kk, t * P:t * P + P], aT_lo[:, kk, t * P:t * P + P],
                                   hi[:, k * CH:k * CH + CH], lo[:, k * CH:k * CH + CH],
                                   start=(kk == 0), stop=(kk == KT - 1))
                last.then_inc(piece_used, 1)

            def turn_rows(r):
                for t in range(TT):
                    pe.wait_ge(rows_done[t], r + 1)
                    for j in range(4):
                        for q in range(2):
                            last = pe.transpose(ps[:, 4 + j, (2 * q + t) * P:(2 * q + t) * P + P],
                                                hn[:, t, (2 * j + q) * P:(2 * j + q) * P + P], ident)
                        if t == TT - 1:
                            last.then_inc(t_done, 1)

            pe.wait_ge(cst_in, 16)
            for l in range(DEPTH):
                n0 = LAYER1 * l
                turn_rows(3 * l)

                def project(u, bank):
                    for half in range(2):
                        if u == 0:
                            pe.wait_ge(t_lo, 12 * l + 2 + 2 * half)
                        (rows_out if u in (2, 5) else columns_out)(n0 + 2 * u + half, bank, half)

                def z_pair(g):
                    for m in range(2):
                        q = qk_sb[HD * m:HD * m + HD, g, :]
                        k = qk_sb[HD * m:HD * m + HD, 4 + g, :]
                        bank = ps[:, (4, 2)[g % 2] + m, :]
                        pe.matmul(bank[:, 0:S], k[:, 0:P], q, start=True, stop=False, skip_group_check=True)
                        last = pe.matmul(bank[:, S:ZW], k[:, P:S], q[:, P:S], start=False, stop=False, skip_group_check=True)
                        if m == 0:
                            last.then_inc(z0_done, 1)
                    last.then_inc(z_done, 1)

                def add_stays(g):
                    pe.wait_ge(spm_done, PAIRS * l + g + 1)
                    for m in range(2):
                        bank = ps[:, (4, 2)[g % 2] + m, :]
                        pe.matmul(bank[:, 0:ZW], neg_tri, spl[:, g % 2, m, :], start=False, stop=False, skip_group_check=True)
                        last = pe.matmul(bank[:, P:S], neg_one, spl[:, g % 2, m, S:ZW], start=False, stop=True,
                                         skip_group_check=True)
                    last.then_inc(tri_done, 1)

                def values(g):
                    pe.wait_ge(am_done, PAIRS * l + g + 1)
                    for m in range(2):
                        a = att[:, g % 2, m, :]
                        c = slice(HD * (2 * g + m), HD * (2 * g + m) + HD)
                        pe.matmul(ps[:, 6, c], a[:, 0:P], v_sb[:, 0, c], start=True, stop=True, skip_group_check=True)
                        pe.matmul(ps[:, 7, c], a[:, P:S], v_sb[:, 0, c], start=True, stop=False, skip_group_check=True)
                        last = pe.matmul(ps[:, 7, c], a[:, S:ZW], v_sb[:, 1, c], start=False, stop=True, skip_group_check=True)
                    last.then_inc(pv_done, 1)

                project(0, 0)
                if l == 0:
                    pe.wait_ge(bkt_in, 64)
                    pe.matmul(ps[0:DF_HEADS, 7, 0:384], bkt[:, 384:384 + DF_HEADS], bkt[:, 0:384],
                              start=True, stop=True).then_inc(vrow_mm, 1)
                project(1, 2)
                pe.wait_ge(proj_saved, 4 * l + 1)
                pe.wait_ge(proj_saved2, l + 1)
                z_pair(0)
                project(2, 0)
                if l == 0:
                    pe.wait_ge(bias_in, 16)
                    pe.wait_ge(vrow_done, 1)
                    for h in range(DF_HEADS):
                        last = pe.matmul(ps[:, 6 + h // 2, (h % 2) * S:(h % 2) * S + S], flip[:], bias_up[:, h, :],
                                         start=(h % 2 == 0), stop=(h % 2 == 1), skip_group_check=True)
                    last.then_inc(bias_mm, 1)
                add_stays(0)
                z_pair(1)
                pe.wait_ge(proj_saved, 4 * l + 2)
                project(3, 0)
                if l == 0:
                    pe.wait_ge(bias_done, 1)
                values(0)
                add_stays(1)
                z_pair(2)
                pe.wait_ge(proj_saved, 4 * l + 3)
                project(4, 0)
                values(1)
                add_stays(2)
                z_pair(3)
                pe.wait_ge(proj_saved, 4 * l + 4)
                project(5, 0)

                def scores(s):
                    h, t = s // 2, s % 2
                    if s >= 2:
                        pe.wait_ge(mx_done, STEPS * l + s - 1)
                    if s == 1:
                        pe.wait_ge(v_df_saved, l + 1)
                    for c in range(2):
                        q = qk_df[HD * c:HD * c + HD, h, t * P:t * P + P]
                        k = qk_df[HD * c:HD * c + HD, 4 + h, 0:P * (t + 1)]
                        last = pe.matmul(ps[:, 4 - 4 * (s % 2) + c, 0:P * (t + 1)], q, k, start=True, stop=True)
                        if c == 0:
                            last.then_inc(zd0_done, 1)
                    last.then_inc(zd_done, 1)

                def turn_weights(j):
                    pe.wait_ge(w_done, STEPS * l + j + 1)
                    if j >= 2:
                        pe.wait_ge(wt_saved, STEPS * l + j - 1)
                    for kb in range(j % 2 + 1):
                        last = pe.transpose(ps[:, 2 + j % 2, kb * P:kb * P + P], wd[:, j % 2, kb * P:kb * P + P], ident)
                    last.then_inc(wt_done, 1)

                def df_values(j):
                    h, t = j // 2, j % 2
                    pe.wait_ge(wt_saved, STEPS * l + j + 1)
                    if j == 0:
                        pe.wait_ge(sbo_saved, l + 1)
                    c = slice(2 * HD * h, 2 * HD * h + 2 * HD)
                    for kb in range(t + 1):
                        last = pe.matmul(ps[:, 6 + t, c], wT[:, j % 2, kb * P:kb * P + P], v_df[:, kb, c],
                                         start=(kb == 0), stop=(kb == t), skip_group_check=True)
                    if j == STEPS - 1:
                        last.then_inc(pvd_done, 1)

                values(2)
                scores(0)
                add_stays(3)
                scores(1)
                values(3)
                for i in range(2, STEPS + 3):
                    if i < STEPS:
                        scores(i)
                    if i - 2 < STEPS:
                        turn_weights(i - 2)
                    if i >= 3:
                        df_values(i - 3)

                turn_rows(3 * l + 1)
                for u in range(2):
                    for half in range(2):
                        if u == 0:
                            pe.wait_ge(t_lo, 12 * l + 6 + 2 * half)
                        rows_out(n0 + PROJ + 2 * u + half, 2 * u, half)
                turn_rows(3 * l + 2)
                if l == 0:
                    for n in range(D_FULL + 1):
                        if n >= 2:
                            pe.wait_ge(hT_lo_done, n - 1)
                        g = PROJ + WOUT + 4 * n
                        bank = 4 * (n % 2)
                        if n < D_FULL:
                            for half in range(2):
                                if n == 0:
                                    pe.wait_ge(t_lo, 10 + 2 * half)
                                columns_out(g + half, bank, half)
                            for half in range(2):
                                columns_out(g + 2 + half, bank + 2, half)
                        else:
                            columns_out(g, bank, 0, KT, D_REST)
                            columns_out(g + 1, bank + 2, 0, KT, D_REST)
                    for i in range(DENSE_DN):
                        hi, lo = piece(PROJ + WOUT + DENSE_GU + i)
                        if i % 2 == 0:
                            pe.wait_ge(hT_lo_done, i // 2 + 1)
                        for t in range(TT):
                            for f in range(2):
                                ff = 2 * i + f
                                for c in range(2):
                                    at = f * D + c * CH
                                    last = mm3(ps[:, 2 * t + c, :], hT_hi[:, ff, t * P:t * P + P], hT_lo[:, ff, t * P:t * P + P],
                                               hi[:, at:at + CH], lo[:, at:at + CH], start=(ff == 0), stop=(ff == FT - 1))
                        last.then_inc(piece_used, 1)

            pe.wait_ge(rT_done, 4)
            pe.wait_ge(rw_in, 16)
            for t in range(TT):
                for k in range(KT):
                    last = pe.matmul(ps[:, 0, t * NE:t * NE + NE], rT[:, k, t * P:t * P + P], rw[:, k, :],
                                     start=(k == 0), stop=(k == KT - 1), skip_group_check=True)
            last.then_inc(lg_done, 1)
            pe.wait_ge(chosen_done, 1)
            pe.matmul(ps[:, 1, 0:NE], tri_strict, chosen[:, 0, :], start=True, stop=True, skip_group_check=True)
            pe.matmul(ps[:, 1, NE:2 * NE], tri_strict, chosen[:, 1, :], start=True, stop=False, skip_group_check=True)
            pe.matmul(ps[:, 1, NE:2 * NE], ones, chosen[:, 0, :], start=False, stop=True, skip_group_check=True)
            pe.matmul(ps[:, 1, 2 * NE:3 * NE], ones, chosen[:, 0, :], start=True, stop=False, skip_group_check=True)
            pe.matmul(ps[:, 1, 2 * NE:3 * NE], ones, chosen[:, 1, :], start=False, stop=True,
                      skip_group_check=True).then_inc(pos_done, 1)

            def gather(count):
                pe.wait_ge(hot_ready, count)
                for j in range(2):
                    for q in range(4):
                        k = 4 * j + q
                        for t in range(TT):
                            for part in range(3):
                                last = pe.matmul(ps[:, 1 + 2 * j, q * P:q * P + P], rows3[:, part, t, k * P:k * P + P],
                                                 onehot[:, t, :], start=(t == 0 and part == 0), stop=(t == 1 and part == 2),
                                                 skip_group_check=True)
                last.then_inc(ga_done, 1)

            def scatter(t, bank=6):
                for c in range(2):
                    for part in (ye_hi, ye_lo):
                        last = pe.matmul(ps[:, bank + c, :], onehotT[:, t, :], part[:, c * CH:c * CH + CH],
                                         start=(part is ye_hi), stop=(part is ye_lo), skip_group_check=True)
                last.then_inc(sc_done[t], 1)

            def expert_block(b, first):
                pe.wait_ge(ga_lo, b + 1)

                def expert_in(kind, c, half):
                    n = MOE0 + AT[(kind, c, half)]
                    hi, lo = piece(n, b)
                    bank = (0 if kind == "gate" else 2) + c % 2
                    for k in range(4):
                        kk = 4 * half + k
                        last = mm3(ps[:, bank, :], xe_hi[:, kk, :], xe_lo[:, kk, :], hi[:, k * CH:k * CH + CH],
                                   lo[:, k * CH:k * CH + CH], start=(kk == 0), stop=(kk == KT - 1))
                    last.then_inc(piece_used, 1)

                def turn_hidden(c):
                    pe.wait_ge(ehid_done, b * E_CH + c + 1)
                    for f in range(4):
                        last = pe.transpose(ps[:, 7, f * P:f * P + P], hid[:, c % 2, f * P:f * P + P], ident)
                    last.then_inc(et_done, 1)

                def expert_down(c, half):
                    hi, lo = piece(MOE0 + AT[("down", c, half)], b)
                    if half == 0:
                        pe.wait_ge(eh_lo, b * E_CH + c + 1)
                    for f in range(2):
                        ff = 2 * half + f
                        for o in range(2):
                            at = f * D + o * CH
                            last = mm3(ps[:, 4 + o, :], he_hi[:, ff, :], he_lo[:, ff, :], hi[:, at:at + CH], lo[:, at:at + CH],
                                       start=(c == 0 and ff == 0), stop=(c == E_CH - 1 and ff == 3))
                    last.then_inc(piece_used, 1)

                for c in range(E_CH + 1):
                    if c < E_CH:
                        expert_in("gate", c, 0)
                        expert_in("gate", c, 1)
                    if c == 0 and not first:
                        pe.wait_ge(y_lo, b)
                        pe.wait_ge(hot_saved, b)
                        scatter(0)
                    if c == 1 and not first:
                        pe.wait_ge(sc_added[1], b)
                    if c > 0:
                        turn_hidden(c - 1)
                    if c == 2:
                        for t in range(TT):
                            last = pe.transpose(ps[:, 6, t * P:t * P + P], hot32[:, t, :], ident)
                        last.then_inc(hot_t, 1)
                    if c < E_CH:
                        expert_in("up", c, 0)
                        expert_in("up", c, 1)
                    else:
                        gather(b + 2)
                    if c == 0 and not first:
                        pe.wait_ge(sc_added[0], b)
                        scatter(1)
                    if c > 0:
                        expert_down(c - 1, 0)
                        expert_down(c - 1, 1)

            pe.wait_ge(rest_done, 2)
            gather(1)
            expert_block(0, True)
            pe.wait_ge(tab_done, 1)
            blocks = pe.value_load(nbi[0:1, 0:1], min_val=4, max_val=MAX_BLOCKS)
            with pe.Fori(1, blocks) as b:
                expert_block(b, False)
            pe.wait_ge(y_lo, blocks)
            pe.wait_ge(hot_saved, blocks)
            scatter(0)
            scatter(1, 0)

        @block.scalar
        def _(act):
            act.dma_start(gain[:, 0, :], attn_norm[0].partition_broadcast(P)).then_inc(gain_first, 16)
            act.dma_start(cst[:], consts[:, 0:CONSTS]).then_inc(cst_in, 16)
            steps = [0]

            def link(ins):
                steps[0] += 1
                ins.then_inc(act_chain, 1)
                act.wait_ge(act_chain, steps[0])

            def copy(dst, src, scale=1.0):
                return nc.scalar.activation(dst, src, ACT.Copy, scale=scale)

            def both(banks):
                return banks.rearrange("p a s -> p (a s)")

            def squares(m):
                if m == 0:
                    act.wait_ge(x_in[0], 16)
                else:
                    act.wait_ge(x_done, m)
                nc.scalar.activation(sq[:, :], xs[:, 0, :], ACT.Square, accum_out=ss[:, 0:1]).then_inc(ss_done, 1)

            def turned(r):
                for j in range(4):
                    act.wait_ge(t_done, 4 * r + j + 1)
                    dst, done = (rT, rT_done) if r == 5 else (aT_hi, t_hi)
                    copy(both(dst[:, 2 * j:2 * j + 2, :]), ps[:, 4 + j, :]).then_inc(done, 1)

            nc.scalar.preload_act_table_set("natural_log_exp_and_others")
            for l in range(DEPTH):
                n0 = LAYER1 * l
                if l == 1:
                    squares(2)
                for n in range(n0, n0 + 3):
                    split_hi(act, n)
                if l == 0:
                    squares(0)
                turned(3 * l)

                def stay_logs(g):
                    act.wait_ge(absz_done, PAIRS * l + g + 1)
                    a = ab[:, g % 2].rearrange("p h q -> p (h q)")
                    link(nc.scalar.activation(a, a, ACT.Exp))
                    nc.scalar.activation(a, a, ACT.Ln, bias=1.0).then_inc(ln_done, 1)

                def weights(g):
                    act.wait_ge(tri_done, PAIRS * l + g + 1)
                    bank = (4, 2)[g % 2]
                    nc.scalar.activation(att[:, g % 2], ps[:, bank:bank + 2, 0:ZW], ACT.Exp).then_inc(a_done, 1)

                split_hi(act, n0 + 3)
                split_hi(act, n0 + 4)
                copy(both(qk_sb[:, 0:4, :]), both(ps[:, 0:2, :]), HD ** -0.5).then_inc(proj_saved, 1)
                split_hi(act, n0 + 5)
                if l == 0:
                    act.wait_ge(lam_sum, 1)
                    nc.scalar.activation(lam_e[:], lam_s[:], ACT.Exp).then_inc(lam_exp, 1)
                split_hi(act, n0 + 6)
                stay_logs(0)
                split_hi(act, n0 + 7)
                act.wait_ge(piece_used, n0 + 6)
                copy(both(v_sb[:]), both(ps[:, 0:2, :])).then_inc(proj_saved, 1)
                weights(0)
                split_hi(act, n0 + 8)
                stay_logs(1)
                split_hi(act, n0 + 9)
                split_hi(act, n0 + 10)
                copy(both(qk_df[:, 0:4, :]), both(ps[:, 0:2, :]), HD ** -0.5).then_inc(proj_saved, 1)
                weights(1)
                stay_logs(2)
                split_hi(act, n0 + 11)
                split_hi(act, n0 + 12)
                copy(both(qk_df[:, 4:8, :]), both(ps[:, 0:2, :])).then_inc(proj_saved, 1)
                weights(2)
                stay_logs(3)
                split_hi(act, n0 + 13)
                split_hi(act, n0 + 14)

                def exponentials(s):
                    act.wait_ge(mx_done, STEPS * l + s + 1)
                    for c in range(2):
                        z = zb[:, s % 3, c, 0:P * (s % 2 + 1)]
                        last = nc.scalar.activation(z, z, ACT.Exp, bias=mx[:, s % 3, c:c + 1], accum_out=es[:, s % 3, c:c + 1])
                    last.then_inc(e_done, 1)

                exponentials(0)
                weights(3)
                exponentials(1)
                act.wait_ge(pv_done, PAIRS * (l + 1))
                nc.scalar.activation(sq[:, :], both(ps[:, 6:8, :]), ACT.Square).then_inc(ss_done, 1)
                for i in range(2, STEPS + 2):
                    if i < STEPS:
                        exponentials(i)
                    j = i - 2
                    act.wait_ge(wt_done, STEPS * l + j + 1)
                    copy(wT[:, j % 2, 0:P * (j % 2 + 1)], ps[:, 2 + j % 2, 0:P * (j % 2 + 1)]).then_inc(wt_saved, 1)
                act.wait_ge(pvd_done, l + 1)
                nc.scalar.activation(sq[:, :], both(ps[:, 6:8, :]), ACT.Square).then_inc(ss_done, 1)
                turned(3 * l + 1)
                split_hi(act, n0 + 15)
                if l == 0:
                    split_hi(act, 16)
                    split_hi(act, 17)
                squares(2 * l + 1)
                if l == 0:
                    split_hi(act, 18)
                else:
                    for n in range(3):
                        split_hi(act, MOE0 + n)
                turned(3 * l + 2)
                if l == 0:
                    for n in range(D_FULL + 1):
                        last_chunk = n == D_FULL
                        g = PROJ + WOUT + 4 * n
                        for i in range(g + 3, min(g + 7, PROJ + WOUT + DENSE_GU)):
                            split_hi(act, i)
                        if last_chunk:
                            for i in range(PROJ + WOUT + DENSE_GU, PROJ + WOUT + DENSE_GU + 2):
                                split_hi(act, i)
                        bank = 4 * (n % 2)
                        width = D_REST * TT if last_chunk else 2 * CH
                        act.wait_ge(piece_used, min(g + 4, PROJ + WOUT + DENSE_GU))
                        h = hn[:, n % 2, 0:width]
                        nc.scalar.activation(h, both(ps[:, bank:bank + 2, :])[:, 0:width], ACT.Silu).then_inc(silu_done, 1)
                        if last_chunk:
                            split_hi(act, PROJ + WOUT + DENSE_GU + 2)
                        act.wait_ge(hid_done, n + 1)
                        copy(both(hT_hi[:, 4 * n:4 * n + width // S, :]), h).then_inc(hT_hi_done, 1)
                    for i in range(PROJ + WOUT + DENSE_GU + 3, LAYER1):
                        split_hi(act, i)
                    nc.scalar.preload_act_table_set("natural_log_exp_and_others")

            act.wait_ge(lg_done, 1)
            copy(rows3[:, 0], hn[:]).then_inc(part_done, 1)
            act.wait_ge(gap_done, 1)
            nc.scalar.activation(ed[:], dm[:], ACT.Exp).then_inc(ge_done, 1)
            act.wait_ge(rest_done, 1)
            copy(rows3[:, 1], hn[:]).then_inc(part_done, 1)
            nc.scalar.preload_act_table(ACT.Silu)

            def gathered(count):
                act.wait_ge(ga_done, count)
                for j in range(2):
                    copy(both(xe_hi[:, 4 * j:4 * j + 4, :]), ps[:, 1 + 2 * j, :]).then_inc(ga_hi, 1)

            def output_hi(b):
                act.wait_ge(piece_used, nth(MOE0, b))
                copy(ye_hi[:], both(ps[:, 4:6, :])).then_inc(y_hi, 1)

            def expert_block(b, first):
                def hi_of(kind, c, half):
                    if not (first and AT[(kind, c, half)] < SPL):
                        split_hi(act, MOE0 + AT[(kind, c, half)], b)

                def silu(c):
                    act.wait_ge(piece_used, nth(MOE0 + AT[("up", c, 1)] + 1, b))
                    nc.scalar.activation(sil[:, c % 2, :], ps[:, c % 2, :], ACT.Silu).then_inc(esilu_done, 1)

                for c in range(E_CH + 1):
                    if c < E_CH:
                        hi_of("gate", c, 0)
                    if c > 0:
                        silu(c - 1)
                    elif not first:
                        output_hi(b)
                    if c < E_CH:
                        hi_of("gate", c, 1)
                        hi_of("up", c, 0)
                        hi_of("up", c, 1)
                    else:
                        hi_of("down", c - 1, 0)
                        hi_of("down", c - 1, 1)
                    if c > 0:
                        act.wait_ge(et_done, b * E_CH + c)
                        copy(both(he_hi[:]), ps[:, 7, :]).then_inc(eh_hi, 1)
                        if c < E_CH:
                            hi_of("down", c - 1, 0)
                            hi_of("down", c - 1, 1)
                gathered(b + 2)

            gathered(1)
            expert_block(0, True)
            act.wait_ge(tab_done, 1)
            blocks = act.value_load(nbi[0:1, 0:1], min_val=4, max_val=MAX_BLOCKS)
            with act.Fori(1, blocks) as b:
                expert_block(b, False)
            output_hi(blocks)
            squares(4)

        @block.vector
        def _(dve):
            steps = [0]

            def link(ins):
                steps[0] += 1
                ins.then_inc(dve_chain, 1)
                dve.wait_ge(dve_chain, steps[0])

            V = nc.vector

            def both(banks):
                return banks.rearrange("p a s -> p (a s)")

            def inverse_root(width, size):
                v, y, a = var[:, 0:width], rstd[:, 0:width], nw1[:, 0:width]
                link(V.tensor_scalar(v, ss[:, 0:width], 1.0 / size, EPS, ALU.mult, ALU.add))
                link(V.tensor_scalar(a.bitcast(I32), v.bitcast(I32), 1, None, ALU.logical_shift_right))
                link(V.tensor_scalar(y.bitcast(I32), a.bitcast(I32), -1.0, ROOT_SEED, ALU.mult, ALU.add))
                for _ in range(3):
                    link(V.scalar_tensor_tensor(out=a, in0=y, scalar=-0.5, in1=y, op0=ALU.mult, op1=ALU.mult))
                    link(V.tensor_tensor(nw2[:, 0:width], a, v, ALU.mult))
                    link(V.scalar_tensor_tensor(out=y, in0=nw2[:, 0:width], scalar=1.5, in1=y, op0=ALU.add, op1=ALU.mult))

            def norm(m):
                if m == 0:
                    dve.wait_ge(x_in[1], 16)
                link(V.tensor_tensor_reduce(out=hn[:, 1, :], in0=xs[:, 1, :], in1=xs[:, 1, :], scale=1.0, scalar=0.0,
                                            op0=ALU.mult, op1=ALU.add, accum_out=ss[:, 1:2]))
                dve.wait_ge(ss_done, [1, 4, 5, 8, 9][m])
                inverse_root(TT, D)
                dve.wait_ge(gain_first if m == 0 else gain_in[m % 2], 16 if m == 0 else 16 * ((m + 1) // 2))
                for t in range(TT):
                    V.scalar_tensor_tensor(out=hn[:, t, :], in0=xs[:, t, :], scalar=rstd[:, t:t + 1],
                                           in1=gain[:, m % 2, :], op0=ALU.mult, op1=ALU.mult).then_inc(
                                               out_rows if m == 4 else rows_done[t], 1)

            def turned(r):
                for j in range(4):
                    dve.wait_ge(t_hi, 4 * r + j + 1)
                    V.tensor_tensor(both(aT_lo[:, 2 * j:2 * j + 2, :]), ps[:, 4 + j, :],
                                    both(aT_hi[:, 2 * j:2 * j + 2, :]).bitcast(F32), ALU.subtract).then_inc(t_lo, 1)

            for l in range(DEPTH):
                n0 = LAYER1 * l
                norm(2 * l)
                for n in range(n0, n0 + 3):
                    split_lo(dve, n)
                turned(3 * l)

                def minus_abs(g):
                    dve.wait_ge(z_done, PAIRS * l + g + 1)
                    dve.wait_ge(z0_done, PAIRS * l + g + 1)
                    bank = (4, 2)[g % 2]
                    V.tensor_scalar(ab[:, g % 2].bitcast(I32), ps[:, bank:bank + 2, 0:ZW].bitcast(I32), SIGN, None,
                                    ALU.bitwise_or).then_inc(absz_done, 1)

                def softplus(g):
                    dve.wait_ge(ln_done, PAIRS * l + g + 1)
                    bank = (4, 2)[g % 2]
                    V.scalar_tensor_tensor(out=spl[:, g % 2], in0=ps[:, bank:bank + 2, 0:ZW], scalar=0.0, in1=ab[:, g % 2],
                                           op0=ALU.max, op1=ALU.add).then_inc(sp_done, 1)

                if l == 0:
                    dve.wait_ge(lam_ld, 16 * 4)
                    link(V.tensor_tensor(lam_pr[:], lam_in[:, 0:2], lam_in[:, 2:4], ALU.mult))
                    V.tensor_reduce(lam_s[:], lam_pr[:], AX.X, ALU.add).then_inc(lam_sum, 1)
                split_lo(dve, n0 + 3)
                split_lo(dve, n0 + 4)
                if l == 0:
                    dve.wait_ge(vrow_mm, 1)
                    V.tensor_copy(vrow[:], ps[0:DF_HEADS, 7, 0:384]).then_inc(vrow_done, 1)
                dve.wait_ge(piece_used, n0 + 4)
                V.tensor_copy(both(qk_sb[:, 4:8, :]), both(ps[:, 2:4, :])).then_inc(proj_saved2, 1)
                split_lo(dve, n0 + 5)
                minus_abs(0)
                if l == 0:
                    dve.wait_ge(lam_exp, 1)
                    link(V.tensor_tensor(lam_d[:], lam_e[:, 1, :], lam_e[:, 0, :], ALU.subtract))
                    for i in range(DEPTH):
                        link(V.tensor_scalar(nlam[:, i:i + 1], lam_d[:, i:i + 1], -lambda_init(i), None, ALU.add))
                split_lo(dve, n0 + 6)
                softplus(0)
                split_lo(dve, n0 + 7)
                if l == 0:
                    dve.wait_ge(bias_mm, 1)
                    V.tensor_copy(bias[:].rearrange("p h k -> p (h k)"), both(ps[:, 6:8, :])).then_inc(bias_done, 1)
                minus_abs(1)
                split_lo(dve, n0 + 8)
                softplus(1)
                split_lo(dve, n0 + 9)
                split_lo(dve, n0 + 10)
                minus_abs(2)
                softplus(2)
                split_lo(dve, n0 + 11)
                split_lo(dve, n0 + 12)
                minus_abs(3)
                softplus(3)
                split_lo(dve, n0 + 13)
                dve.wait_ge(piece_used, n0 + 12)
                V.tensor_copy(both(v_df[:]), both(ps[:, 0:2, :])).then_inc(v_df_saved, 1)
                split_lo(dve, n0 + 14)

                def scores(s):
                    h, n_k, bank = s // 2, P * (s % 2 + 1), 4 - 4 * (s % 2)
                    dve.wait_ge(zd_done, STEPS * l + s + 1)
                    dve.wait_ge(zd0_done, STEPS * l + s + 1)
                    z = zb[:, s % 3, :, 0:n_k]
                    link(V.tensor_tensor(z, ps[:, bank:bank + 2, 0:n_k],
                                         bias[:, h, S - n_k:S].unsqueeze(1).to_broadcast([P, 2, n_k]), ALU.add))
                    V.tensor_reduce(mx[:, s % 3, :], z, AX.X, ALU.max, negate=True).then_inc(mx_done, 1)

                def weigh(s):
                    h, t, n_k = s // 2, s % 2, P * (s % 2 + 1)
                    dve.wait_ge(e_done, STEPS * l + s + 1)
                    link(V.reciprocal(rr[:, t, h, :], es[:, s % 3, :]))
                    link(V.scalar_tensor_tensor(out=coef[:, s % 3, :], in0=es[:, s % 3, 0:1], scalar=nlam[:, l:l + 1],
                                                in1=rr[:, t, h, 1:2], op0=ALU.mult, op1=ALU.mult))
                    if s >= 2:
                        dve.wait_ge(wt_done, STEPS * l + s - 1)
                    V.scalar_tensor_tensor(out=wd[:, s % 2, 0:n_k], in0=zb[:, s % 3, 1, 0:n_k], scalar=coef[:, s % 3, :],
                                           in1=zb[:, s % 3, 0, 0:n_k], op0=ALU.mult, op1=ALU.add).then_inc(w_done, 1)

                def rows(c0, t, n_heads):
                    return hn[:, t, c0:c0 + HALF].rearrange("p (h d) -> p h d", h=n_heads)

                def over_d(a, n_heads):
                    return a.unsqueeze(2).to_broadcast([P, n_heads, HALF // n_heads])

                scores(0)
                scores(1)
                dve.wait_ge(ss_done, 4 * l + 2)
                link(V.tensor_reduce(ss[:, 0:16], sq[:].rearrange("p (a d) -> p a d", d=HD), AX.X, ALU.add))
                inverse_root(16, HD)
                for t in range(TT):
                    last = V.tensor_tensor(rows(0, t, SB_HEADS), ps[:, 6 + t, :].rearrange("p (h d) -> p h d", d=HD),
                                           over_d(rstd[:, 8 * t:8 * t + 8], SB_HEADS), ALU.mult)
                last.then_inc(sbo_saved, 1)
                if l == 0:
                    dve.wait_ge(small_in, 16 * 2)
                    for i in range(DEPTH):
                        V.tensor_scalar(g_df[:, i, :], g_df[:, i, :], 1.0 - lambda_init(i), None, ALU.mult)
                for i in range(2, STEPS + 2):
                    if i < STEPS:
                        scores(i)
                    weigh(i - 2)
                dve.wait_ge(sbo_saved, l + 1)
                for t in range(TT):
                    V.tensor_tensor(rows(0, t, SB_HEADS), rows(0, t, SB_HEADS),
                                    g_sb[:, l, :].unsqueeze(1).to_broadcast([P, SB_HEADS, HD]), ALU.mult)
                r0 = rr[:, :, :, 0]
                link(V.tensor_tensor(r0s[:], r0, r0, ALU.mult))
                dve.wait_ge(ss_done, 4 * l + 3)
                link(V.tensor_reduce(ss[:, 8:16], sq[:].rearrange("p (a d) -> p a d", d=2 * HD), AX.X, ALU.add))
                link(V.tensor_tensor(ss[:, 0:8], ss[:, 8:16], r0s[:].rearrange("p t h -> p (t h)"), ALU.mult))
                inverse_root(8, 2 * HD)
                link(V.tensor_tensor(scl[:], rstd[:, 0:8].rearrange("p (t h) -> p t h", t=TT), r0, ALU.mult))
                for t in range(TT):
                    last = V.tensor_tensor(rows(HALF, t, DF_HEADS), ps[:, 6 + t, :].rearrange("p (h d) -> p h d", h=DF_HEADS),
                                           over_d(scl[:, t, :], DF_HEADS), ALU.mult)
                link(last)
                for t in range(TT):
                    V.tensor_tensor(rows(HALF, t, DF_HEADS), rows(HALF, t, DF_HEADS),
                                    g_df[:, l, :].unsqueeze(1).to_broadcast([P, DF_HEADS, 2 * HD]), ALU.mult).then_inc(rows_done[t], 1)
                turned(3 * l + 1)
                split_lo(dve, n0 + 15)
                if l == 0:
                    split_lo(dve, 16)
                for u in range(2):
                    dve.wait_ge(piece_used, n0 + PROJ + 2 * u + 2)
                    for t in range(TT):
                        xv = xs[:, t, u * CH:u * CH + CH]
                        last = V.tensor_tensor(xv, xv, ps[:, 2 * u + t, :], ALU.add)
                        if u == 1 and t == 0:
                            last.then_inc(x_done, 1)
                link(last)
                norm(2 * l + 1)
                if l == 0:
                    split_lo(dve, 17)
                    split_lo(dve, 18)
                    turned(2)
                    for n in range(D_FULL + 1):
                        last_chunk = n == D_FULL
                        g = PROJ + WOUT + 4 * n
                        for i in range(g + 3, min(g + 7, PROJ + WOUT + DENSE_GU)):
                            split_lo(dve, i)
                        if last_chunk:
                            for i in range(PROJ + WOUT + DENSE_GU, PROJ + WOUT + DENSE_GU + 2):
                                split_lo(dve, i)
                        bank = 4 * (n % 2) + 2
                        width = D_REST * TT if last_chunk else 2 * CH
                        dve.wait_ge(silu_done, n + 1)
                        h = hn[:, n % 2, 0:width]
                        V.tensor_tensor(h, h, both(ps[:, bank:bank + 2, :])[:, 0:width], ALU.mult).then_inc(hid_done, 1)
                        if last_chunk:
                            split_lo(dve, PROJ + WOUT + DENSE_GU + 2)
                        dve.wait_ge(hT_hi_done, n + 1)
                        V.tensor_tensor(both(hT_lo[:, 4 * n:4 * n + width // S, :]), h,
                                        both(hT_hi[:, 4 * n:4 * n + width // S, :]).bitcast(F32),
                                        ALU.subtract).then_inc(hT_lo_done, 1)
                    for i in range(PROJ + WOUT + DENSE_GU + 3, LAYER1):
                        split_lo(dve, i)
                    dve.wait_ge(piece_used, LAYER1)
                    for t in range(TT):
                        last = V.tensor_tensor(xs[:, t, :], xs[:, t, :], both(ps[:, 2 * t:2 * t + 2, :]), ALU.add)
                        if t == 0:
                            last.then_inc(x_done, 1)
                    link(last)
            for n in range(3):
                split_lo(dve, MOE0 + n)

            def row(a, width=NE):
                return cst[:, a:a + width]

            def over_e(a):
                return a.unsqueeze(2).to_broadcast([P, TT, NE])

            dve.wait_ge(lg_done, 1)
            link(V.tensor_copy(lg[:].rearrange("p t e -> p (t e)"), ps[:, 0, 0:TT * NE]))
            rev = row(C_REV).unsqueeze(1).to_broadcast([P, TT, NE])
            for lgs, m, eq, rk, r, oh in ((lg, m1, eq1, rk1, r1, oh1), (lg2, m2, eq2, rk2, r2, oh2)):
                link(V.tensor_reduce(m[:], lgs[:], AX.X, ALU.max))
                link(V.tensor_tensor(eq[:], lgs[:], over_e(m[:]), ALU.is_equal))
                link(V.tensor_tensor(rk[:], eq[:], rev, ALU.mult))
                link(V.tensor_reduce(r[:], rk[:], AX.X, ALU.max))
                link(V.tensor_tensor(oh[:], rk[:], over_e(r[:]), ALU.is_equal))
                if lgs is lg:
                    link(V.scalar_tensor_tensor(out=lg2[:], in0=oh1[:], scalar=-3.0e38, in1=lg[:], op0=ALU.mult, op1=ALU.add))
            V.tensor_tensor(chosen[:], oh1[:], oh2[:], ALU.add).then_inc(chosen_done, 1)
            V.tensor_tensor(dm[:], m2[:], m1[:], ALU.subtract).then_inc(gap_done, 1)
            dve.wait_ge(part_done, 1)
            link(V.tensor_tensor(hn[:], hn[:], rows3[:, 0], ALU.subtract))
            V.tensor_copy(dn[:], m1[:]).then_inc(rest_done, 1)
            dve.wait_ge(pos_done, 1)
            link(V.tensor_scalar(posm0[:].rearrange("p t e -> p (t e)"), ps[:, 1, 0:TT * NE], NOT_CHOSEN, None, ALU.add))
            link(V.tensor_tensor(pm1[:], posm0[:], chosen[:], ALU.mult))
            link(V.tensor_scalar(posm[:], pm1[:], -NOT_CHOSEN, None, ALU.add))
            link(V.tensor_copy(cnt[:], ps[:, 1, TT * NE:TT * NE + NE]))

            def one_hot(places):
                for t in range(TT):
                    V.tensor_scalar(hot32[:, t, :], iota, places(t), None, ALU.is_equal)
                    last = V.tensor_scalar(onehot[:, t, :], iota, places(t), None, ALU.is_equal)
                last.then_inc(hot_ready, 1)

            one_hot(lambda t: posm[:, t, 0:1])
            dve.wait_ge(part_done, 2)
            V.tensor_tensor(rows3[:, 2], hn[:], rows3[:, 1], ALU.subtract).then_inc(rest_done, 1)

            def gates():
                dve.wait_ge(ge_done, 1)
                link(V.tensor_scalar(dn[:], ed[:], 1.0, None, ALU.add))
                link(V.reciprocal(g1[:], dn[:]))
                link(V.tensor_tensor(g2[:], ed[:], g1[:], ALU.mult))
                link(V.tensor_tensor(gg1[:], oh1[:], over_e(g1[:]), ALU.mult))
                link(V.tensor_tensor(gg[:], oh2[:], over_e(g2[:]), ALU.mult))
                link(V.tensor_tensor(gg[:], gg[:], gg1[:], ALU.add))
                link(V.tensor_scalar(nb1[:], cnt[:], 0.0, None, ALU.is_gt))
                link(V.memset(nb1[:, 0:1], 1.0))
                link(V.tensor_scalar(nb2[:], cnt[:], float(P), None, ALU.is_gt))
                link(V.tensor_tensor(nbe[:], nb1[:], nb2[:], ALU.add))

            def block_list():
                link(V.tensor_tensor(le8[:], cst[:, C_LE:C_LE + NE * NE].rearrange("p (j e) -> p j e", e=NE),
                                     nbe[:].unsqueeze(1).to_broadcast([P, NE, NE]), ALU.mult))
                link(V.tensor_reduce(ends[:], le8[:], AX.X, ALU.add))
                ends_b = ends[:].unsqueeze(1).to_broadcast([P, TAB, NE])
                link(V.tensor_tensor(cmpb[:], ends_b, row(C_B, TAB).unsqueeze(2).to_broadcast([P, TAB, NE]), ALU.is_le))
                link(V.tensor_reduce(eb[:], cmpb[:], AX.X, ALU.add))
                link(V.tensor_tensor(stb[:], cmpb[:], ends_b, ALU.mult))
                link(V.tensor_reduce(start[:], stb[:], AX.X, ALU.max))
                link(V.tensor_tensor(local[:], row(C_B, TAB), start[:], ALU.subtract))
                link(V.tensor_tensor(cm[:], row(C_E).unsqueeze(1).to_broadcast([P, TAB, NE]),
                                     eb[:].unsqueeze(2).to_broadcast([P, TAB, NE]), ALU.is_equal))
                link(V.tensor_scalar(ebi[:], eb[:], float(NE - 1), None, ALU.min))
                V.tensor_copy(nbi[:], ends[:, NE - 1:NE]).then_inc(tab_done, 1)

            def block_columns():
                for t in range(TT):
                    for i, (table, res) in enumerate(((posm, sel0), (gg, gate))):
                        link(V.tensor_tensor(tmpb[:, i, t], cm[:], table[:, t, :].unsqueeze(1).to_broadcast([P, TAB, NE]), ALU.mult))
                        link(V.tensor_reduce(res[:, t, :], tmpb[:, i, t], AX.X, ALU.add))
                    link(V.scalar_tensor_tensor(out=sel[:, t, :], in0=local[:], scalar=-float(P), in1=sel0[:, t, :],
                                                op0=ALU.mult, op1=ALU.add))

            def gathered(halves_before):
                for j in range(2):
                    dve.wait_ge(ga_hi, halves_before + j + 1)
                    last = V.tensor_tensor(both(xe_lo[:, 4 * j:4 * j + 4, :]), ps[:, 1 + 2 * j, :],
                                           both(xe_hi[:, 4 * j:4 * j + 4, :]).bitcast(F32), ALU.subtract)
                last.then_inc(ga_lo, 1)

            def output_lo(b):
                dve.wait_ge(y_hi, b)
                V.tensor_tensor(ye_lo[:], both(ps[:, 4:6, :]), ye_hi[:].bitcast(F32), ALU.subtract).then_inc(y_lo, 1)

            def add_back(b, t, bank=6):
                dve.wait_ge(sc_done[t], b)
                return V.scalar_tensor_tensor(out=xs[:, t, :], in0=both(ps[:, bank:bank + 2, :]),
                                              scalar=gate[:, t, bass.ds(b - 1, 1)], in1=xs[:, t, :], op0=ALU.mult, op1=ALU.add)

            def expert_block(b, first):
                def lo_of(kind, c, half):
                    if not (first and AT[(kind, c, half)] < SPL):
                        split_lo(dve, MOE0 + AT[(kind, c, half)], b)

                for c in range(E_CH + 1):
                    if c < E_CH:
                        lo_of("gate", c, 0)
                    if c > 0:
                        dve.wait_ge(esilu_done, b * E_CH + c)
                        V.tensor_tensor(hid[:, (c - 1) % 2, :], sil[:, (c - 1) % 2, :], ps[:, 2 + (c - 1) % 2, :],
                                        ALU.mult).then_inc(ehid_done, 1)
                    elif not first:
                        output_lo(b)
                    if c == 1 and not first:
                        add_back(b, 1).then_inc(sc_added[1], 1)
                    if c < E_CH:
                        lo_of("gate", c, 1)
                        lo_of("up", c, 0)
                        if c == 0 and not first:
                            add_back(b, 0).then_inc(sc_added[0], 1)
                        lo_of("up", c, 1)
                    else:
                        lo_of("down", c - 1, 0)
                        lo_of("down", c - 1, 1)
                    if c > 0:
                        dve.wait_ge(eh_hi, b * E_CH + c)
                        V.tensor_tensor(both(he_lo[:]), ps[:, 7, :], both(he_hi[:]).bitcast(F32), ALU.subtract).then_inc(eh_lo, 1)
                    if c == 2:
                        dve.wait_ge(hot_t, b + 1)
                        V.tensor_copy(onehotT[:].rearrange("p t s -> p (t s)"), ps[:, 6, 0:TT * P]).then_inc(hot_saved, 1)
                    if first and c == 1:
                        gates()
                    if first and c == 2:
                        block_list()
                    if first and c == 3:
                        block_columns()
                    if c == 4:
                        one_hot(lambda t: sel[:, t, bass.ds(b + 1, 1)])
                    if 0 < c < E_CH:
                        lo_of("down", c - 1, 0)
                        lo_of("down", c - 1, 1)
                gathered(b * 2 + 2)

            gathered(0)
            expert_block(0, True)
            dve.wait_ge(tab_done, 1)
            blocks = dve.value_load(nbi[0:1, 0:1], min_val=4, max_val=MAX_BLOCKS)
            with dve.Fori(1, blocks) as b:
                expert_block(b, False)
            output_lo(blocks)
            add_back(blocks, 0).then_inc(x_done, 1)
            link(add_back(blocks, 1, 0))
            norm(4)


_INS = ["x", "w_in", "w_out", "attn_norm", "ffn_norm", "sb_out_norm", "diff_subln", "lambda_q1", "lambda_k1",
        "lambda_q2", "lambda_k2", "rel_bias", "dense_w_gate", "dense_w_up", "dense_w_down", "router_w",
        "expert_w_gate", "expert_w_up", "expert_w_down", "final_norm"]


def kernel(**inputs):
    import concourse.bacc as bacc
    from concourse.bass_utils import run_bass_kernel_spmd

    nc = bacc.Bacc("TRN2", target_bir_lowering=False, num_devices=1)
    arrays = {f"in_{n}": np.ascontiguousarray(inputs[n]) for n in _INS}
    arrays["in_consts"] = constants()
    args = [nc.dram_tensor(n, a.shape, mybir.dt.from_np(a.dtype), kind="ExternalInput").ap() for n, a in arrays.items()]
    out = nc.dram_tensor("out_x", (1, S, D), F32, kind="ExternalOutput").ap()
    build(nc, *args, out)
    r = run_bass_kernel_spmd(nc, [arrays], core_ids=[0])
    return r.results[0]["out_x"]
```

```python
from contextlib import ExitStack
import math

import numpy as np

import concourse.bass as bass
from concourse import mybir

F32 = mybir.dt.float32
F32R = mybir.dt.float32r
BF16 = mybir.dt.bfloat16
I32 = mybir.dt.int32
ALU = mybir.AluOpType
ACT = mybir.ActivationFunctionType
AX = mybir.AxisListType

P = 128
D = 1024
S = 256
TT = S // P
KT = D // P
DEPTH = 2
SB_HEADS, DF_HEADS, HD = 8, 4, 64
HALF = SB_HEADS * HD
QKV = 6 * HALF
FD = 2816
FE = 3584
NE = 8
EPS = 1e-6
CH = 512
N_BUCKETS, MAX_DISTANCE = 32, 128
MASKED = -1.0e30
PIECE = 2048
RAW = 7
SPL = 3
D_FULL = FD // CH
D_REST = FD - D_FULL * CH
FT = FD // P
E_CH = FE // CH
PROJ = 12
WOUT = 4
DENSE_GU = 4 * D_FULL + 2
DENSE_DN = FD * D // (P * PIECE)
LAYER1 = PROJ + WOUT + DENSE_GU + DENSE_DN
MOE0 = LAYER1 + PROJ + WOUT
PER_BLOCK = 6 * E_CH
MAX_BLOCKS = S * 2 // P + NE - 1
TAB = MAX_BLOCKS + 1
NOT_CHOSEN = 1000.0
PAIRS = SB_HEADS // 2
ZW = 3 * P
STEPS = DF_HEADS * TT
SIGN = -2 ** 31
C_ID, C_NTRI, C_NONE, C_TRIS, C_ONE, C_IOTA = (P * i for i in range(6))
C_REV = 6 * P
C_E = C_REV + NE
C_LE = C_E + NE
C_B = C_LE + NE * NE
C_OH = C_B + TAB
C_MASKED = C_OH + 384
C_FLIP = C_MASKED + DF_HEADS
C_END = C_FLIP + P
CONSTS = C_OH


def constants():
    c = np.zeros((P, C_END), np.float32)
    r = np.arange(P)
    c[:, C_ID:C_ID + P] = np.eye(P)
    c[:, C_NTRI:C_NTRI + P] = -(r[:, None] >= r[None, :]).astype(np.float32)
    c[:, C_NONE:C_NONE + P] = -1.0
    c[:, C_TRIS:C_TRIS + P] = r[:, None] < r[None, :]
    c[:, C_ONE:C_ONE + P] = 1.0
    c[:, C_IOTA:C_IOTA + P] = r[None, :]
    e = np.arange(NE)
    c[:, C_REV:C_REV + NE] = NE - e
    c[:, C_E:C_E + NE] = e
    c[:, C_LE:C_LE + NE * NE] = (e[None, :] <= e[:, None]).astype(np.float32).reshape(-1)
    c[:, C_B:C_B + TAB] = np.arange(TAB)
    i = np.arange(384)
    dist = S - 1 - i
    exact = N_BUCKETS // 2
    n = np.maximum(dist, 1).astype(np.float32)
    large = exact + (np.log(n / np.float32(exact)) / np.float32(math.log(MAX_DISTANCE / exact))
                     * np.float32(N_BUCKETS - exact)).astype(np.int32)
    bucket = np.where(dist < exact, dist, np.minimum(large, N_BUCKETS - 1))
    bucket = np.where(dist < 0, N_BUCKETS, bucket)
    c[bucket, C_OH + i] = 1.0
    c[:, C_FLIP:C_FLIP + P] = np.eye(P)[::-1]
    c[N_BUCKETS, C_MASKED:C_MASKED + DF_HEADS] = MASKED
    return c


def lambda_init(layer):
    return 0.8 - 0.6 * math.exp(-0.3 * layer)


def build(nc, x, w_in, w_out, attn_norm, ffn_norm, sb_out_norm, diff_subln, lambda_q1, lambda_k1,
          lambda_q2, lambda_k2, rel_bias, dense_w_gate, dense_w_up, dense_w_down, router_w,
          expert_w_gate, expert_w_up, expert_w_down, final_norm, consts, out):
    with ExitStack() as ctx:
        def sb(name, shape, dt=F32, stack=ctx):
            return stack.enter_context(nc.sbuf_tensor(name, shape, dt))

        def sem(name):
            return ctx.enter_context(nc.semaphore(name))

        raw = sb("raw", [P, RAW, PIECE])
        w_hi = sb("w_hi", [P, SPL, PIECE], F32R)
        w_lo = sb("w_lo", [P, SPL, PIECE], F32R)
        xs = sb("xs", [P, TT, D])
        hn = sb("hn", [P, TT, D])
        gain = sb("gain", [P, D])
        g_sb = sb("g_sb", [P, DEPTH, HD])
        g_df = sb("g_df", [P, DEPTH, 2 * HD])
        cst = sb("cst", [P, CONSTS])
        eps = sb("eps", [P, 1])
        row_ss, row_ln, row_rstd, row_fine, row_var, row_tmp = (
            sb(n, [P, TT]) for n in ("row_ss", "row_ln", "row_rstd", "row_fine", "row_var", "row_tmp"))
        head_ss, head_ln, head_rstd, head_fine, head_var, head_tmp = (
            sb(n, [P, 16]) for n in ("head_ss", "head_ln", "head_rstd", "head_fine", "head_var", "head_tmp"))
        nlam = sb("nlam", [P, DEPTH])
        bias = sb("bias", [P, DF_HEADS, S])
        ps = ctx.enter_context(nc.psum_tensor("ps", [P, 8, 512], F32))

        until_experts = ExitStack()
        aT_hi = sb("aT_hi", [P, KT, S], F32R, until_experts)
        aT_lo = sb("aT_lo", [P, KT, S], F32R, until_experts)
        with ExitStack() as phase:
            def sp_(name, shape, dt=F32):
                return sb(name, shape, dt, phase)
            qk_sb = sp_("qk_sb", [P, 8, S])
            qk_df = sp_("qk_df", [P, 8, S])
            v_sb = sp_("v_sb", [P, TT, HALF])
            v_df = sp_("v_df", [P, TT, HALF])
            ab = sp_("ab", [P, 2, 2, ZW])
            sq = ab[:].rearrange("p a h q -> p (a h q)")[:, 0:TT * HALF]
            spl = sp_("spl", [P, 2, 2, ZW])
            zb = sp_("zb", [P, 4, 2, S])
            bias_up = zb[:, 0:2].rearrange("p a c k -> p (a c) k")
            wT = sp_("wT", [P, 2, S])
            mx = sp_("mx", [P, 3, 2])
            es = sp_("es", [P, 3, 2])
            rr = sp_("rr", [P, TT, DF_HEADS, 2])
            r0s = sp_("r0s", [P, TT, DF_HEADS])
            scl = sp_("scl", [P, TT, DF_HEADS])
            coef = sp_("coef", [P, 3, 1])
            with ExitStack() as early:
                lam_in = sb("lam_in", [P, 4, DEPTH, HD], F32, early)
                lam_pr = sb("lam_pr", [P, 2, DEPTH, HD], F32, early)
                lam_s = sb("lam_s", [P, 2, DEPTH], F32, early)
                lam_e = sb("lam_e", [P, 2, DEPTH], F32, early)
                lam_d = sb("lam_d", [P, DEPTH], F32, early)
                bkt = sb("bkt", [N_BUCKETS + 1, 384 + DF_HEADS], F32, early)
                vrow = sb("vrow", [DF_HEADS, 384], F32, early)
                flip = sb("flip", [P, P], F32, early)
            att = sp_("att", [P, 2, 2, ZW])
            wd = sp_("wd", [P, 2, S])
        with ExitStack() as phase:
            hT_hi = sb("hT_hi", [P, FT, S], F32R, phase)
            hT_lo = sb("hT_lo", [P, FT, S], F32R, phase)
        until_experts.close()
        with ExitStack() as phase:
            def se(name, shape, dt=F32):
                return sb(name, shape, dt, phase)
            rT = se("rT", [P, KT, S])
            rw = se("rw", [P, KT, NE])
            lgT = se("lgT", [NE, S])
            lg = se("lg", [P, TT, NE])
            lg2 = se("lg2", [P, TT, NE])
            m1 = se("m1", [P, TT])
            m2 = se("m2", [P, TT])
            eq1, rk1, oh1 = se("eq1", [P, TT, NE]), se("rk1", [P, TT, NE]), se("oh1", [P, TT, NE])
            eq2, rk2, oh2 = se("eq2", [P, TT, NE]), se("rk2", [P, TT, NE]), se("oh2", [P, TT, NE])
            r1, r2 = se("r1", [P, TT]), se("r2", [P, TT])
            dm, ed, dn = se("dm", [P, TT]), se("ed", [P, TT]), se("dn", [P, TT])
            g1, g2 = se("g1", [P, TT]), se("g2", [P, TT])
            chosen = se("chosen", [P, TT, NE], BF16)
            counts = se("counts", [P, 2, P], BF16)
            gg1, gg = se("gg1", [P, TT, NE]), se("gg", [P, TT, NE])
            pm1, posm0, posm = se("pm1", [P, TT, NE]), se("posm0", [P, TT, NE]), se("posm", [P, TT, NE])
            cnt = se("cnt", [P, NE])
            nb1, nb2, nbe = se("nb1", [P, NE]), se("nb2", [P, NE]), se("nbe", [P, NE])
            le8 = se("le8", [P, NE, NE])
            ends = se("ends", [P, NE])
            cmpb = se("cmpb", [P, TAB, NE])
            eb = se("eb", [P, TAB])
            stb = se("stb", [P, TAB, NE])
            start = se("start", [P, TAB])
            local = se("local", [P, TAB])
            cm = se("cm", [P, TAB, NE])
            tmpb = se("tmpb", [P, 2, TT, TAB, NE])
            sel0 = se("sel0", [P, TT, TAB])
            sel = se("sel", [P, TT, TAB])
            gate = se("gate", [P, TT, TAB])
            ebi = se("ebi", [P, TAB], I32)
            nbi = se("nbi", [P, 1], I32)
            xe_hi = se("xe_hi", [P, KT, P], F32R)
            xe_lo = se("xe_lo", [P, KT, P], F32R)
            rows3 = se("rows3", [P, 3, TT, D], BF16)
            onehot = se("onehot", [P, TT, P], BF16)
            hot32 = se("hot32", [P, TT, P])
            onehotT = se("onehotT", [P, TT, P], F32R)
            he_hi = se("he_hi", [P, 4, P], F32R)
            he_lo = se("he_lo", [P, 4, P], F32R)
            ye_hi = se("ye_hi", [P, D], F32R)
            ye_lo = se("ye_lo", [P, D], F32R)
            sil = se("sil", [P, 2, CH])
            hid = se("hid", [P, 2, CH])

        scratch = nc.dram_tensor("bias_scratch", (DF_HEADS, 384), F32, kind="Internal").ap()
        ident = cst[:, C_ID:C_ID + P]
        neg_tri = cst[:, C_NTRI:C_NTRI + P]
        neg_one = cst[:, C_NONE:C_NONE + P]
        iota = cst[:, C_IOTA:C_IOTA + P]

        raw_in = [sem(f"raw_in{i}") for i in range(RAW)]
        hi_ready, lo_ready, piece_used = sem("hi_ready"), sem("lo_ready"), sem("piece_used")
        x_in = [sem("x_in0"), sem("x_in1")]
        cst_in, small_in, lam_ld, bkt_in = (sem(n) for n in ("cst_in", "small_in", "lam_ld", "bkt_in"))
        rw_in = sem("rw_in")
        gain_first, gain_in = sem("gain_first"), sem("gain_in")
        x_done, tile0_done = [sem("x_done0"), sem("x_done1")], sem("tile0_done")
        eps_done, row_rstd_done = sem("eps_done"), sem("row_rstd_done")
        row_ss_done = sem("row_ss_done")
        ss_done, head_sums, head_rstd_done, sb_rows = (sem(n) for n in ("ss_done", "head_sums", "head_rstd_done", "sb_rows"))
        rows_done = [sem("rows_done0"), sem("rows_done1")]
        t_done, t_hi, t_lo = sem("t_done"), sem("t_hi"), sem("t_lo")
        proj_saved, proj_saved2 = sem("proj_saved"), sem("proj_saved2")
        z_done, absz_done, ln_done, sp_done, spm_done, tri_done, a_done, am_done, pv_done = (
            sem(n) for n in ("z_done", "absz_done", "ln_done", "sp_done", "spm_done", "tri_done", "a_done", "am_done", "pv_done"))
        z0_done, zd0_done, v_df_saved = sem("z0_done"), sem("zd0_done"), sem("v_df_saved")
        sbo_saved = sem("sbo_saved")
        zd_done, mx_done, e_done, w_done, wt_done, wt_saved, pvd_done = (
            sem(n) for n in ("zd_done", "mx_done", "e_done", "w_done", "wt_done", "wt_saved", "pvd_done"))
        lam_sum, lam_exp = sem("lam_sum"), sem("lam_exp")
        vrow_mm, vrow_done, scratch_done, bias_in = sem("vrow_mm"), sem("vrow_done"), sem("scratch_done"), sem("bias_in")
        bias_mm, bias_done = sem("bias_mm"), sem("bias_done")
        silu_done, hid_done, hT_hi_done, hT_lo_done = (
            sem(n) for n in ("silu_done", "hid_done", "hT_hi_done", "hT_lo_done"))
        rT_done, lg_done, gap_done, ge_done, chosen_done, pos_done, tab_done = (
            sem(n) for n in ("rT_done", "lg_done", "gap_done", "ge_done", "chosen_done", "pos_done", "tab_done"))
        lgT_done, lgT_saved = sem("lgT_done"), sem("lgT_saved")
        part_done, rest_done = sem("part_done"), sem("rest_done")
        ga_done, ga_hi, ga_lo = sem("ga_done"), sem("ga_hi"), sem("ga_lo")
        esilu_done, ehid_done, et_done, eh_hi, eh_lo = (
            sem(n) for n in ("esilu_done", "ehid_done", "et_done", "eh_hi", "eh_lo"))
        y_hi, y_lo = sem("y_hi"), sem("y_lo")
        sc_done, sc_added = [sem("sc_done0"), sem("sc_done1")], [sem("sc_added0"), sem("sc_added1")]
        hot_t, hot_saved, hot_ready = (sem(n) for n in ("hot_t", "hot_saved", "hot_ready"))
        out_rows, out_sent = sem("out_rows"), sem("out_sent")
        dve_chain, act_chain = sem("dve_chain"), sem("act_chain")

        win_v = [w_in[l].rearrange("(k p) n -> p k n", p=P) for l in range(DEPTH)]
        wout_v = [w_out[l].rearrange("(k p) n -> p k n", p=P) for l in range(DEPTH)]
        gate_v = dense_w_gate[0].rearrange("(k p) n -> p k n", p=P)
        up_v = dense_w_up[0].rearrange("(k p) n -> p k n", p=P)
        down_v = dense_w_down[0].rearrange("(f p) n -> p f n", p=P)
        egate_v = expert_w_gate[0].rearrange("e (k p) n -> e p k n", p=P)
        eup_v = expert_w_up[0].rearrange("e (k p) n -> e p k n", p=P)
        edown_v = expert_w_down[0].rearrange("e (f p) n -> e p f n", p=P)

        def halves(view, col):
            return [view[:, 4 * h:4 * h + 4, col:col + CH] for h in range(2)]

        sources = []
        for l in range(DEPTH):
            for u in range(PROJ // 2):
                sources += halves(win_v[l], u * CH)
            per_unit = [halves(wout_v[l], u * CH) for u in range(WOUT // 2)]
            sources += [unit[h] for h in range(2) for unit in per_unit]
            if l == 0:
                for n in range(D_FULL):
                    sources += halves(gate_v, n * CH) + halves(up_v, n * CH)
                sources += [gate_v[:, :, D_FULL * CH:FD], up_v[:, :, D_FULL * CH:FD]]
                sources += [down_v[:, 2 * i:2 * i + 2, :] for i in range(DENSE_DN)]
        assert len(sources) == MOE0

        def expert_pieces():
            order = []
            for c in range(E_CH + 1):
                if c < E_CH:
                    order += [("gate", c, 0), ("gate", c, 1), ("up", c, 0), ("up", c, 1)]
                if c > 0:
                    order += [("down", c - 1, 0), ("down", c - 1, 1)]
            return order

        ORDER = expert_pieces()
        assert len(ORDER) == PER_BLOCK and PER_BLOCK % RAW == 0 and PER_BLOCK % SPL == 0
        AT = {k: i for i, k in enumerate(ORDER)}
        ROUNDS = PER_BLOCK // RAW

        def landed(n, b=None):
            return 16 * (n // RAW + 1) if b is None else b * (16 * ROUNDS) + 16 * (n // RAW + 1)

        def nth(n, b=None):
            return n if b is None else b * PER_BLOCK + n

        def split_hi(act, n, b=None):
            act.wait_ge(raw_in[n % RAW], landed(n, b))
            if n >= SPL:
                act.wait_ge(piece_used, nth(n - SPL + 1, b))
            nc.scalar.activation(w_hi[:, n % SPL, :], raw[:, n % RAW, :], ACT.Copy).then_inc(hi_ready, 1)

        def split_lo(dve, n, b=None):
            dve.wait_ge(hi_ready, nth(n + 1, b))
            nc.vector.tensor_tensor(w_lo[:, n % SPL, :], raw[:, n % RAW, :],
                                    w_hi[:, n % SPL, :].bitcast(F32), ALU.subtract).then_inc(lo_ready, 1)

        block = ctx.enter_context(nc.Block())

        @block.sync
        def _(sp):
            for t in range(TT):
                sp.dma_start(xs[:, t, :], x[0, t * P:t * P + P, :]).then_inc(x_in[t], 16)

            def load(n, src, b=None):
                if n >= RAW:
                    sp.wait_ge(lo_ready, nth(n - RAW + 1, b))
                dst = raw[:, n % RAW, :].rearrange("p (k n) -> p k n", n=src.shape[-1])
                sp.dma_start(dst, src).then_inc(raw_in[n % RAW], 16)

            for n, src in enumerate(sources):
                load(n, src)

            def load_block(b, e):
                for i, (kind, c, h) in enumerate(ORDER):
                    if kind == "down":
                        src = edown_v[e, :, 4 * c + 2 * h:4 * c + 2 * h + 2, :]
                    else:
                        src = (egate_v if kind == "gate" else eup_v)[e, :, 4 * h:4 * h + 4, c * CH:c * CH + CH]
                    load(MOE0 + i, src.rearrange("e p k n -> (e p) k n"), b)

            load_block(0, slice(0, 1))
            sp.wait_ge(tab_done, 1)
            final = sp.value_load(nbi[0:1, 0:1], min_val=3, max_val=MAX_BLOCKS - 1)
            with sp.Fori(1, final + 1) as b:
                load_block(b, bass.ds(sp.value_load(ebi[0:1, bass.ds(b, 1)], min_val=0, max_val=NE - 1), 1))
            for t in range(TT):
                sp.wait_ge(out_rows, t + 1)
                sp.dma_start(out[0, t * P:t * P + P, :], hn[:, t, :]).then_inc(out_sent, 16)
            sp.wait_ge(out_sent, 16 * TT)

        @block.gpsimd
        def _(pool):
            norms = [attn_norm[0], ffn_norm[0], attn_norm[1], ffn_norm[1], final_norm]

            def load_gain(m):
                pool.wait_ge(rows_done[1], [None, 1, 3, 4, 6][m])
                pool.dma_start(gain[:], norms[m].partition_broadcast(P)).then_inc(gain_in, 16)

            pool.dma_start(bkt[:, 0:384], consts[0:N_BUCKETS + 1, C_OH:C_OH + 384]).then_inc(bkt_in, 16)
            pool.dma_start(bkt[0:N_BUCKETS, 384:384 + DF_HEADS], rel_bias[:, :]).then_inc(bkt_in, 16)
            pool.dma_start(bkt[N_BUCKETS:N_BUCKETS + 1, 384:384 + DF_HEADS],
                           consts[N_BUCKETS:N_BUCKETS + 1, C_MASKED:C_FLIP]).then_inc(bkt_in, 16)
            pool.dma_start(flip[:], consts[:, C_FLIP:C_END]).then_inc(bkt_in, 16)
            for i, v in enumerate((lambda_q1, lambda_q2, lambda_k1, lambda_k2)):
                pool.dma_start(lam_in[:, i], v.rearrange("l d -> (l d)").partition_broadcast(P)).then_inc(lam_ld, 16)
            pool.dma_start(g_sb[:].rearrange("p l d -> p (l d)"),
                           sb_out_norm.rearrange("l d -> (l d)").partition_broadcast(P)).then_inc(small_in, 16)
            pool.dma_start(g_df[:].rearrange("p l d -> p (l d)"),
                           diff_subln.rearrange("l d -> (l d)").partition_broadcast(P)).then_inc(small_in, 16)
            pool.wait_ge(vrow_done, 1)
            pool.dma_start(scratch, vrow[:]).then_inc(scratch_done, 16)
            pool.wait_ge(scratch_done, 16)
            pool.dma_start(bias_up, bass.AP(scratch.tensor, 0, [[1, P], [384, DF_HEADS], [1, S]])).then_inc(bias_in, 16)

            def causal(tile, parity):
                for h in range(2):
                    v = tile[:, parity, h].rearrange("p (a q) -> p a q", q=P)[:, 0:3:2, :]
                    last = nc.gpsimd.affine_select(out=v, in_=v, compare_op=ALU.is_gt, fill=0.0, base=0,
                                                   pattern=[[0, 2], [1, P]], channel_multiplier=-1)
                return last

            for l in range(DEPTH):
                for g in range(PAIRS):
                    i = PAIRS * l + g
                    pool.wait_ge(sp_done, i + 1)
                    causal(spl, g % 2).then_inc(spm_done, 1)
                    pool.wait_ge(a_done, i + 1)
                    causal(att, g % 2).then_inc(am_done, 1)
                    if g == 0 and l == 0:
                        load_gain(1)
                pool.wait_ge(sbo_saved, l + 1)
                pool.wait_ge(small_in, 16 * 2)
                for t in range(TT):
                    h = hn[:, t, 0:HALF].rearrange("p (h d) -> p h d", d=HD)
                    nc.gpsimd.tensor_tensor(h, h, g_sb[:, l, :].unsqueeze(1).to_broadcast([P, SB_HEADS, HD]),
                                            ALU.mult).then_inc(sb_rows, 1)
                if l == 0:
                    load_gain(2)
                    load_gain(3)
            pool.wait_ge(piece_used, MOE0)
            pool.dma_start(rw[:], router_w[0].rearrange("(k p) e -> p k e", p=P)).then_inc(rw_in, 16)
            for t in range(TT):
                pool.wait_ge(rows_done[t], 6)
                nc.gpsimd.tensor_copy(rows3[:, 0, t], hn[:, t]).then_inc(part_done, 1)
            pool.wait_ge(part_done, TT + 1)
            nc.gpsimd.tensor_tensor(rows3[:, 2], hn[:], rows3[:, 1], ALU.subtract).then_inc(rest_done, 1)
            load_gain(4)

        @block.tensor
        def _(pe):
            def mm3(o, s_hi, s_lo, m_hi, m_lo, start, stop):
                pe.matmul(o, s_hi, m_hi, start=start, stop=False, skip_group_check=True)
                pe.matmul(o, s_hi, m_lo, start=False, stop=False, skip_group_check=True)
                return pe.matmul(o, s_lo, m_hi, start=False, stop=stop, skip_group_check=True)

            def piece(n, b=None):
                pe.wait_ge(lo_ready, nth(n + 1, b))
                return w_hi[:, n % SPL, :], w_lo[:, n % SPL, :]

            def columns_out(n, bank, half, k_tiles=4, width=CH):
                hi, lo = piece(n)
                for ct in range(width // P):
                    o = ps[:, bank + ct // 2, (ct % 2) * S:(ct % 2) * S + S]
                    for k in range(k_tiles):
                        kk = k_tiles * half + k
                        c0 = k * width + ct * P
                        last = mm3(o, hi[:, c0:c0 + P], lo[:, c0:c0 + P], aT_hi[:, kk, :], aT_lo[:, kk, :],
                                   start=(kk == 0 and ct % 2 == 0), stop=(kk == KT - 1))
                last.then_inc(piece_used, 1)

            def rows_out(n, bank, half, ends=False):
                hi, lo = piece(n)
                for t in range(TT):
                    for k in range(4):
                        kk = 4 * half + k
                        last = mm3(ps[:, bank + t, :], aT_hi[:, kk, t * P:t * P + P], aT_lo[:, kk, t * P:t * P + P],
                                   hi[:, k * CH:k * CH + CH], lo[:, k * CH:k * CH + CH],
                                   start=(kk == 0), stop=(kk == KT - 1))
                    if ends and t == 0:
                        last.then_inc(tile0_done, 1)
                last.then_inc(piece_used, 1)

            def turn_rows(r, banks=range(4)):
                for t in range(TT):
                    if len(banks) == 4:
                        pe.wait_ge(rows_done[t], r + 1)
                    for j in banks:
                        for q in range(2):
                            last = pe.transpose(ps[:, 4 + j, (2 * q + t) * P:(2 * q + t) * P + P],
                                                hn[:, t, (2 * j + q) * P:(2 * j + q) * P + P], ident)
                        if t == TT - 1:
                            last.then_inc(t_done, 1)

            pe.wait_ge(cst_in, 16)
            for l in range(DEPTH):
                n0 = LAYER1 * l
                turn_rows(3 * l)

                def project(u, bank):
                    for half in range(2):
                        if u == 0:
                            pe.wait_ge(t_lo, 12 * l + 2 + 2 * half)
                        (rows_out if u in (2, 5) else columns_out)(n0 + 2 * u + half, bank, half)

                def z_pair(g):
                    for m in range(2):
                        q = qk_sb[HD * m:HD * m + HD, g, :]
                        k = qk_sb[HD * m:HD * m + HD, 4 + g, :]
                        bank = ps[:, (4, 2)[g % 2] + m, :]
                        pe.matmul(bank[:, 0:S], k[:, 0:P], q, start=True, stop=False, skip_group_check=True)
                        last = pe.matmul(bank[:, S:ZW], k[:, P:S], q[:, P:S], start=False, stop=False, skip_group_check=True)
                        if m == 0:
                            last.then_inc(z0_done, 1)
                    last.then_inc(z_done, 1)

                def add_stays(g):
                    pe.wait_ge(spm_done, PAIRS * l + g + 1)
                    for m in range(2):
                        bank = ps[:, (4, 2)[g % 2] + m, :]
                        pe.matmul(bank[:, 0:ZW], neg_tri, spl[:, g % 2, m, :], start=False, stop=False, skip_group_check=True)
                        last = pe.matmul(bank[:, P:S], neg_one, spl[:, g % 2, m, S:ZW], start=False, stop=True,
                                         skip_group_check=True)
                    last.then_inc(tri_done, 1)

                def values(g):
                    pe.wait_ge(am_done, PAIRS * l + g + 1)
                    for m in range(2):
                        a = att[:, g % 2, m, :]
                        c = slice(HD * (2 * g + m), HD * (2 * g + m) + HD)
                        pe.matmul(ps[:, 6, c], a[:, 0:P], v_sb[:, 0, c], start=True, stop=True, skip_group_check=True)
                        pe.matmul(ps[:, 7, c], a[:, P:S], v_sb[:, 0, c], start=True, stop=False, skip_group_check=True)
                        last = pe.matmul(ps[:, 7, c], a[:, S:ZW], v_sb[:, 1, c], start=False, stop=True, skip_group_check=True)
                    last.then_inc(pv_done, 1)

                project(0, 0)
                if l == 0:
                    pe.wait_ge(bkt_in, 64)
                    pe.matmul(ps[0:DF_HEADS, 7, 0:384], bkt[:, 384:384 + DF_HEADS], bkt[:, 0:384],
                              start=True, stop=True).then_inc(vrow_mm, 1)
                project(1, 2)
                pe.wait_ge(proj_saved, 4 * l + 1)
                pe.wait_ge(proj_saved2, l + 1)
                z_pair(0)
                project(2, 0)
                if l == 0:
                    pe.wait_ge(bias_in, 16)
                    pe.wait_ge(vrow_done, 1)
                    for h in range(DF_HEADS):
                        last = pe.matmul(ps[:, 6 + h // 2, (h % 2) * S:(h % 2) * S + S], flip[:], bias_up[:, h, :],
                                         start=(h % 2 == 0), stop=(h % 2 == 1), skip_group_check=True)
                    last.then_inc(bias_mm, 1)
                add_stays(0)
                z_pair(1)
                pe.wait_ge(proj_saved, 4 * l + 2)
                project(3, 0)
                if l == 0:
                    pe.wait_ge(bias_done, 1)
                values(0)
                add_stays(1)
                z_pair(2)
                pe.wait_ge(proj_saved, 4 * l + 3)
                project(4, 0)
                values(1)
                add_stays(2)
                z_pair(3)
                pe.wait_ge(proj_saved, 4 * l + 4)

                def scores(s):
                    h, t = s // 2, s % 2
                    if s >= 2:
                        pe.wait_ge(mx_done, STEPS * l + s - 1)
                    if s == 1:
                        pe.wait_ge(v_df_saved, l + 1)
                    for c in range(2):
                        q = qk_df[HD * c:HD * c + HD, h, t * P:t * P + P]
                        k = qk_df[HD * c:HD * c + HD, 4 + h, 0:P * (t + 1)]
                        last = pe.matmul(ps[:, 4 - 4 * (s % 2) + c, 0:P * (t + 1)], q, k, start=True, stop=True)
                        if c == 0:
                            last.then_inc(zd0_done, 1)
                    last.then_inc(zd_done, 1)

                def turn_weights(j):
                    pe.wait_ge(w_done, STEPS * l + j + 1)
                    if j >= 2:
                        pe.wait_ge(wt_saved, STEPS * l + j - 1)
                    for kb in range(j % 2 + 1):
                        last = pe.transpose(ps[:, 2 + j % 2, kb * P:kb * P + P], wd[:, j % 2, kb * P:kb * P + P], ident)
                    last.then_inc(wt_done, 1)

                def df_values(j):
                    h, t = j // 2, j % 2
                    pe.wait_ge(wt_saved, STEPS * l + j + 1)
                    if j == 0:
                        pe.wait_ge(sbo_saved, l + 1)
                    c = slice(2 * HD * h, 2 * HD * h + 2 * HD)
                    for kb in range(t + 1):
                        last = pe.matmul(ps[:, 6 + t, c], wT[:, j % 2, kb * P:kb * P + P], v_df[:, kb, c],
                                         start=(kb == 0), stop=(kb == t), skip_group_check=True)
                    if j == STEPS - 1:
                        last.then_inc(pvd_done, 1)

                rows_out(n0 + 10, 0, 0)
                values(2)
                scores(0)
                add_stays(3)
                rows_out(n0 + 11, 0, 1)
                values(3)
                scores(1)
                for i in range(2, STEPS + 4):
                    if i < STEPS:
                        scores(i)
                    if 3 <= i < STEPS + 3:
                        turn_weights(i - 3)
                    if i >= 4:
                        df_values(i - 4)
                    if i == STEPS:
                        pe.wait_ge(sb_rows, TT * (l + 1))
                        pe.wait_ge(mx_done, STEPS * l + STEPS - 1)
                        turn_rows(3 * l + 1, range(2))

                pe.wait_ge(t_lo, 12 * l + 6)
                pe.wait_ge(mx_done, STEPS * (l + 1))
                for u in range(2):
                    rows_out(n0 + PROJ + u, 2 * u, 0)
                for t in range(TT):
                    pe.wait_ge(rows_done[t], 3 * l + 2)
                turn_rows(3 * l + 1, range(2, 4))
                pe.wait_ge(t_lo, 12 * l + 8)
                for u in range(2):
                    rows_out(n0 + PROJ + 2 + u, 2 * u, 1, ends=(u == 1))
                turn_rows(3 * l + 2)
                if l == 0:
                    for n in range(D_FULL + 1):
                        if n >= 2:
                            pe.wait_ge(hT_lo_done, n - 1)
                        g = PROJ + WOUT + 4 * n
                        bank = 4 * (n % 2)
                        if n < D_FULL:
                            for half in range(2):
                                if n == 0:
                                    pe.wait_ge(t_lo, 10 + 2 * half)
                                columns_out(g + half, bank, half)
                            for half in range(2):
                                columns_out(g + 2 + half, bank + 2, half)
                        else:
                            columns_out(g, bank, 0, KT, D_REST)
                            columns_out(g + 1, bank + 2, 0, KT, D_REST)
                    for i in range(DENSE_DN):
                        hi, lo = piece(PROJ + WOUT + DENSE_GU + i)
                        if i % 2 == 0:
                            pe.wait_ge(hT_lo_done, i // 2 + 1)
                        for t in range(TT):
                            for f in range(2):
                                ff = 2 * i + f
                                for c in range(2):
                                    at = f * D + c * CH
                                    last = mm3(ps[:, 2 * t + c, :], hT_hi[:, ff, t * P:t * P + P], hT_lo[:, ff, t * P:t * P + P],
                                               hi[:, at:at + CH], lo[:, at:at + CH], start=(ff == 0), stop=(ff == FT - 1))
                            if i == DENSE_DN - 1 and t == 0:
                                last.then_inc(tile0_done, 1)
                        last.then_inc(piece_used, 1)

            pe.wait_ge(rw_in, 16)
            for k in range(KT):
                pe.wait_ge(rT_done, k // 2 + 1)
                last = pe.matmul(ps[0:NE, 0, 0:S], rw[:, k, :], rT[:, k, :], start=(k == 0), stop=(k == KT - 1))
            last.then_inc(lgT_done, 1)
            pe.wait_ge(lgT_saved, 1)
            for t in range(TT):
                last = pe.transpose(ps[:, 2, t * NE:t * NE + NE], lgT[:, t * P:t * P + P], ident[0:NE, 0:NE])
            last.then_inc(lg_done, 1)
            pe.wait_ge(chosen_done, 1)
            pe.matmul(ps[:, 1, 0:NE], counts[:, 0, :], chosen[:, 0, :], start=True, stop=True, skip_group_check=True)
            pe.matmul(ps[:, 1, NE:2 * NE], counts[:, 0, :], chosen[:, 1, :], start=True, stop=False, skip_group_check=True)
            pe.matmul(ps[:, 1, NE:2 * NE], counts[:, 1, :], chosen[:, 0, :], start=False, stop=True, skip_group_check=True)
            pe.matmul(ps[:, 1, 2 * NE:3 * NE], counts[:, 1, :], chosen[:, 0, :], start=True, stop=False, skip_group_check=True)
            pe.matmul(ps[:, 1, 2 * NE:3 * NE], counts[:, 1, :], chosen[:, 1, :], start=False, stop=True,
                      skip_group_check=True).then_inc(pos_done, 1)

            def gather(count):
                pe.wait_ge(hot_ready, count)
                for j in range(2):
                    for q in range(4):
                        k = 4 * j + q
                        for t in range(TT):
                            for part in range(3):
                                last = pe.matmul(ps[:, 1 + 2 * j, q * P:q * P + P], rows3[:, part, t, k * P:k * P + P],
                                                 onehot[:, t, :], start=(t == 0 and part == 0), stop=(t == 1 and part == 2),
                                                 skip_group_check=True)
                    last.then_inc(ga_done, 1)

            def scatter(t, bank=6):
                for c in range(2):
                    for part in (ye_hi, ye_lo):
                        last = pe.matmul(ps[:, bank + c, :], onehotT[:, t, :], part[:, c * CH:c * CH + CH],
                                         start=(part is ye_hi), stop=(part is ye_lo), skip_group_check=True)
                last.then_inc(sc_done[t], 1)

            def expert_block(b, first, last_block=False):
                def expert_in(kind, c, half):
                    n = MOE0 + AT[(kind, c, half)]
                    hi, lo = piece(n, b)
                    if kind == "gate" and c == 0:
                        pe.wait_ge(ga_lo, b * 2 + half + 1)
                    bank = (0 if kind == "gate" else 2) + c % 2
                    for k in range(4):
                        kk = 4 * half + k
                        last = mm3(ps[:, bank, :], xe_hi[:, kk, :], xe_lo[:, kk, :], hi[:, k * CH:k * CH + CH],
                                   lo[:, k * CH:k * CH + CH], start=(kk == 0), stop=(kk == KT - 1))
                    last.then_inc(piece_used, 1)

                def turn_hidden(c):
                    pe.wait_ge(ehid_done, b * E_CH + c + 1)
                    for f in range(4):
                        last = pe.transpose(ps[:, 7, f * P:f * P + P], hid[:, c % 2, f * P:f * P + P], ident)
                    last.then_inc(et_done, 1)

                def expert_down(c, half):
                    hi, lo = piece(MOE0 + AT[("down", c, half)], b)
                    if half == 0:
                        pe.wait_ge(eh_lo, b * E_CH + c + 1)
                    for f in range(2):
                        ff = 2 * half + f
                        for o in range(2):
                            at = f * D + o * CH
                            last = mm3(ps[:, 4 + o, :], he_hi[:, ff, :], he_lo[:, ff, :], hi[:, at:at + CH], lo[:, at:at + CH],
                                       start=(c == 0 and ff == 0), stop=(c == E_CH - 1 and ff == 3))
                    last.then_inc(piece_used, 1)

                for c in range(E_CH + 1):
                    if c < E_CH:
                        expert_in("gate", c, 0)
                        expert_in("gate", c, 1)
                    if c == 0 and not first:
                        pe.wait_ge(y_lo, b)
                        pe.wait_ge(hot_saved, b)
                        scatter(0)
                    if c == 1 and not first:
                        pe.wait_ge(sc_added[1], b)
                    if c > 0:
                        turn_hidden(c - 1)
                    if c == 2:
                        for t in range(TT):
                            last = pe.transpose(ps[:, 6, t * P:t * P + P], hot32[:, t, :], ident)
                        last.then_inc(hot_t, 1)
                    if c == E_CH - 1 and not last_block:
                        gather(b + 2)
                    if c < E_CH:
                        expert_in("up", c, 0)
                        expert_in("up", c, 1)
                    if c == 0 and not first:
                        pe.wait_ge(sc_added[0], b)
                        scatter(1)
                    if c > 0:
                        expert_down(c - 1, 0)
                        expert_down(c - 1, 1)

            pe.wait_ge(rest_done, 2)
            gather(1)
            expert_block(0, True)
            pe.wait_ge(tab_done, 1)
            final = pe.value_load(nbi[0:1, 0:1], min_val=3, max_val=MAX_BLOCKS - 1)
            with pe.Fori(1, final) as b:
                expert_block(b, False)
            expert_block(final, False, last_block=True)
            blocks = final + 1
            pe.wait_ge(y_lo, blocks)
            pe.wait_ge(hot_saved, blocks)
            scatter(0)
            scatter(1, 0)

        @block.scalar
        def _(act):
            act.dma_start(gain[:], attn_norm[0].partition_broadcast(P)).then_inc(gain_first, 16)
            act.dma_start(cst[:], consts[:, 0:CONSTS]).then_inc(cst_in, 16)
            steps = [0]

            def link(ins):
                steps[0] += 1
                ins.then_inc(act_chain, 1)
                act.wait_ge(act_chain, steps[0])

            def copy(dst, src, scale=1.0):
                return nc.scalar.activation(dst, src, ACT.Copy, scale=scale)

            def both(banks):
                return banks.rearrange("p a s -> p (a s)")

            def inverse_root(dst, ln, sums, size):
                link(nc.scalar.activation(ln, sums, ACT.Ln, scale=1.0 / size, bias=eps[:, 0:1]))
                return nc.scalar.activation(dst, ln, ACT.Exp, scale=-0.5)

            def row_norms(m):
                for t in range(TT):
                    if m == 0:
                        act.wait_ge(x_in[t], 16)
                    else:
                        act.wait_ge(x_done[t], m)
                    one = slice(t, t + 1)
                    nc.scalar.activation(hn[:, t, :], xs[:, t, :], ACT.Square, accum_out=row_ss[:, one]).then_inc(row_ss_done, 1)
                    act.wait_ge(row_ss_done, TT * m + t + 1)
                    inverse_root(row_rstd[:, one], row_ln[:, one], row_ss[:, one], D).then_inc(row_rstd_done, 1)

            def turned(r, banks=range(4)):
                for j in banks:
                    act.wait_ge(t_done, 4 * r + j + 1)
                    dst, done = (rT, rT_done) if r == 5 else (aT_hi, t_hi)
                    copy(both(dst[:, 2 * j:2 * j + 2, :]), ps[:, 4 + j, :]).then_inc(done, 1)

            nc.scalar.preload_act_table_set("natural_log_exp_and_others")
            for l in range(DEPTH):
                n0 = LAYER1 * l
                if l == 0:
                    act.wait_ge(eps_done, 1)
                    row_norms(0)
                    split_hi(act, 0)
                    turned(0)
                    split_hi(act, 1)
                    split_hi(act, 2)
                else:
                    row_norms(2)
                    split_hi(act, n0 + 2)
                    turned(3 * l)

                def stay_logs(g):
                    act.wait_ge(absz_done, PAIRS * l + g + 1)
                    a = ab[:, g % 2].rearrange("p h q -> p (h q)")
                    link(nc.scalar.activation(a, a, ACT.Exp))
                    nc.scalar.activation(a, a, ACT.Ln, bias=1.0).then_inc(ln_done, 1)

                def weights(g):
                    act.wait_ge(tri_done, PAIRS * l + g + 1)
                    bank = (4, 2)[g % 2]
                    nc.scalar.activation(att[:, g % 2], ps[:, bank:bank + 2, 0:ZW], ACT.Exp).then_inc(a_done, 1)

                split_hi(act, n0 + 3)
                split_hi(act, n0 + 4)
                copy(both(qk_sb[:, 0:4, :]), both(ps[:, 0:2, :]), HD ** -0.5).then_inc(proj_saved, 1)
                split_hi(act, n0 + 5)
                if l == 0:
                    act.wait_ge(lam_sum, 1)
                    nc.scalar.activation(lam_e[:], lam_s[:], ACT.Exp).then_inc(lam_exp, 1)
                split_hi(act, n0 + 6)
                stay_logs(0)
                split_hi(act, n0 + 7)
                act.wait_ge(piece_used, n0 + 6)
                copy(both(v_sb[:]), both(ps[:, 0:2, :])).then_inc(proj_saved, 1)
                weights(0)
                split_hi(act, n0 + 8)
                stay_logs(1)
                split_hi(act, n0 + 9)
                split_hi(act, n0 + 10)
                copy(both(qk_df[:, 0:4, :]), both(ps[:, 0:2, :]), HD ** -0.5).then_inc(proj_saved, 1)
                weights(1)
                stay_logs(2)
                split_hi(act, n0 + 11)
                split_hi(act, n0 + 12)
                copy(both(qk_df[:, 4:8, :]), both(ps[:, 0:2, :])).then_inc(proj_saved, 1)
                weights(2)
                stay_logs(3)
                split_hi(act, n0 + 13)

                def exponentials(s):
                    act.wait_ge(mx_done, STEPS * l + s + 1)
                    for c in range(2):
                        z = zb[:, s % 4, c, 0:P * (s % 2 + 1)]
                        last = nc.scalar.activation(z, z, ACT.Exp, bias=mx[:, s % 3, c:c + 1], accum_out=es[:, s % 3, c:c + 1])
                    last.then_inc(e_done, 1)

                exponentials(0)
                weights(3)
                split_hi(act, n0 + 14)
                exponentials(1)
                act.wait_ge(pv_done, PAIRS * (l + 1))
                nc.scalar.activation(sq, both(ps[:, 6:8, :]), ACT.Square).then_inc(ss_done, 1)
                for i in range(2, STEPS + 3):
                    if i == 2:
                        exponentials(i)
                        act.wait_ge(head_sums, 2 * l + 1)
                        inverse_root(head_rstd[:], head_ln[:], head_ss[:], HD).then_inc(head_rstd_done, 1)
                    j = i - 3
                    if j >= 0:
                        act.wait_ge(wt_done, STEPS * l + j + 1)
                        copy(wT[:, j % 2, 0:P * (j % 2 + 1)], ps[:, 2 + j % 2, 0:P * (j % 2 + 1)]).then_inc(wt_saved, 1)
                    if 3 <= i < STEPS:
                        exponentials(i)
                    if i == STEPS + 1:
                        turned(3 * l + 1, range(2))
                act.wait_ge(pvd_done, l + 1)
                nc.scalar.activation(sq, both(ps[:, 6:8, :]), ACT.Square).then_inc(ss_done, 1)
                act.wait_ge(head_sums, 2 * l + 2)
                inverse_root(head_rstd[:, 0:8], head_ln[:, 0:8], head_ss[:, 0:8], 2 * HD).then_inc(head_rstd_done, 1)
                split_hi(act, n0 + 15)
                turned(3 * l + 1, range(2, 4))
                split_hi(act, n0 + 16)
                split_hi(act, n0 + 17)
                row_norms(2 * l + 1)
                split_hi(act, n0 + 18)
                turned(3 * l + 2)
                if l == 0:
                    for n in range(D_FULL + 1):
                        last_chunk = n == D_FULL
                        g = PROJ + WOUT + 4 * n
                        for i in range(g + 3, min(g + 7, PROJ + WOUT + DENSE_GU)):
                            split_hi(act, i)
                        if last_chunk:
                            for i in range(PROJ + WOUT + DENSE_GU, PROJ + WOUT + DENSE_GU + 2):
                                split_hi(act, i)
                        bank = 4 * (n % 2)
                        width = D_REST * TT if last_chunk else 2 * CH
                        act.wait_ge(piece_used, min(g + 4, PROJ + WOUT + DENSE_GU))
                        h = hn[:, n % 2, 0:width]
                        nc.scalar.activation(h, both(ps[:, bank:bank + 2, :])[:, 0:width], ACT.Silu).then_inc(silu_done, 1)
                        if last_chunk:
                            split_hi(act, PROJ + WOUT + DENSE_GU + 2)
                        act.wait_ge(hid_done, n + 1)
                        copy(both(hT_hi[:, 4 * n:4 * n + width // S, :]), h).then_inc(hT_hi_done, 1)
                    for i in range(PROJ + WOUT + DENSE_GU + 3, LAYER1 + 2):
                        split_hi(act, i)
                    nc.scalar.preload_act_table_set("natural_log_exp_and_others")

            act.wait_ge(rest_done, 1)
            copy(rows3[:, 1], hn[:]).then_inc(part_done, 1)
            act.wait_ge(gap_done, 1)
            nc.scalar.activation(ed[:], dm[:], ACT.Exp).then_inc(ge_done, 1)
            nc.scalar.preload_act_table(ACT.Silu)

            def gathered(count):
                for j in range(2):
                    act.wait_ge(ga_done, (count - 1) * 2 + j + 1)
                    copy(both(xe_hi[:, 4 * j:4 * j + 4, :]), ps[:, 1 + 2 * j, :]).then_inc(ga_hi, 1)

            def output_hi(b):
                act.wait_ge(piece_used, nth(MOE0, b))
                copy(ye_hi[:], both(ps[:, 4:6, :])).then_inc(y_hi, 1)

            def expert_block(b, first, last_block=False):
                def hi_of(kind, c, half):
                    if not (first and AT[(kind, c, half)] < SPL):
                        split_hi(act, MOE0 + AT[(kind, c, half)], b)

                def silu(c):
                    act.wait_ge(piece_used, nth(MOE0 + AT[("up", c, 1)] + 1, b))
                    nc.scalar.activation(sil[:, c % 2, :], ps[:, c % 2, :], ACT.Silu).then_inc(esilu_done, 1)

                for c in range(E_CH + 1):
                    if c < E_CH:
                        hi_of("gate", c, 0)
                    if c < 2:
                        hi_of("gate", c, 1)
                    if c > 0:
                        silu(c - 1)
                    elif not first:
                        output_hi(b)
                    if 2 <= c < E_CH:
                        hi_of("gate", c, 1)
                    if c < E_CH:
                        hi_of("up", c, 0)
                        hi_of("up", c, 1)
                    else:
                        hi_of("down", c - 1, 0)
                        if not last_block:
                            gathered(b + 2)
                    if c > 0:
                        act.wait_ge(et_done, b * E_CH + c)
                        copy(both(he_hi[:]), ps[:, 7, :]).then_inc(eh_hi, 1)
                        if c < E_CH:
                            hi_of("down", c - 1, 0)
                        hi_of("down", c - 1, 1)

            gathered(1)
            expert_block(0, True)
            act.wait_ge(tab_done, 1)
            final = act.value_load(nbi[0:1, 0:1], min_val=3, max_val=MAX_BLOCKS - 1)
            with act.Fori(1, final) as b:
                expert_block(b, False)
            expert_block(final, False, last_block=True)
            blocks = final + 1
            nc.scalar.preload_act_table_set("natural_log_exp_and_others")
            output_hi(blocks)
            row_norms(4)

        @block.vector
        def _(dve):
            steps = [0]

            def link(ins):
                steps[0] += 1
                ins.then_inc(dve_chain, 1)
                dve.wait_ge(dve_chain, steps[0])

            V = nc.vector

            def both(banks):
                return banks.rearrange("p a s -> p (a s)")

            def mean_square(v, sums, size):
                return V.tensor_scalar(v, sums, 1.0 / size, EPS, ALU.mult, ALU.add)

            def refine(fine, y, v, tmp):
                link(V.scalar_tensor_tensor(out=tmp, in0=y, scalar=-0.5, in1=y, op0=ALU.mult, op1=ALU.mult))
                link(V.tensor_tensor(fine, tmp, v, ALU.mult))
                link(V.scalar_tensor_tensor(out=fine, in0=fine, scalar=1.5, in1=y, op0=ALU.add, op1=ALU.mult))

            def normalise(m, t):
                one = slice(t, t + 1)
                dve.wait_ge(row_ss_done, TT * m + t + 1)
                link(mean_square(row_var[:, one], row_ss[:, one], D))
                dve.wait_ge(row_rstd_done, TT * m + t + 1)
                refine(row_fine[:, one], row_rstd[:, one], row_var[:, one], row_tmp[:, one])
                if t == 0:
                    dve.wait_ge(gain_first if m == 0 else gain_in, 16 * max(m, 1))
                V.scalar_tensor_tensor(out=hn[:, t, :], in0=xs[:, t, :], scalar=row_fine[:, t:t + 1],
                                       in1=gain[:], op0=ALU.mult, op1=ALU.mult).then_inc(
                                           out_rows if m == 4 else rows_done[t], 1)

            def turned(r, banks=range(4)):
                for j in banks:
                    dve.wait_ge(t_hi, 4 * r + j + 1)
                    V.tensor_tensor(both(aT_lo[:, 2 * j:2 * j + 2, :]), ps[:, 4 + j, :],
                                    both(aT_hi[:, 2 * j:2 * j + 2, :]).bitcast(F32), ALU.subtract).then_inc(t_lo, 1)

            V.memset(eps[:], EPS).then_inc(eps_done, 1)
            for l in range(DEPTH):
                n0 = LAYER1 * l
                if l == 0:
                    for t in range(TT):
                        normalise(0, t)
                    split_lo(dve, 0)
                turned(3 * l)
                split_lo(dve, n0 + 1)
                split_lo(dve, n0 + 2)

                def minus_abs(g):
                    dve.wait_ge(z_done, PAIRS * l + g + 1)
                    dve.wait_ge(z0_done, PAIRS * l + g + 1)
                    bank = (4, 2)[g % 2]
                    V.tensor_scalar(ab[:, g % 2].bitcast(I32), ps[:, bank:bank + 2, 0:ZW].bitcast(I32), SIGN, None,
                                    ALU.bitwise_or).then_inc(absz_done, 1)

                def softplus(g):
                    dve.wait_ge(ln_done, PAIRS * l + g + 1)
                    bank = (4, 2)[g % 2]
                    V.scalar_tensor_tensor(out=spl[:, g % 2], in0=ps[:, bank:bank + 2, 0:ZW], scalar=0.0, in1=ab[:, g % 2],
                                           op0=ALU.max, op1=ALU.add).then_inc(sp_done, 1)

                if l == 0:
                    dve.wait_ge(lam_ld, 16 * 4)
                    link(V.tensor_tensor(lam_pr[:], lam_in[:, 0:2], lam_in[:, 2:4], ALU.mult))
                    V.tensor_reduce(lam_s[:], lam_pr[:], AX.X, ALU.add).then_inc(lam_sum, 1)
                split_lo(dve, n0 + 3)
                split_lo(dve, n0 + 4)
                if l == 0:
                    dve.wait_ge(vrow_mm, 1)
                    V.tensor_copy(vrow[:], ps[0:DF_HEADS, 7, 0:384]).then_inc(vrow_done, 1)
                dve.wait_ge(piece_used, n0 + 4)
                V.tensor_copy(both(qk_sb[:, 4:8, :]), both(ps[:, 2:4, :])).then_inc(proj_saved2, 1)
                split_lo(dve, n0 + 5)
                minus_abs(0)
                if l == 0:
                    dve.wait_ge(lam_exp, 1)
                    link(V.tensor_tensor(lam_d[:], lam_e[:, 1, :], lam_e[:, 0, :], ALU.subtract))
                    for i in range(DEPTH):
                        link(V.tensor_scalar(nlam[:, i:i + 1], lam_d[:, i:i + 1], -lambda_init(i), None, ALU.add))
                split_lo(dve, n0 + 6)
                softplus(0)
                split_lo(dve, n0 + 7)
                if l == 0:
                    dve.wait_ge(bias_mm, 1)
                    V.tensor_copy(bias[:].rearrange("p h k -> p (h k)"), both(ps[:, 6:8, :])).then_inc(bias_done, 1)
                minus_abs(1)
                split_lo(dve, n0 + 8)
                softplus(1)
                split_lo(dve, n0 + 9)
                split_lo(dve, n0 + 10)
                minus_abs(2)
                softplus(2)
                split_lo(dve, n0 + 11)
                split_lo(dve, n0 + 12)
                minus_abs(3)
                softplus(3)
                split_lo(dve, n0 + 13)

                def scores(s):
                    h, n_k, bank = s // 2, P * (s % 2 + 1), 4 - 4 * (s % 2)
                    dve.wait_ge(zd_done, STEPS * l + s + 1)
                    dve.wait_ge(zd0_done, STEPS * l + s + 1)
                    z = zb[:, s % 4, :, 0:n_k]
                    link(V.tensor_tensor(z, ps[:, bank:bank + 2, 0:n_k],
                                         bias[:, h, S - n_k:S].unsqueeze(1).to_broadcast([P, 2, n_k]), ALU.add))
                    V.tensor_reduce(mx[:, s % 3, :], z, AX.X, ALU.max, negate=True).then_inc(mx_done, 1)

                def weigh(s):
                    h, t, n_k = s // 2, s % 2, P * (s % 2 + 1)
                    dve.wait_ge(e_done, STEPS * l + s + 1)
                    link(V.reciprocal(rr[:, t, h, :], es[:, s % 3, :]))
                    link(V.scalar_tensor_tensor(out=coef[:, s % 3, :], in0=es[:, s % 3, 0:1], scalar=nlam[:, l:l + 1],
                                                in1=rr[:, t, h, 1:2], op0=ALU.mult, op1=ALU.mult))
                    if s >= 2:
                        dve.wait_ge(wt_done, STEPS * l + s - 1)
                    V.scalar_tensor_tensor(out=wd[:, s % 2, 0:n_k], in0=zb[:, s % 4, 1, 0:n_k], scalar=coef[:, s % 3, :],
                                           in1=zb[:, s % 4, 0, 0:n_k], op0=ALU.mult, op1=ALU.add).then_inc(w_done, 1)

                def rows(c0, t, n_heads):
                    return hn[:, t, c0:c0 + HALF].rearrange("p (h d) -> p h d", h=n_heads)

                def over_d(a, n_heads):
                    return a.unsqueeze(2).to_broadcast([P, n_heads, HALF // n_heads])

                scores(0)
                dve.wait_ge(piece_used, n0 + 12)
                V.tensor_copy(both(v_df[:]), both(ps[:, 0:2, :])).then_inc(v_df_saved, 1)
                if l == 0:
                    dve.wait_ge(small_in, 16 * 2)
                    for i in range(DEPTH):
                        V.tensor_scalar(g_df[:, i, :], g_df[:, i, :], 1.0 - lambda_init(i), None, ALU.mult)
                scores(1)
                for i in range(2, STEPS + 2):
                    if i < STEPS:
                        scores(i)
                    weigh(i - 2)
                    if i == 2:
                        dve.wait_ge(ss_done, 2 * l + 1)
                        V.tensor_reduce(head_ss[:], sq.rearrange("p (a d) -> p a d", d=HD), AX.X, ALU.add).then_inc(head_sums, 1)
                        dve.wait_ge(head_sums, 2 * l + 1)
                        mean_square(head_var[:], head_ss[:], HD)
                    if i == 3:
                        dve.wait_ge(head_rstd_done, 2 * l + 1)
                        refine(head_fine[:], head_rstd[:], head_var[:], head_tmp[:])
                        for t in range(TT):
                            last = V.tensor_tensor(rows(0, t, SB_HEADS), ps[:, 6 + t, :].rearrange("p (h d) -> p h d", d=HD),
                                                   over_d(head_fine[:, 8 * t:8 * t + 8], SB_HEADS), ALU.mult)
                        last.then_inc(sbo_saved, 1)
                split_lo(dve, n0 + 14)
                turned(3 * l + 1, range(2))
                r0 = rr[:, :, :, 0]
                link(V.tensor_tensor(r0s[:], r0, r0, ALU.mult))
                dve.wait_ge(ss_done, 2 * l + 2)
                link(V.tensor_reduce(head_ss[:, 8:16], sq.rearrange("p (a d) -> p a d", d=2 * HD), AX.X, ALU.add))
                V.tensor_tensor(head_ss[:, 0:8], head_ss[:, 8:16], r0s[:].rearrange("p t h -> p (t h)"), ALU.mult).then_inc(head_sums, 1)
                dve.wait_ge(head_sums, 2 * l + 2)
                link(mean_square(head_var[:, 0:8], head_ss[:, 0:8], 2 * HD))
                dve.wait_ge(head_rstd_done, 2 * l + 2)
                refine(head_fine[:, 0:8], head_rstd[:, 0:8], head_var[:, 0:8], head_tmp[:, 0:8])
                link(V.tensor_tensor(scl[:], head_fine[:, 0:8].rearrange("p (t h) -> p t h", t=TT), r0, ALU.mult))
                for t in range(TT):
                    last = V.tensor_tensor(rows(HALF, t, DF_HEADS), ps[:, 6 + t, :].rearrange("p (h d) -> p h d", h=DF_HEADS),
                                           over_d(scl[:, t, :], DF_HEADS), ALU.mult)
                link(last)
                for t in range(TT):
                    V.tensor_tensor(rows(HALF, t, DF_HEADS), rows(HALF, t, DF_HEADS),
                                    g_df[:, l, :].unsqueeze(1).to_broadcast([P, DF_HEADS, 2 * HD]), ALU.mult).then_inc(rows_done[t], 1)
                split_lo(dve, n0 + 15)
                turned(3 * l + 1, range(2, 4))
                dve.wait_ge(piece_used, n0 + PROJ + 3)
                for t in range(TT):
                    xv = xs[:, t, 0:CH]
                    V.tensor_tensor(xv, xv, ps[:, t, :], ALU.add)
                split_lo(dve, n0 + 16)
                for t in range(TT):
                    if t == 0:
                        dve.wait_ge(tile0_done, 2 * l + 1)
                    else:
                        dve.wait_ge(piece_used, n0 + PROJ + WOUT)
                    xv = xs[:, t, CH:D]
                    V.tensor_tensor(xv, xv, ps[:, 2 + t, :], ALU.add).then_inc(x_done[t], 1)
                for t in range(TT):
                    normalise(2 * l + 1, t)
                if l == 0:
                    turned(2)
                    split_lo(dve, 17)
                    split_lo(dve, 18)
                    for n in range(D_FULL + 1):
                        last_chunk = n == D_FULL
                        g = PROJ + WOUT + 4 * n
                        for i in range(g + 3, min(g + 7, PROJ + WOUT + DENSE_GU)):
                            split_lo(dve, i)
                        if last_chunk:
                            for i in range(PROJ + WOUT + DENSE_GU, PROJ + WOUT + DENSE_GU + 2):
                                split_lo(dve, i)
                        bank = 4 * (n % 2) + 2
                        width = D_REST * TT if last_chunk else 2 * CH
                        dve.wait_ge(silu_done, n + 1)
                        h = hn[:, n % 2, 0:width]
                        V.tensor_tensor(h, h, both(ps[:, bank:bank + 2, :])[:, 0:width], ALU.mult).then_inc(hid_done, 1)
                        if last_chunk:
                            split_lo(dve, PROJ + WOUT + DENSE_GU + 2)
                        dve.wait_ge(hT_hi_done, n + 1)
                        V.tensor_tensor(both(hT_lo[:, 4 * n:4 * n + width // S, :]), h,
                                        both(hT_hi[:, 4 * n:4 * n + width // S, :]).bitcast(F32),
                                        ALU.subtract).then_inc(hT_lo_done, 1)
                    for i in range(PROJ + WOUT + DENSE_GU + 3, LAYER1 + 1):
                        split_lo(dve, i)
                    for t in range(TT):
                        if t == 0:
                            dve.wait_ge(tile0_done, 2)
                        else:
                            dve.wait_ge(piece_used, LAYER1)
                        V.tensor_tensor(xs[:, t, :], xs[:, t, :], both(ps[:, 2 * t:2 * t + 2, :]), ALU.add).then_inc(x_done[t], 1)
                    for t in range(TT):
                        normalise(2, t)
            V.tensor_copy(counts[:].rearrange("p a k -> p (a k)"), cst[:, C_TRIS:C_TRIS + 2 * P])
            split_lo(dve, MOE0 + 1)
            dve.wait_ge(part_done, TT)
            dve.wait_ge(t_done, 24)
            V.tensor_tensor(hn[:], hn[:], rows3[:, 0], ALU.subtract).then_inc(rest_done, 1)

            def row(a, width=NE):
                return cst[:, a:a + width]

            def over_e(a):
                return a.unsqueeze(2).to_broadcast([P, TT, NE])

            dve.wait_ge(lgT_done, 1)
            V.tensor_copy(lgT[:], ps[0:NE, 0, 0:S]).then_inc(lgT_saved, 1)
            dve.wait_ge(lg_done, 1)
            link(V.tensor_copy(lg[:].rearrange("p t e -> p (t e)"), ps[:, 2, 0:TT * NE]))
            rev = row(C_REV).unsqueeze(1).to_broadcast([P, TT, NE])
            for lgs, m, eq, rk, r, oh in ((lg, m1, eq1, rk1, r1, oh1), (lg2, m2, eq2, rk2, r2, oh2)):
                link(V.tensor_reduce(m[:], lgs[:], AX.X, ALU.max))
                link(V.tensor_tensor(eq[:], lgs[:], over_e(m[:]), ALU.is_equal))
                link(V.tensor_tensor(rk[:], eq[:], rev, ALU.mult))
                link(V.tensor_reduce(r[:], rk[:], AX.X, ALU.max))
                link(V.tensor_tensor(oh[:], rk[:], over_e(r[:]), ALU.is_equal))
                if lgs is lg:
                    link(V.scalar_tensor_tensor(out=lg2[:], in0=oh1[:], scalar=-3.0e38, in1=lg[:], op0=ALU.mult, op1=ALU.add))
            V.tensor_tensor(chosen[:], oh1[:], oh2[:], ALU.add).then_inc(chosen_done, 1)
            V.tensor_tensor(dm[:], m2[:], m1[:], ALU.subtract).then_inc(gap_done, 1)
            dve.wait_ge(pos_done, 1)
            link(V.tensor_scalar(posm0[:].rearrange("p t e -> p (t e)"), ps[:, 1, 0:TT * NE], NOT_CHOSEN, None, ALU.add))
            link(V.tensor_tensor(pm1[:], posm0[:], chosen[:], ALU.mult))
            link(V.tensor_scalar(posm[:], pm1[:], -NOT_CHOSEN, None, ALU.add))
            link(V.tensor_copy(cnt[:], ps[:, 1, TT * NE:TT * NE + NE]))

            def one_hot(places):
                for t in range(TT):
                    last = V.tensor_scalar(onehot[:, t, :], iota, places(t), None, ALU.is_equal)
                last.then_inc(hot_ready, 1)
                for t in range(TT):
                    V.tensor_scalar(hot32[:, t, :], iota, places(t), None, ALU.is_equal)

            one_hot(lambda t: posm[:, t, 0:1])
            split_lo(dve, MOE0 + 2)

            def gates():
                dve.wait_ge(ge_done, 1)
                link(V.tensor_scalar(dn[:], ed[:], 1.0, None, ALU.add))
                link(V.reciprocal(g1[:], dn[:]))
                link(V.tensor_tensor(g2[:], ed[:], g1[:], ALU.mult))
                link(V.tensor_tensor(gg1[:], oh1[:], over_e(g1[:]), ALU.mult))
                link(V.tensor_tensor(gg[:], oh2[:], over_e(g2[:]), ALU.mult))
                link(V.tensor_tensor(gg[:], gg[:], gg1[:], ALU.add))
                link(V.tensor_scalar(nb1[:], cnt[:], 0.0, None, ALU.is_gt))
                link(V.memset(nb1[:, 0:1], 1.0))
                link(V.tensor_scalar(nb2[:], cnt[:], float(P), None, ALU.is_gt))
                link(V.tensor_tensor(nbe[:], nb1[:], nb2[:], ALU.add))

            def block_list():
                link(V.tensor_tensor(le8[:], cst[:, C_LE:C_LE + NE * NE].rearrange("p (j e) -> p j e", e=NE),
                                     nbe[:].unsqueeze(1).to_broadcast([P, NE, NE]), ALU.mult))
                link(V.tensor_reduce(ends[:], le8[:], AX.X, ALU.add))
                ends_b = ends[:].unsqueeze(1).to_broadcast([P, TAB, NE])
                link(V.tensor_tensor(cmpb[:], ends_b, row(C_B, TAB).unsqueeze(2).to_broadcast([P, TAB, NE]), ALU.is_le))
                link(V.tensor_reduce(eb[:], cmpb[:], AX.X, ALU.add))
                link(V.tensor_tensor(stb[:], cmpb[:], ends_b, ALU.mult))
                link(V.tensor_reduce(start[:], stb[:], AX.X, ALU.max))
                link(V.tensor_tensor(local[:], row(C_B, TAB), start[:], ALU.subtract))
                link(V.tensor_tensor(cm[:], row(C_E).unsqueeze(1).to_broadcast([P, TAB, NE]),
                                     eb[:].unsqueeze(2).to_broadcast([P, TAB, NE]), ALU.is_equal))
                link(V.tensor_scalar(ebi[:], eb[:], float(NE - 1), None, ALU.min))
                V.tensor_scalar(nbi[:], ends[:, NE - 1:NE], -1.0, None, ALU.add).then_inc(tab_done, 1)

            def block_columns():
                for t in range(TT):
                    for i, (table, res) in enumerate(((posm, sel0), (gg, gate))):
                        link(V.tensor_tensor(tmpb[:, i, t], cm[:], table[:, t, :].unsqueeze(1).to_broadcast([P, TAB, NE]), ALU.mult))
                        link(V.tensor_reduce(res[:, t, :], tmpb[:, i, t], AX.X, ALU.add))
                    link(V.scalar_tensor_tensor(out=sel[:, t, :], in0=local[:], scalar=-float(P), in1=sel0[:, t, :],
                                                op0=ALU.mult, op1=ALU.add))

            def gathered(halves_before):
                for j in range(2):
                    dve.wait_ge(ga_hi, halves_before + j + 1)
                    V.tensor_tensor(both(xe_lo[:, 4 * j:4 * j + 4, :]), ps[:, 1 + 2 * j, :],
                                    both(xe_hi[:, 4 * j:4 * j + 4, :]).bitcast(F32), ALU.subtract).then_inc(ga_lo, 1)

            def output_lo(b):
                dve.wait_ge(y_hi, b)
                V.tensor_tensor(ye_lo[:], both(ps[:, 4:6, :]), ye_hi[:].bitcast(F32), ALU.subtract).then_inc(y_lo, 1)

            def add_back(b, t, bank=6):
                dve.wait_ge(sc_done[t], b)
                return V.scalar_tensor_tensor(out=xs[:, t, :], in0=both(ps[:, bank:bank + 2, :]),
                                              scalar=gate[:, t, bass.ds(b - 1, 1)], in1=xs[:, t, :], op0=ALU.mult, op1=ALU.add)

            def expert_block(b, first, last_block=False):
                def lo_of(kind, c, half):
                    if not (first and AT[(kind, c, half)] < SPL):
                        split_lo(dve, MOE0 + AT[(kind, c, half)], b)

                for c in range(E_CH + 1):
                    if c < E_CH:
                        lo_of("gate", c, 0)
                    if c < 2:
                        lo_of("gate", c, 1)
                    if c > 0:
                        dve.wait_ge(esilu_done, b * E_CH + c)
                        V.tensor_tensor(hid[:, (c - 1) % 2, :], sil[:, (c - 1) % 2, :], ps[:, 2 + (c - 1) % 2, :],
                                        ALU.mult).then_inc(ehid_done, 1)
                    elif not first:
                        output_lo(b)
                    if c == 1 and not first:
                        add_back(b, 1).then_inc(sc_added[1], 1)
                    if 2 <= c < E_CH:
                        lo_of("gate", c, 1)
                    if c < E_CH:
                        lo_of("up", c, 0)
                        if c == 0 and not first:
                            add_back(b, 0).then_inc(sc_added[0], 1)
                        lo_of("up", c, 1)
                    else:
                        lo_of("down", c - 1, 0)
                        if not last_block:
                            gathered(b * 2 + 2)
                    if c > 0:
                        dve.wait_ge(eh_hi, b * E_CH + c)
                        V.tensor_tensor(both(he_lo[:]), ps[:, 7, :], both(he_hi[:]).bitcast(F32), ALU.subtract).then_inc(eh_lo, 1)
                    if c == 2:
                        dve.wait_ge(hot_t, b + 1)
                        V.tensor_copy(onehotT[:].rearrange("p t s -> p (t s)"), ps[:, 6, 0:TT * P]).then_inc(hot_saved, 1)
                    if first and c == 1:
                        gates()
                    if first and c == 2:
                        block_list()
                    if first and c == 3:
                        block_columns()
                    if c == 4 and not last_block:
                        one_hot(lambda t: sel[:, t, bass.ds(b + 1, 1)])
                    if 0 < c < E_CH:
                        lo_of("down", c - 1, 0)
                    if c > 0:
                        lo_of("down", c - 1, 1)

            gathered(0)
            expert_block(0, True)
            dve.wait_ge(tab_done, 1)
            final = dve.value_load(nbi[0:1, 0:1], min_val=3, max_val=MAX_BLOCKS - 1)
            with dve.Fori(1, final) as b:
                expert_block(b, False)
            expert_block(final, False, last_block=True)
            blocks = final + 1
            output_lo(blocks)
            add_back(blocks, 0).then_inc(x_done[0], 1)
            add_back(blocks, 1, 0).then_inc(x_done[1], 1)
            for t in range(TT):
                normalise(4, t)


_INS = ["x", "w_in", "w_out", "attn_norm", "ffn_norm", "sb_out_norm", "diff_subln", "lambda_q1", "lambda_k1",
        "lambda_q2", "lambda_k2", "rel_bias", "dense_w_gate", "dense_w_up", "dense_w_down", "router_w",
        "expert_w_gate", "expert_w_up", "expert_w_down", "final_norm"]


def kernel(**inputs):
    import concourse.bacc as bacc
    from concourse.bass_utils import run_bass_kernel_spmd

    nc = bacc.Bacc("TRN2", target_bir_lowering=False, num_devices=1)
    arrays = {f"in_{n}": np.ascontiguousarray(inputs[n]) for n in _INS}
    arrays["in_consts"] = constants()
    args = [nc.dram_tensor(n, a.shape, mybir.dt.from_np(a.dtype), kind="ExternalInput").ap() for n, a in arrays.items()]
    out = nc.dram_tensor("out_x", (1, S, D), F32, kind="ExternalOutput").ap()
    build(nc, *args, out)
    r = run_bass_kernel_spmd(nc, [arrays], core_ids=[0])
    return r.results[0]["out_x"]
```
